# Optimizing a Trainium2 kernel written in Bass

```python
import jax, jax.numpy as jnp
from jax import lax
import numpy as np

D_MODEL = 1024
BATCH = 1
SEQ = 1024
DEPTH = 2
DEC_BATCH = 8
DEC_SEQ = 8
PAST_LEN = 2048
PAGE_SIZE = 128

N_REC_LAYERS = (DEPTH + 1) // 2
N_ATT_LAYERS = DEPTH // 2
EPS = 1e-6
RET_HEADS = 4
RET_DK = 64
RET_DV = 128
RET_CHUNK = 128
LRU_WIDTH = 512
LRU_BLOCKS = 4
LRU_BLOCK = LRU_WIDTH // LRU_BLOCKS
CONV_WIDTH = 4
LRU_C = 8.0
REC_SPLITS = (RET_HEADS * RET_DK, 2 * RET_HEADS * RET_DK, 2 * RET_HEADS * RET_DK + RET_HEADS * RET_DV,
              2 * RET_HEADS * RET_DK + 2 * RET_HEADS * RET_DV,
              2 * RET_HEADS * RET_DK + 2 * RET_HEADS * RET_DV + LRU_WIDTH)
REC_IN = 2 * RET_HEADS * RET_DK + 2 * RET_HEADS * RET_DV + 2 * LRU_WIDTH
REC_OUT = RET_HEADS * RET_DV + LRU_WIDTH
ATT_HEADS = 16
ATT_DH = D_MODEL // ATT_HEADS
PATTERNS = ((128, 1), (512, 4), (2048, 16))
MAX_WINDOW = 2048
ATT_BLOCK = 128
D_FF = -(-8 * D_MODEL // (3 * 256)) * 256

kernel_name = "retnet_griffin_longnet_hybrid_step"

def rmsnorm(x, g):
    xf = x.astype(jnp.float32)
    y = xf * lax.rsqrt(jnp.mean(xf * xf, axis=-1, keepdims=True) + EPS)
    return (y * g.astype(jnp.float32)).astype(x.dtype)

def head_rms(a, g):
    return a * lax.rsqrt(jnp.mean(a * a, axis=-1, keepdims=True) + EPS) * g.astype(jnp.float32)

def swiglu_block(x, g, w_gate, w_up, w_down):
    h = rmsnorm(x, g)
    return x + (jax.nn.silu(h @ w_gate) * (h @ w_up)) @ w_down

def retention(q, k, v, s0):
    B, T = q.shape[:2]
    C = RET_CHUNK if T % RET_CHUNK == 0 else T
    n = T // C
    log_g = jnp.log1p(-jnp.power(2.0, -5.0 - jnp.arange(RET_HEADS, dtype=jnp.float32)))
    idx = jnp.arange(C, dtype=jnp.float32)
    diff = idx[:, None] - idx[None, :]
    decay = jnp.where(diff >= 0, jnp.exp(log_g[:, None, None] * jnp.maximum(diff, 0.0)), 0.0)
    q_dec = jnp.exp(log_g[:, None] * (idx + 1.0))
    k_dec = jnp.exp(log_g[:, None] * (C - 1.0 - idx))
    c_dec = jnp.exp(log_g * C)

    def blocks(a):
        return a.reshape(B, n, C, RET_HEADS, a.shape[-1]).transpose(1, 0, 3, 2, 4)

    def step(S, inp):
        qc, kc, vc = inp
        att = jnp.einsum('bhqd,bhkd->bhqk', qc, kc) * decay
        o = (jnp.einsum('bhqk,bhkv->bhqv', att, vc)
             + jnp.einsum('bhqd,bhdv->bhqv', qc * q_dec[..., None], S))
        S = S * c_dec[:, None, None] + jnp.einsum('bhkd,bhkv->bhdv', kc * k_dec[..., None], vc)
        return S, o

    S, o = lax.scan(step, s0, (blocks(q), blocks(k), blocks(v)))
    o = o.transpose(1, 0, 3, 2, 4).reshape(B, T, RET_HEADS, RET_DV)
    return o, S

def causal_conv(x, buf, w, b):
    T = x.shape[1]
    xp = jnp.concatenate([buf.astype(x.dtype), x], axis=1)
    y = b + xp[:, 0:T] * w[0]
    for j in range(1, CONV_WIDTH):
        y = y + xp[:, j:j + T] * w[j]
    return y, xp[:, -(CONV_WIDTH - 1):]

def rg_lru(x, w_rg, b_rg, w_ig, b_ig, lam, h0):
    B, T, W = x.shape
    f32 = jnp.float32
    xb = x.reshape(B, T, LRU_BLOCKS, LRU_BLOCK)
    r = jax.nn.sigmoid(jnp.einsum('btni,nij->btnj', xb, w_rg.astype(f32)).reshape(B, T, W) + b_rg.astype(f32))
    i = jax.nn.sigmoid(jnp.einsum('btni,nij->btnj', xb, w_ig.astype(f32)).reshape(B, T, W) + b_ig.astype(f32))
    log_a = -LRU_C * r * jax.nn.softplus(-lam.astype(f32))
    a = jnp.exp(log_a)
    bterm = jnp.sqrt(-jnp.expm1(2.0 * log_a)) * (i * x)
    bterm = bterm.at[:, 0].add(a[:, 0] * h0)

    def comb(lhs, rhs):
        a1, b1 = lhs
        a2, b2 = rhs
        return a1 * a2, a2 * b1 + b2

    _, h = lax.associative_scan(comb, (a, bterm), axis=1)
    return h, h[:, -1]

def rec_mixer(h, s_ret0, h_lru0, conv0, w_in, w_out, ret_g, conv_w, conv_b, w_rg, b_rg, w_ig, b_ig, lam):
    B, T, _ = h.shape
    f32 = jnp.float32
    proj = h @ w_in
    q, k, v, g, xl, yl = jnp.split(proj, list(REC_SPLITS), axis=-1)
    q = q.astype(f32).reshape(B, T, RET_HEADS, RET_DK)
    k = k.astype(f32).reshape(B, T, RET_HEADS, RET_DK) * (RET_DK ** -0.5)
    v = v.astype(f32).reshape(B, T, RET_HEADS, RET_DV)
    o, s_ret = retention(q, k, v, s_ret0.astype(f32))
    ret_out = head_rms(o, ret_g).reshape(B, T, RET_HEADS * RET_DV) * jax.nn.silu(g.astype(f32))
    xc, conv_new = causal_conv(xl, conv0, conv_w, conv_b)
    hl, h_last = rg_lru(xc.astype(f32), w_rg, b_rg, w_ig, b_ig, lam, h_lru0.astype(f32))
    lru_out = hl * jax.nn.gelu(yl.astype(f32))
    mix = jnp.concatenate([ret_out, lru_out], axis=-1).astype(h.dtype)
    return mix @ w_out, s_ret.astype(s_ret0.dtype), h_last.astype(h_lru0.dtype), conv_new

def alibi_slopes():
    return jnp.power(2.0, -8.0 * jnp.arange(1, ATT_HEADS + 1, dtype=jnp.float32) / ATT_HEADS)

def att_qkv(h, w_in, qg, kg):
    B, T, _ = h.shape
    q, k, v = jnp.split((h @ w_in).astype(jnp.float32), 3, axis=-1)
    q = head_rms(q.reshape(B, T, ATT_HEADS, ATT_DH), qg)
    k = head_rms(k.reshape(B, T, ATT_HEADS, ATT_DH), kg)
    v = v.reshape(B, T, ATT_HEADS, ATT_DH)
    return q, k, v

def dilated_band(q, k, v, d, span):
    B, T, H, Dh = q.shape
    L = T // d
    Lp = -(-L // ATT_BLOCK) * ATT_BLOCK
    nb = Lp // ATT_BLOCK
    Z = B * d

    def sub(a):
        a = a.reshape(B, L, d, H, Dh).transpose(0, 2, 1, 3, 4).reshape(Z, L, H, Dh)
        a = jnp.pad(a, ((0, 0), (0, Lp - L), (0, 0), (0, 0)))
        return a.reshape(Z, nb, ATT_BLOCK, H, Dh)

    def with_prev(a):
        prev = jnp.pad(a[:, :-1], ((0, 0), (1, 0), (0, 0), (0, 0), (0, 0)))
        return jnp.concatenate([prev, a], axis=2)

    qb = sub(q)
    kc = with_prev(sub(k))
    vc = with_prev(sub(v))
    s = jnp.einsum('znqhd,znkhd->znhqk', qb, kc) * (Dh ** -0.5)
    qq = jnp.arange(ATT_BLOCK)
    kk = jnp.arange(2 * ATT_BLOCK)
    diff = ATT_BLOCK + qq[:, None] - kk[None, :]
    first = (jnp.arange(nb) == 0)[:, None, None]
    valid = (diff >= 0) & (diff <= span) & (~first | (kk >= ATT_BLOCK)[None, None, :])
    s = s - alibi_slopes()[:, None, None] * (d * diff)
    s = jnp.where(valid[:, None], s, -jnp.inf)
    m = jnp.max(s, axis=-1, keepdims=True)
    p = jnp.exp(s - m)
    den = jnp.sum(p, axis=-1)
    o = jnp.einsum('znhqk,znkhd->znqhd', p, vc) / den.transpose(0, 1, 3, 2)[..., None]
    lse = (m[..., 0] + jnp.log(den)).transpose(0, 1, 3, 2)
    o = o.reshape(Z, Lp, H, Dh)[:, :L].reshape(B, d, L, H, Dh).transpose(0, 2, 1, 3, 4).reshape(B, T, H, Dh)
    lse = lse.reshape(Z, Lp, H)[:, :L].reshape(B, d, L, H).transpose(0, 2, 1, 3).reshape(B, T, H)
    return o, lse

def dilated_gather(q, kall, vall, d, span):
    S = q.shape[1]
    NP = kall.shape[1] - S
    j = jnp.arange(span + 1)
    kidx = NP + jnp.arange(S)[:, None] - d * j[None, :]
    valid = kidx >= 0
    kidx = jnp.maximum(kidx, 0)
    kg = kall[:, kidx]
    vg = vall[:, kidx]
    s = jnp.einsum('bshd,bsjhd->bhsj', q, kg) * (q.shape[-1] ** -0.5)
    s = s - alibi_slopes()[:, None, None] * (d * j)[None, None, :]
    s = jnp.where(valid[None, None], s, -jnp.inf)
    m = jnp.max(s, axis=-1, keepdims=True)
    p = jnp.exp(s - m)
    den = jnp.sum(p, axis=-1)
    o = jnp.einsum('bhsj,bsjhd->bshd', p, vg) / den.transpose(0, 2, 1)[..., None]
    lse = (m[..., 0] + jnp.log(den)).transpose(0, 2, 1)
    return o, lse

def combine_patterns(os, lses):
    w = jax.nn.softmax(jnp.stack(lses, axis=0), axis=0)
    return jnp.sum(w[..., None] * jnp.stack(os, axis=0), axis=0)

def setup_inputs(seed: int = 0) -> dict:
    key = jax.random.key(seed)
    ks = jax.random.split(key, 32)
    f32 = jnp.float32

    def nrm(k, shape, scale):
        return jax.random.normal(k, shape, f32) * scale

    win = min(MAX_WINDOW, PAST_LEN)
    u = jax.random.uniform(ks[14], (N_REC_LAYERS, LRU_WIDTH), f32, minval=0.9, maxval=0.999)
    a0 = jnp.power(u, 1.0 / LRU_C)
    lru_lambda = jnp.log(a0) - jnp.log1p(-a0)
    return {
        "x_prompt": nrm(ks[0], (BATCH, SEQ, D_MODEL), 1.0),
        "x_sample": nrm(ks[1], (DEC_BATCH, DEC_SEQ, D_MODEL), 1.0),
        "state_ret": nrm(ks[2], (N_REC_LAYERS, DEC_BATCH, RET_HEADS, RET_DK, RET_DV), 0.1),
        "state_lru": nrm(ks[3], (N_REC_LAYERS, DEC_BATCH, LRU_WIDTH), 0.5),
        "state_conv": nrm(ks[4], (N_REC_LAYERS, DEC_BATCH, CONV_WIDTH - 1, LRU_WIDTH), 1.0),
        "cache_k": nrm(ks[5], (N_ATT_LAYERS, DEC_BATCH, win, ATT_HEADS, ATT_DH), 1.0),
        "cache_v": nrm(ks[6], (N_ATT_LAYERS, DEC_BATCH, win, ATT_HEADS, ATT_DH), 1.0),
        "norm_mix": 1.0 + nrm(ks[7], (DEPTH, D_MODEL), 0.01),
        "norm_ffn": 1.0 + nrm(ks[8], (DEPTH, D_MODEL), 0.01),
        "w_in_rec": nrm(ks[9], (N_REC_LAYERS, D_MODEL, REC_IN), D_MODEL ** -0.5),
        "w_out_rec": nrm(ks[10], (N_REC_LAYERS, REC_OUT, D_MODEL), REC_OUT ** -0.5),
        "ret_norm_g": 1.0 + nrm(ks[11], (N_REC_LAYERS, RET_HEADS, RET_DV), 0.01),
        "conv_w": nrm(ks[12], (N_REC_LAYERS, CONV_WIDTH, LRU_WIDTH), CONV_WIDTH ** -0.5),
        "conv_b": nrm(ks[13], (N_REC_LAYERS, LRU_WIDTH), 0.01),
        "w_rgate": nrm(ks[15], (N_REC_LAYERS, LRU_BLOCKS, LRU_BLOCK, LRU_BLOCK), LRU_BLOCK ** -0.5),
        "b_rgate": nrm(ks[16], (N_REC_LAYERS, LRU_WIDTH), 0.01),
        "w_igate": nrm(ks[17], (N_REC_LAYERS, LRU_BLOCKS, LRU_BLOCK, LRU_BLOCK), LRU_BLOCK ** -0.5),
        "b_igate": nrm(ks[18], (N_REC_LAYERS, LRU_WIDTH), 0.01),
        "lru_lambda": lru_lambda,
        "w_in_att": nrm(ks[19], (N_ATT_LAYERS, D_MODEL, 3 * ATT_HEADS * ATT_DH), D_MODEL ** -0.5),
        "w_out_att": nrm(ks[20], (N_ATT_LAYERS, ATT_HEADS * ATT_DH, D_MODEL), (ATT_HEADS * ATT_DH) ** -0.5),
        "q_norm_g": 1.0 + nrm(ks[21], (N_ATT_LAYERS, ATT_DH), 0.01),
        "k_norm_g": 1.0 + nrm(ks[22], (N_ATT_LAYERS, ATT_DH), 0.01),
        "w_ffn_gate": nrm(ks[23], (DEPTH, D_MODEL, D_FF), D_MODEL ** -0.5),
        "w_ffn_up": nrm(ks[24], (DEPTH, D_MODEL, D_FF), D_MODEL ** -0.5),
        "w_ffn_down": nrm(ks[25], (DEPTH, D_FF, D_MODEL), D_FF ** -0.5),
    }

def reference(x_prompt, x_sample, state_ret, state_lru, state_conv, cache_k, cache_v,
              norm_mix, norm_ffn, w_in_rec, w_out_rec, ret_norm_g, conv_w, conv_b,
              w_rgate, b_rgate, w_igate, b_igate, lru_lambda,
              w_in_att, w_out_att, q_norm_g, k_norm_g, w_ffn_gate, w_ffn_up, w_ffn_down):
    yp, ys = x_prompt, x_sample
    B, T, _ = x_prompt.shape
    ret_p, lru_p, conv_p, kp, vp = [], [], [], [], []
    ret_s, lru_s, conv_s, ksl, vsl = [], [], [], [], []
    for l in range(DEPTH):
        i = l // 2
        if l % 2 == 0:
            prm = (w_in_rec[i], w_out_rec[i], ret_norm_g[i], conv_w[i], conv_b[i],
                   w_rgate[i], b_rgate[i], w_igate[i], b_igate[i], lru_lambda[i])
            out_p, sr, sl, sc = rec_mixer(
                rmsnorm(yp, norm_mix[l]),
                jnp.zeros((B, RET_HEADS, RET_DK, RET_DV), jnp.float32),
                jnp.zeros((B, LRU_WIDTH), jnp.float32),
                jnp.zeros((B, CONV_WIDTH - 1, LRU_WIDTH), yp.dtype), *prm)
            out_s, sr2, sl2, sc2 = rec_mixer(
                rmsnorm(ys, norm_mix[l]), state_ret[i], state_lru[i], state_conv[i], *prm)
            ret_p.append(sr); lru_p.append(sl); conv_p.append(sc)
            ret_s.append(sr2); lru_s.append(sl2); conv_s.append(sc2)
        else:
            q, k, v = att_qkv(rmsnorm(yp, norm_mix[l]), w_in_att[i], q_norm_g[i], k_norm_g[i])
            res = [dilated_band(q, k, v, d, w // d) for (w, d) in PATTERNS]
            o = combine_patterns([r[0] for r in res], [r[1] for r in res])
            out_p = o.reshape(B, T, ATT_HEADS * ATT_DH).astype(yp.dtype) @ w_out_att[i]
            keep = min(MAX_WINDOW, T)
            kp.append(k[:, T - keep:].astype(cache_k.dtype)); vp.append(v[:, T - keep:].astype(cache_v.dtype))
            qs, kn, vn = att_qkv(rmsnorm(ys, norm_mix[l]), w_in_att[i], q_norm_g[i], k_norm_g[i])
            kall = jnp.concatenate([cache_k[i].astype(jnp.float32), kn], axis=1)
            vall = jnp.concatenate([cache_v[i].astype(jnp.float32), vn], axis=1)
            res = [dilated_gather(qs, kall, vall, d, w // d) for (w, d) in PATTERNS]
            os_ = combine_patterns([r[0] for r in res], [r[1] for r in res])
            out_s = os_.reshape(ys.shape[0], ys.shape[1], ATT_HEADS * ATT_DH).astype(ys.dtype) @ w_out_att[i]
            ksl.append(kn.astype(cache_k.dtype)); vsl.append(vn.astype(cache_v.dtype))
        yp = swiglu_block(yp + out_p, norm_ffn[l], w_ffn_gate[l], w_ffn_up[l], w_ffn_down[l])
        ys = swiglu_block(ys + out_s, norm_ffn[l], w_ffn_gate[l], w_ffn_up[l], w_ffn_down[l])
    return (yp, ys,
            jnp.stack(ret_p), jnp.stack(lru_p), jnp.stack(conv_p), jnp.stack(kp), jnp.stack(vp),
            jnp.stack(ret_s), jnp.stack(lru_s), jnp.stack(conv_s), jnp.stack(ksl), jnp.stack(vsl))


_drawn_inputs = setup_inputs


def setup_inputs(seed=0):
    import zlib

    import numpy as np

    out = dict(_drawn_inputs(seed))
    spreads = {}
    factors = {'norm_mix': 3.554,
     'norm_ffn': 5.937,
     'ret_norm_g': 8.0,
     'b_rgate': 29.94,
     'b_igate': 28.504,
     'q_norm_g': 62.145,
     'k_norm_g': 49.486,
     'cache_k': 3.249,
     'cache_v': 3.647,
     'conv_b': 3.03}
    for name, (base, spread) in spreads.items():
        noise = np.random.default_rng([zlib.crc32(name.encode()), seed]).standard_normal(out[name].shape)
        drawn = base * np.exp(spread * noise) if base else spread * noise
        out[name] = __import__('jax').numpy.asarray(drawn.astype(out[name].dtype))
    for name, factor in factors.items():
        out[name] = (out[name] * factor).astype(out[name].dtype)
    return out
```

```python
from contextlib import ExitStack

import numpy as np

import concourse.bass as bass
from concourse import mybir

F32 = mybir.dt.float32
F32R = mybir.dt.float32r
ALU = mybir.AluOpType
ACT = mybir.ActivationFunctionType
AX = mybir.AxisListType

P = 128
D = 1024
KT = D // P
SEQ = 1024
QT = SEQ // P
DB, DS = 8, 8
NS = DB * DS
PAST = 2048
F = 2816
EPS = 1e-6
RH, DK, DV = 4, 64, 128
LW = 512
CONV = 4
LRU_C = 8.0
H, DH = 16, 64
HP = H // 2
CW = 364
NCH = 3
TW = CW * NCH
S0 = TW - NS
PAD = S0 - SEQ
NT = QT + 1
BW = 256
BE = KT * BW
RING = 3
NG = F // BW
REC_IN = 2560
N_IN0, N_OUT, N_FFN, N_QKV = REC_IN // BW, D // BW, 3 * NG, 3 * D // BW
B_IN0 = 0
B_OUT0 = B_IN0 + N_IN0
B_FFN0 = B_OUT0 + N_OUT
B_QKV = B_FFN0 + N_FFN
B_OUT1 = B_QKV + N_QKV
B_FFN1 = B_OUT1 + N_OUT
NBLK = B_FFN1 + N_FFN
MASKED = -1.0e30
RS_CHUNK = 128


def win(t):
    return t * P if t < QT else TW - P


def constants():
    gamma = 1.0 - 2.0 ** (-5.0 - np.arange(RH))
    i = np.arange(P)
    c = {}
    c["c_ident"] = np.eye(P, dtype=np.float32)
    diff = i[None, :] - i[:, None]
    scale = DK ** -0.5
    dec = np.where(diff >= 0, gamma[:, None, None] ** np.maximum(diff, 0), 0.0) * scale
    c["c_dec"] = np.ascontiguousarray(dec.transpose(1, 0, 2)).astype(np.float32)
    j = np.arange(NS)
    sd = (j % DS)[None, :] - (j % DS)[:, None]
    same = (j // DS)[None, :] == (j // DS)[:, None]
    decs = np.where(same & (sd >= 0), gamma[:, None, None] ** np.maximum(sd, 0), 0.0) * scale
    c["c_decs"] = np.ascontiguousarray(decs.transpose(1, 0, 2)).astype(np.float32)
    qd = np.zeros((P, 2, P + NS))
    for h in range(RH):
        rows = slice(DK * (h % 2), DK * (h % 2) + DK)
        qd[rows, h // 2, :P] = gamma[h] ** (i + 1.0)
        qd[rows, h // 2, P:] = gamma[h] ** (j % DS + 1.0)
    c["c_qd"] = qd.astype(np.float32)
    kd = np.zeros((P, RH + RH * DB))
    for h in range(RH):
        kd[:, h] = gamma[h] ** (P - 1.0 - i) * scale
        for b in range(DB):
            r = slice(b * DS, b * DS + DS)
            kd[r, RH + h * DB + b] = gamma[h] ** (DS - 1.0 - np.arange(DS)) * scale
    c["c_kd"] = kd.astype(np.float32)
    slope = 2.0 ** (-8.0 * np.arange(1, H + 1) / H)

    def bias(delta, sl):
        n = ((delta >= 0) & (delta <= 128)).astype(np.float64)
        n += (delta >= 0) & (delta <= 512) & (delta % 4 == 0)
        n += (delta >= 0) & (delta <= 2048) & (delta % 16 == 0)
        return np.where(n > 0, (np.log(np.maximum(n, 1)) - sl * delta) * DH ** 0.5, MASKED)

    x = np.arange(SEQ)
    c["c_bp"] = bias((SEQ - P) + i[None, :, None] - x[None, None, :], slope[:, None, None]).astype(np.float32)
    pos = sample_positions()
    hq_s = np.tile(np.arange(DS), H)
    hq_h = np.repeat(np.arange(H), DS)
    c["c_bs"] = bias(PAST + hq_s[:, None] - pos[None, :], slope[hq_h][:, None]).astype(np.float32)
    m = np.zeros((P, 4))
    m[i, (i // DS) % 4] = 1.0
    c["c_mask"] = m.astype(np.float32)
    return c


def sample_positions():
    a = np.arange(P)
    pos = [16 * a + r for r in range(8)]
    p = np.arange(P)
    for e in range(2):
        pos.append(1536 + 16 * (p % 32) + 8 + 2 * (p // 32) + e)
    pos.append(PAST + np.arange(DS))
    return np.concatenate(pos)


CONSTS = {k: v.shape for k, v in constants().items()}


def build(nc, a):
    ctx = ExitStack()
    base = (nc.sbuf_base + 31) // 32 * 32
    base = max(base, 16512)

    def at(name, off, shape, dt=F32):
        return nc.alloc_sbuf_tensor_at(name, shape, dt, offset=base + off)

    names = {}

    def sem(name):
        names[name] = ctx.enter_context(nc.semaphore(name))
        return names[name]

    TB = TW * 4
    TA = (TB + 31) // 32 * 32
    O_X, O_HH, O_HL = 0, KT * TB, 2 * KT * TB
    O_WH = 3 * KT * TB
    O_WL = O_WH + RING * BE * 4
    O_RAW = O_WL + RING * BE * 4
    O_C = O_RAW + BE * 4
    O_WORK = O_C + 2080
    X = at("x_res", O_X, [P, KT, TW])
    HHI = at("h_hi", O_HH, [P, KT, TW], F32R)
    HLO = at("h_lo", O_HL, [P, KT, TW], F32R)
    WHI = at("w_hi", O_WH, [P, RING, BE], F32R)
    WLO = at("w_lo", O_WL, [P, RING, BE], F32R)
    RAW = at("w_raw", O_RAW, [P, BE])
    ident = at("ident", O_C, [P, P])
    ones = at("ones", O_C + 512, [P, P])
    mean1 = at("mean1", O_C + 1024, [P, 2])
    vecr = at("vec_rows", O_WORK, [P, P])
    NV = 68
    vec = at("vec_cols", O_C + 1056, [P, NV])
    rtok = at("rtok", O_C + 1344, [P, NT, 2])
    gqk = at("gqk", O_C + 1440, [P, 2, DH])
    spl = at("spl", O_C + 1952, [P, 4, 4])
    mask4 = at("mask4", O_C + 2016, [P, 4])
    XN = at("x_natural", O_HH, [P, NT, D])
    G_MIX, G_FFN = (0, 8), (16, 24)
    V_CW, V_CB, V_BR, V_BI, V_LAM, V_RG = 32, 48, 52, 56, 60, 64

    PS = ctx.enter_context(nc.psum_tensor("psum", [P, 8, 512], F32))

    def dram(name, shape):
        return nc.dram_tensor(name, shape, F32, kind="Internal").ap()

    proj = dram("proj_t", [16, P, TW])
    vtok = dram("v_tok", [NT * P, LW])
    parkx = dram("park_x", [P, KT * TW])
    qtok = dram("q_tok", [NT * P, D])

    met = sem("stages_met")
    tick = {e: sem(f"tick_{e}") for e in ("pe", "act", "dve", "pool", "sp")}
    raw_in, wh_done, wl_done, pe_done = sem("raw_in"), sem("wh_done"), sem("wl_done"), sem("pe_done")

    def hold(eng, s, value, who):
        eng.wait_ge(s, value)
        if not isinstance(value, int):
            eng.sem_inc(tick[who], 1)

    def meet(eng, n):
        eng.drain().then_inc(met, 1)
        eng.wait_ge(met, 4 * n)

    def load_block(sp, n, src, wait=True):
        if wait:
            hold(sp, wl_done, n, "sp")
        sp.dma_start(RAW[:, :].rearrange("p (k c) -> p k c", k=src.shape[1]), src).then_inc(raw_in, 16)

    def columns(w, j):
        return w.rearrange("(k p) c -> p k c", p=P)[:, :, bass.ds(j * BW, BW)]

    def rows(w, g):
        return w[bass.ds(g * BW, BW), :].rearrange("(f p) c -> p f c", p=P)

    def split_hi(act, n, slot, first=False):
        if not first:
            hold(act, pe_done, n - RING + 1, "act")
        hold(act, raw_in, n * 16 + 16, "act")
        act.activation(WHI[:, slot, :], RAW[:, :], ACT.Copy).then_inc(wh_done, 1)

    def split_lo(dve, n, slot):
        hold(dve, wh_done, n + 1, "dve")
        dve.tensor_tensor(WLO[:, slot, :], RAW[:, :], WHI[:, slot, :].bitcast(F32),
                          ALU.subtract).then_inc(wl_done, 1)

    def fm_tile(pe, bank, slot, kcols, kind, hi, lo, done):
        nk = len(kcols)
        i = 0
        for k, wc in enumerate(kcols):
            for st, mv in ((WHI, hi), (WHI, lo), (WLO, hi)):
                for c in range(NCH):
                    mm = pe.matmul(PS[:, bank + c, 0:CW], st[:, slot, wc:wc + P],
                                   mv[:, k, c * CW:(c + 1) * CW],
                                   start=(i < NCH), stop=(i >= 3 * NCH * nk - NCH))
                    i += 1
        mm.then_inc(done, 1)
        return mm

    def col_tiles(m):
        return [k * BW + m * P for k in range(KT)]

    ld, vt_done, xt_in, xt_v, xt_a, cst = (sem(x) for x in
                                           ("loaded", "vec_turned", "x_turned", "x_out_dve", "x_out_act", "consts"))
    vt_out, pr_chain = sem("vec_out"), sem("prep_chain")

    def s1_pool(pool):
        pool.dma_start(ident[:, :], a["c_ident"]).then_inc(ld, 16)
        r = 0
        for name, n in (("norm_mix", 16), ("norm_ffn", 16), ("conv_w", 16), ("conv_b", 4), ("b_rgate", 4),
                        ("b_igate", 4), ("lru_lambda", 4)):
            src = a[name]
            src = (src[0] if name == "conv_w" else src).rearrange("a (k p) -> (a k) p", p=P)
            pool.dma_start(vecr[r:r + n, :], src).then_inc(ld, 16)
            r += n
        pool.dma_start(vecr[r:r + RH, :], a["ret_norm_g"][0]).then_inc(ld, 16)
        for i, name in enumerate(("q_norm_g", "k_norm_g")):
            pool.dma_start(gqk[:, i, :], a[name].to_broadcast([P, DH])).then_inc(ld, 16)
        pool.dma_start(mask4[:, :], a["c_mask"]).then_inc(ld, 16)
        x = a["x_prompt"][0].rearrange("(t p) c -> p t c", p=P)
        for t in range(0, QT, 2):
            pool.dma_start(XN[:, t:t + 2, :], x[:, t:t + 2, :]).then_inc(ld, 16)
        pool.dma_start(XN[P - NS:P, QT, :], a["x_sample"].rearrange("b s c -> (b s) c")).then_inc(ld, 16)
        pool.memset(ones[:, :], 1.0).then_inc(cst, 1)
        pool.memset(mean1[:, :], 1.0 / P).then_inc(cst, 1)
        pool.memset(X[:, :, SEQ:S0], 0.0).then_inc(cst, 1)

    N_LD = 12 + 5

    def s1_pe(pe):
        pe.wait_ge(ld, 16 * N_LD)
        pe.transpose(PS[:, 7, 0:NV], vecr[0:NV, :], ident[0:NV, 0:NV]).then_inc(vt_done, 1)
        for t in range(NT):
            if t >= 3:
                pe.wait_ge((xt_v, xt_a)[(t - 3) % 2], (t - 3) // 2 + 1)
            r0 = 0 if t < QT else P - NS
            for k in range(KT):
                mm = pe.transpose(PS[:, 2 * (t % 3) + k // 4, (k % 4) * P:(k % 4) * P + P - r0],
                                  XN[r0:P, t, k * P:(k + 1) * P], ident[r0:P, r0:P])
            mm.then_inc(xt_in, 1)

    def x_tile(t):
        r0 = 0 if t < QT else P - NS
        c0 = t * P if t < QT else S0
        src = PS[:, 2 * (t % 3):2 * (t % 3) + 2, :].rearrange("p a (k c) -> p (a k) c", c=P)
        return X[:, :, c0:c0 + P - r0], src[:, :, 0:P - r0]

    def s1_act(act):
        for n in range(RING):
            split_hi(act, n, n, first=True)
        for t in range(1, NT, 2):
            act.wait_ge(xt_in, t + 1)
            o, i = x_tile(t)
            act.activation(o, i, ACT.Copy).then_inc(xt_a, 1)

    def s1_dve(dve):
        for n in range(RING):
            split_lo(dve, n, n)
        dve.wait_ge(vt_done, 1)
        dve.tensor_copy(vec[:, :], PS[:, 7, 0:NV]).then_inc(vt_out, 1)
        for t in range(0, NT, 2):
            dve.wait_ge(xt_in, t + 1)
            o, i = x_tile(t)
            dve.tensor_copy(o, i).then_inc(xt_v, 1)

    R = at("rstd", O_WORK, [P, TW])
    VV = at("prep_v", O_WORK + 2 * TA, [P, TW])
    UU = at("prep_u", O_WORK + 3 * TA, [P, TW])
    SQ = at("prep_sq", O_WORK + 4 * TA, [P, 2, TW])

    PREP = {"sq_in": KT, "sq_used": KT, "hh_in": KT, "hl_in": KT, "stat": 1, "rchain": 6, "rroot": 1}
    prep_sem = {k: sem(k) for k in PREP}

    def prep_wait(eng, use, k, value):
        eng.wait_ge(prep_sem[k], use * PREP[k] + value)

    def prep_act(act, q, g):
        for k in range(KT):
            if k >= 2:
                prep_wait(act, q, "sq_used", k - 1)
            act.activation(SQ[:, k % 2, :], X[:, k, :], ACT.Square).then_inc(prep_sem["sq_in"], 1)
            act.activation(HHI[:, k, :], X[:, k, :], ACT.Copy, scale=vec[:, g + k:g + k + 1]).then_inc(prep_sem["hh_in"], 1)
        prep_wait(act, q, "rchain", 2)
        act.activation(R[:, :], UU[:, :], ACT.Sqrt).then_inc(prep_sem["rroot"], 1)

    def prep_dve(dve, q, g):
        for k in range(KT):
            prep_wait(dve, q, "hh_in", k + 1)
            dve.scalar_tensor_tensor(HLO[:, k, :], X[:, k, :], vec[:, g + k:g + k + 1],
                                     HHI[:, k, :].bitcast(F32), ALU.mult, ALU.subtract).then_inc(prep_sem["hl_in"], 1)
        c = prep_sem["rchain"]
        prep_wait(dve, q, "stat", 1)
        dve.tensor_scalar(VV[:, :].rearrange("p (c w) -> p c w", c=NCH), PS[:, 3:6, 0:CW], 1.0 / D, EPS,
                          ALU.mult, ALU.add).then_inc(c, 1)
        prep_wait(dve, q, "rchain", 1)
        dve.reciprocal(UU[:, :], VV[:, :]).then_inc(c, 1)
        prep_wait(dve, q, "rroot", 1)
        dve.tensor_tensor(UU[:, :], R[:, :], R[:, :], ALU.mult).then_inc(c, 1)
        prep_wait(dve, q, "rchain", 3)
        dve.tensor_tensor(UU[:, :], UU[:, :], VV[:, :], ALU.mult).then_inc(c, 1)
        prep_wait(dve, q, "rchain", 4)
        dve.tensor_scalar(UU[:, :], UU[:, :], -0.5, 1.5, ALU.mult, ALU.add).then_inc(c, 1)
        prep_wait(dve, q, "rchain", 5)
        dve.tensor_tensor(R[:, :], R[:, :], UU[:, :], ALU.mult).then_inc(c, 1)
        prep_wait(dve, q, "rchain", 6)

    def prep_pe(pe, q):
        for k in range(KT):
            prep_wait(pe, q, "sq_in", k + 1)
            for c in range(NCH):
                mm = pe.matmul(PS[:, 3 + c, 0:CW], ones[:, :], SQ[:, k % 2, c * CW:(c + 1) * CW],
                               start=(k == 0), stop=(k == KT - 1))
            mm.then_inc(prep_sem["sq_used"], 1)
            if k == KT - 1:
                prep_wait(pe, q, "sq_used", KT)
        pe.sem_inc(prep_sem["stat"], 1)
        prep_wait(pe, q, "hl_in", KT)

    def rtok_pe(pe, q, done):
        prep_wait(pe, q, "rchain", 6)
        for t in range(NT):
            mm = pe.matmul(PS[:, 7, 2 * t:2 * t + 2], R[:, win(t):win(t) + P], mean1[:, :], start=(t == 0),
                           stop=(t == NT - 1), skip_group_check=True)
        mm.then_inc(done, 1)

    q2 = 0
    fm_in, fm_out, tm_in, tm_out, rt_in, rt_out = (sem(x + "_in0") for x in
                                                   ("fm_in", "fm_out", "tm_in", "tm_out", "rt_in", "rt_out"))
    stg_out = [sem(f"stg_out{i}_in0") for i in range(2)]
    vst_out = [sem(f"vst_out{i}_in0") for i in range(2)]
    xpark = sem("x_parked_0")
    STG = at("in0_stage", O_WORK + 6 * TA, [P, 2, TW])
    VST = at("in0_vstage", O_WORK + 8 * TA, [P, 2, BW])

    def tm_unit(pe, bank, slot, t, done):
        w = win(t)
        i = 0
        for k in range(KT):
            for st, mv in ((HHI, WHI), (HHI, WLO), (HLO, WHI)):
                mm = pe.matmul(PS[:, bank, 0:BW], st[:, k, w:w + P], mv[:, slot, k * BW:(k + 1) * BW],
                               start=(i == 0), stop=(i == 3 * KT - 1))
                i += 1
        mm.then_inc(done, 1)
        return mm

    def s2_pe(pe):
        prep_pe(pe, q2)

        def block(idx, n, slot, first):
            hold(pe, wl_done, n + 1, "pe")
            for m in range(2):
                if first and m == 1:
                    prep_wait(pe, q2, "rchain", 1)
                if not first:
                    hold(pe, fm_out, idx + m - 1, "pe")
                mm = fm_tile(pe, 3 * m, slot, col_tiles(m), None, HHI, HLO, fm_in)
            return mm

        def finished(pe):
            pe.drain().then_inc(pe_done, 1)

        block(0, 0, 0, True); finished(pe)
        block(2, 1, 1, False); finished(pe)
        rtok_pe(pe, q2, rt_in)
        pe.wait_ge(rt_out, 1)
        u = 0
        for j in (2, 3):
            pe.wait_ge(wl_done, j + 1)
            for t in range(NT):
                if u >= 2:
                    pe.wait_ge(tm_out, u - 1)
                tm_unit(pe, 6 + u % 2, j % RING, t, tm_in)
                u += 1
            finished(pe)
        with pe.Fori(0, 2) as i:
            for jj in range(3):
                block(4 + i * 6 + 2 * jj, 4 + i * 3 + jj, (4 + jj) % RING, False)
                finished(pe)

    def s2_act(act):
        prep_act(act, q2, G_MIX[0])
        split_hi(act, 3, 0)
        split_hi(act, 4, 1)
        u = 0
        for j in (2, 3):
            for t in range(NT):
                act.wait_ge(tm_in, u + 1)
                if u == 0:
                    act.wait_ge(rt_out, 1)
                if u >= 2:
                    act.wait_ge(vst_out[u % 2], 16 * (u // 2))
                act.activation(VST[:, u % 2, :], PS[:, 6 + u % 2, 0:BW], ACT.Copy,
                               scale=rtok[:, t, 0:1]).then_inc(tm_out, 1)
                u += 1
            split_hi(act, j + 3, (j + 3) % RING)
        with act.Fori(0, 2) as i:
            for jj in range(3):
                split_hi(act, 7 + i * 3 + jj, (7 + jj) % RING)

    def s2_dve(dve):
        prep_dve(dve, q2, G_MIX[0])

        def evac(use, half, free):
            hold(dve, fm_in, use * 2 + half + 1, "dve")
            if free:
                hold(dve, stg_out[half], use * 16, "dve")
            dve.tensor_tensor(STG[:, half, :].rearrange("p (c w) -> p c w", c=NCH), PS[:, 3 * half:3 * half + 3, 0:CW],
                              R[:, :].rearrange("p (c w) -> p c w", c=NCH), ALU.mult).then_inc(fm_out, 1)

        evac(0, 0, False)
        evac(0, 1, False)
        split_lo(dve, 3, 0)
        evac(1, 0, True)
        evac(1, 1, True)
        dve.wait_ge(rt_in, 1)
        dve.tensor_copy(rtok[:, :, :], PS[:, 7, 0:2 * NT].rearrange("p (t e) -> p t e", e=2)).then_inc(rt_out, 1)
        for n in (4, 5, 6):
            split_lo(dve, n, n % RING)
        with dve.Fori(0, 2) as i:
            for jj in range(3):
                for m in range(2):
                    evac(2 + i * 3 + jj, m, True)
                split_lo(dve, 7 + i * 3 + jj, (7 + jj) % RING)

    def s2_pool(pool):
        pool.dma_start(parkx, X[:, :, :].rearrange("p k w -> p (k w)")).then_inc(xpark, 16)

        def out(idx, half):
            hold(pool, fm_out, idx + 1, "pool")
            pool.dma_start(proj[bass.ds(idx, 1), :, :].rearrange("a p w -> p (a w)"), STG[:, half, :]).then_inc(stg_out[half], 16)

        for i in range(4):
            out(i, i % 2)
        u = 0
        for j in (2, 3):
            for t in range(NT):
                pool.wait_ge(tm_out, u + 1)
                pool.dma_start(vtok[t * P:(t + 1) * P, (j - 2) * BW:(j - 1) * BW], VST[:, u % 2, :]).then_inc(vst_out[u % 2], 16)
                u += 1
        with pool.Fori(0, 6) as i:
            for half in range(2):
                out(4 + i * 2 + half, half)
        for half in range(2):
            pool.wait_ge(stg_out[half], 16 * 8)
            pool.wait_ge(vst_out[half], 16 * NT)
        pool.wait_ge(xpark, 16)

    stages = {e: [] for e in ("pe", "act", "dve", "pool")}

    def stage(pe, act, dve, pool):
        for e, f in zip(("pe", "act", "dve", "pool"), (pe, act, dve, pool)):
            stages[e].append(f)

    stage(s1_pe, s1_act, s1_dve, s1_pool)
    stage(s2_pe, s2_act, s2_dve, s2_pool)

    gam = [1.0 - 2.0 ** (-5.0 - h) for h in range(RH)]
    OTP = at("ret_o", O_X + 4 * TB, [P, RH, TW])
    VS = at("ret_vs", O_X, [P, RH * DV])
    KM = at("ret_km", O_X + 2048, [NS, DB, RH, DK])
    ATTS = at("ret_atts", O_X + 10240, [P, 2, 2, NS])
    KTS = at("ret_kts", O_X + 11264, [NS, RH, DK])
    QKS = at("ret_qks", O_X + 12288, [P, 2, 2, NS])
    QDS = at("ret_qds", O_X + 13312, [P, 2, NS])
    w = O_WORK
    S0S = at("ret_s0", w, [P, DB, 2, DV])
    DEC = at("ret_dec", w + 8192, [P, RH, P])
    DECS = at("ret_decs", w + 10240, [NS, RH, NS])
    QD = at("ret_qd", w + 11264, [P, 2, P + NS])
    KD = at("ret_kd", w + 12800, [P, RH + RH * DB])
    ST = at("ret_state", w + 12960, [P, 2, DV])
    QC = at("ret_q", w + 13984, [P, 2, 2, P])
    KC = at("ret_k", w + 16032, [P, 2, 2, P])
    VC = at("ret_v", w + 18080, [P, 2, RH * DV])
    ATT = at("ret_att", w + 22176, [P, 2, 2, P])
    KTOK = at("ret_ktok", w + 24224, [P, RH, DK])
    QDT = at("ret_qdt", w + 25248, [P, 2, P])
    NCHK = SEQ // P
    (r_cst, r_tab, r_kt, r_att, r_o, r_s, r_ktok, r_attr, r_qd, r_str, r_oo, r_so, r_sld, r_sstep) = (
        sem("ret_" + x) for x in ("cst", "tables", "kt_in", "att_in", "o_in", "s_in", "ktok_rdy", "att_rdy", "qd_rdy",
                                  "state_rdy", "o_out", "stored", "sample_in", "sample_steps"))
    r_ld = [sem(f"ret_chunk_in{i}") for i in range(2)]
    projc = proj.rearrange("m p w -> p m w")

    def par(h):
        return slice(DK * (h % 2), DK * (h % 2) + DK)

    def s3_pool(pool):
        pool.memset(OTP[:, :, SEQ:S0], 0.0).then_inc(r_cst, 1)
        pool.memset(ST[:, :, :], 0.0).then_inc(r_cst, 1)
        pool.memset(VS[:, :], 0.0).then_inc(r_cst, 1)
        pool.memset(ATTS[:, :, :, :], 0.0).then_inc(r_cst, 1)
        for t, c in ((DEC, "c_dec"), (DECS, "c_decs"), (QD, "c_qd")):
            src = a[c]
            pool.dma_start(t[:, :, :], src).then_inc(r_tab, 16)
        pool.dma_start(KD[:, :], a["c_kd"]).then_inc(r_tab, 16)

        def load(c, slot):
            pool.dma_start(QC[:, slot, :, :], projc[:, 0:2, bass.ds(c * P, P)]).then_inc(r_ld[slot], 16)
            pool.dma_start(KC[:, slot, :, :], projc[:, 2:4, bass.ds(c * P, P)]).then_inc(r_ld[slot], 16)
            pool.dma_start(VC[:, slot, :], vtok[bass.ds(c * P, P), :]).then_inc(r_ld[slot], 16)

        for slot in range(2):
            load(slot, slot)
        with pool.Fori(0, NCHK // 2 - 1) as i:
            for slot in range(2):
                hold(pool, r_s, 2 * i + slot + 1, "pool")
                load(2 * i + 2 + slot, slot)
        pool.wait_ge(r_cst, 3)
        pool.dma_start(VS[0:NS, :], vtok[(NT - 1) * P + P - NS:NT * P, :]).then_inc(r_sld, 16)
        for i in range(2):
            pool.dma_start(QKS[:, i, :, :], projc[:, 2 * i:2 * i + 2, S0:TW]).then_inc(r_sld, 16)
        s0 = a["state_ret"][0].rearrange("b (g e) k v -> g e k b v", e=2)
        for g in range(2):
            for e in range(2):
                pool.dma_start(S0S[e * DK:(e + 1) * DK, :, g, :], s0[g, e]).then_inc(r_sld, 16)
        pool.wait_ge(r_str, NCHK + 1)
        sp = a["ret_prompt"][0, 0].rearrange("(g e) k v -> e k g v", e=2)
        so = a["ret_sample"][0].rearrange("b (g e) k v -> g e k b v", e=2)
        for e in range(2):
            pool.dma_start(sp[e], ST[e * DK:(e + 1) * DK, :, :]).then_inc(r_so, 16)
        pool.wait_ge(r_sstep, 10)
        for g in range(2):
            for e in range(2):
                pool.dma_start(so[g, e], S0S[e * DK:(e + 1) * DK, :, g, :]).then_inc(r_so, 16)
        pool.wait_ge(r_so, 16 * 6)

    def s3_pe(pe):
        pe.wait_ge(r_cst, 4)
        pe.wait_ge(r_tab, 64)

        def chunk(i, s):
            c = 2 * i + s
            hold(pe, r_ld[s], i * 48 + 48, "pe")
            hold(pe, r_ktok, c + 1, "pe")
            for g in range(2):
                mm = pe.transpose(PS[:, 0, g * P:(g + 1) * P], KC[:, s, g, :], ident[:, :])
            mm.then_inc(r_kt, 1)
            hold(pe, r_attr, c + 1, "pe")
            for h in range(RH):
                mm = pe.matmul(PS[:, 1 + h % 2, (h // 2) * P:(h // 2 + 1) * P], KC[par(h), s, h // 2, :],
                               QC[par(h), s, h // 2, :], start=True, stop=True)
                if h >= 2:
                    mm.then_inc(r_att, 1)
            hold(pe, r_attr, c + 2, "pe")
            hold(pe, r_qd, c + 1, "pe")
            hold(pe, r_str, c + 1, "pe")
            hold(pe, r_oo, c + 1, "pe")
            for h in range(RH):
                o = PS[:, 3 + h % 2, (h // 2) * P:(h // 2 + 1) * P]
                pe.matmul(o, VC[:, s, h * DV:(h + 1) * DV], ATT[:, h % 2, h // 2, :], start=True, stop=False)
                mm = pe.matmul(o, ST[par(h), h // 2, :], QDT[par(h), h // 2, :], start=False, stop=True)
                if h >= 2:
                    mm.then_inc(r_o, 1)
            hold(pe, r_ktok, c + 2, "pe")
            for h in range(RH):
                mm = pe.matmul(PS[par(h), 5, (h // 2) * DV:(h // 2 + 1) * DV], KTOK[:, h, :],
                               VC[:, s, h * DV:(h + 1) * DV], start=True, stop=True)
            mm.then_inc(r_s, 1)

        with pe.Fori(0, NCHK // 2) as i:
            for s in range(2):
                chunk(i, s)
        pe.wait_ge(r_sld, 16 * 7)
        pe.wait_ge(r_ktok, NCHK + 1)
        for g in range(2):
            mm = pe.transpose(PS[0:NS, 0, g * P:(g + 1) * P], QKS[:, 1, g, :], ident[:, :])
        mm.then_inc(r_sstep, 1)
        for h in range(RH):
            mm = pe.matmul(PS[0:NS, 1 + h % 2, (h // 2) * NS:(h // 2 + 1) * NS], QKS[par(h), 1, h // 2, :],
                           QKS[par(h), 0, h // 2, :], start=True, stop=True)
            if h >= 2:
                mm.then_inc(r_sstep, 1)
        pe.wait_ge(r_sstep, 6)
        pe.wait_ge(r_oo, NCHK + 1)
        for h in range(RH):
            c0 = (h // 2) * NS
            pe.matmul(PS[:, 3 + h % 2, c0:c0 + NS], VS[:, h * DV:(h + 1) * DV], ATTS[:, h % 2, h // 2, :],
                      start=True, stop=False, skip_group_check=True)
            for b in range(DB):
                mm = pe.matmul(PS[:, 3 + h % 2, c0 + b * DS:c0 + (b + 1) * DS], S0S[par(h), b, h // 2, :],
                               QDS[par(h), h // 2, b * DS:(b + 1) * DS], start=False, stop=(b == DB - 1),
                               skip_group_check=True)
            if h >= 2:
                mm.then_inc(r_o, 1)
        pe.wait_ge(r_sstep, 7)
        for b in range(DB):
            for h in range(RH):
                c0 = ((b % 2) * 2 + h // 2) * DV
                mm = pe.matmul(PS[par(h), (0, 1, 2, 5)[b // 2], c0:c0 + DV], KM[:, b, h, :],
                               VS[0:NS, h * DV:(h + 1) * DV], start=True, stop=True)
        mm.then_inc(r_sstep, 1)

    def s3_act(act):
        act.sem_inc(r_ktok, 1)
        act.sem_inc(r_oo, 1)
        act.wait_ge(r_tab, 64)
        act.wait_ge(r_cst, 1)

        def chunk(c):
            hold(act, r_kt, c + 1, "act")
            for h in range(RH):
                i = act.activation(KTOK[:, h, :], PS[:, 0, h * DK:(h + 1) * DK], ACT.Copy, scale=KD[:, h:h + 1])
            i.then_inc(r_ktok, 1)
            hold(act, r_o, 2 * c + 2, "act")
            for e in range(2):
                out = OTP[:, :, bass.ds(c * P, P)].rearrange("p (g e) w -> p e g w", e=2)[:, e]
                i = act.activation(out, PS[:, 3 + e, 0:2 * P].rearrange("p (g w) -> p g w", g=2), ACT.Copy)
            i.then_inc(r_oo, 1)

        with act.Fori(0, NCHK) as c:
            chunk(c)
        act.wait_ge(r_o, 2 * NCHK + 2)
        for e in range(2):
            out = OTP[:, :, S0:TW].rearrange("p (g e) w -> p e g w", e=2)[:, e]
            act.activation(out, PS[:, 3 + e, 0:2 * NS].rearrange("p (g w) -> p g w", g=2), ACT.Copy)

    def s3_dve(dve):
        dve.wait_ge(r_cst, 2)
        dve.sem_inc(r_attr, 1)
        dve.sem_inc(r_str, 1)
        dve.wait_ge(r_tab, 64)
        dec = DEC[:, :, :].rearrange("p (g e) w -> p e g w", e=2)
        with dve.Fori(0, NCHK // 2) as i:
            for s in range(2):
                c = 2 * i + s
                hold(dve, r_att, 2 * c + 2, "dve")
                for e in range(2):
                    x = dve.tensor_tensor(ATT[:, e, :, :], PS[:, 1 + e, 0:2 * P].rearrange("p (g w) -> p g w", g=2),
                                          dec[:, e], ALU.mult)
                x.then_inc(r_attr, 1)
                dve.tensor_tensor(QDT[:, :, :], QC[:, s, :, :], QD[:, :, 0:P], ALU.mult).then_inc(r_qd, 1)
                hold(dve, r_s, c + 1, "dve")
                hold(dve, r_str, c + 1, "dve")
                for h in range(RH):
                    x = dve.scalar_tensor_tensor(ST[par(h), h // 2, :], ST[par(h), h // 2, :], gam[h] ** RS_CHUNK,
                                                 PS[par(h), 5, (h // 2) * DV:(h // 2 + 1) * DV], ALU.mult, ALU.add)
                x.then_inc(r_str, 1)
        dve.wait_ge(r_cst, 4)
        dve.wait_ge(r_sstep, 3)
        dve.tensor_tensor(QDS[:, :, :], QKS[:, 0, :, :], QD[:, :, P:P + NS], ALU.mult).then_inc(r_sstep, 1)
        decs = DECS[:, :, :].rearrange("p (g e) w -> p e g w", e=2)
        for e in range(2):
            dve.tensor_tensor(ATTS[0:NS, e, :, :], PS[0:NS, 1 + e, 0:2 * NS].rearrange("p (g w) -> p g w", g=2),
                              decs[:, e], ALU.mult).then_inc(r_sstep, 1)
        kdm = KD[0:NS, RH:RH + RH * DB].rearrange("p (h b) -> p b h", b=DB)
        for b in range(DB):
            x = dve.tensor_tensor(KM[:, b, :, :], PS[0:NS, 0, 0:RH * DK].rearrange("p (h k) -> p h k", h=RH),
                                  kdm[:, b, :].unsqueeze(2).to_broadcast([NS, RH, DK]), ALU.mult)
        x.then_inc(r_sstep, 1)
        dve.wait_ge(r_sstep, 8)
        for h in range(RH):
            for q, bank in enumerate((0, 1, 2, 5)):
                st = S0S[par(h), 2 * q:2 * q + 2, h // 2, :]
                src = PS[par(h), bank, :].rearrange("p (b g v) -> p b g v", b=2, g=2)[:, :, h // 2, :]
                x = dve.scalar_tensor_tensor(st, st, gam[h] ** DS, src, ALU.mult, ALU.add)
            if h >= 2:
                x.then_inc(r_sstep, 1)

    stage(s3_pe, s3_act, s3_dve, s3_pool)

    T1 = at("cmb_1", O_HH + 4 * TB, [P, RH, TW])
    T2 = at("cmb_2", O_HL + 4 * TB, [P, RH, TW])
    T3 = at("cmb_3", O_WORK, [P, RH, TW])
    T4 = at("cmb_4", O_WORK + 4 * TB, [P, RH, TW])
    c_sq, c_ps, c_v, c_ch, c_rt, c_gt, c_th, c_hh = (sem("cmb_" + x) for x in (
        "squares", "sums", "v", "chain", "root", "gate_in", "tanh", "hi"))

    def s4_pool(pool):
        pool.wait_ge(c_ps, RH)
        pool.dma_start(T1[:, :, :], proj[4:8].rearrange("m p w -> p m w")).then_inc(c_gt, 16)
        pool.wait_ge(c_gt, 16)

    def s4_act(act):
        for h in range(RH):
            act.activation(T1[:, h, :], OTP[:, h, :], ACT.Square).then_inc(c_sq, 1)
        act.wait_ge(c_ch, 1)
        act.activation(T4[:, :, :], T3[:, :, :], ACT.Sqrt).then_inc(c_rt, 1)
        act.wait_ge(c_gt, 16)
        act.wait_ge(c_ch, 5)
        act.activation(T3[:, :, :], T1[:, :, :], ACT.Tanh, scale=0.5).then_inc(c_th, 1)
        for h in range(RH):
            act.wait_ge(c_ch, 8 + 2 * h)
            act.activation(HHI[:, h, :], OTP[:, h, :], ACT.Copy, scale=0.5).then_inc(c_hh, 1)

    def s4_pe(pe):
        for h in range(RH):
            pe.wait_ge(c_sq, h + 1)
            if h >= 2:
                pe.wait_ge(c_v, h - 1)
            for c in range(NCH):
                mm = pe.matmul(PS[:, 3 * (h % 2) + c, 0:CW], ones[:, :], T1[:, h, c * CW:(c + 1) * CW],
                               start=True, stop=True)
            mm.then_inc(c_ps, 1)

    def s4_dve(dve):
        for h in range(RH):
            dve.wait_ge(c_ps, h + 1)
            dve.tensor_scalar(T2[:, h, :].rearrange("p (c w) -> p c w", c=NCH),
                              PS[:, 3 * (h % 2):3 * (h % 2) + 3, 0:CW], 1.0 / DV, EPS, ALU.mult, ALU.add).then_inc(c_v, 1)
        dve.wait_ge(c_v, RH)
        dve.reciprocal(T3[:, :, :], T2[:, :, :]).then_inc(c_ch, 1)
        dve.wait_ge(c_rt, 1)
        dve.tensor_tensor(T3[:, :, :], T4[:, :, :], T4[:, :, :], ALU.mult).then_inc(c_ch, 1)
        dve.wait_ge(c_ch, 2)
        dve.tensor_tensor(T3[:, :, :], T3[:, :, :], T2[:, :, :], ALU.mult).then_inc(c_ch, 1)
        dve.wait_ge(c_ch, 3)
        dve.tensor_scalar(T3[:, :, :], T3[:, :, :], -0.5, 1.5, ALU.mult, ALU.add).then_inc(c_ch, 1)
        dve.wait_ge(c_ch, 4)
        dve.tensor_tensor(T4[:, :, :], T4[:, :, :], T3[:, :, :], ALU.mult).then_inc(c_ch, 1)
        dve.wait_ge(c_th, 1)
        dve.scalar_tensor_tensor(T2[:, :, :], T3[:, :, :], 1.0, T1[:, :, :], ALU.add, ALU.mult).then_inc(c_ch, 1)
        dve.wait_ge(c_ch, 6)
        for h in range(RH):
            dve.scalar_tensor_tensor(OTP[:, h, :], OTP[:, h, :], vec[:, V_RG + h:V_RG + h + 1], T4[:, h, :],
                                     ALU.mult, ALU.mult).then_inc(c_ch, 1)
            dve.wait_ge(c_ch, 7 + 2 * h)
            dve.tensor_tensor(OTP[:, h, :], OTP[:, h, :], T2[:, h, :], ALU.mult).then_inc(c_ch, 1)
        for h in range(RH):
            dve.wait_ge(c_hh, h + 1)
            dve.scalar_tensor_tensor(HLO[:, h, :], OTP[:, h, :], 0.5, HHI[:, h, :].bitcast(F32), ALU.mult, ALU.subtract)

    stage(s4_pe, s4_act, s4_dve, s4_pool)

    w = O_X
    XPP = at("lru_x", w, [P, 2, CONV - 1 + SEQ])
    XPS = at("lru_xs", w + 8224, [P, 2, DB, CONV - 1 + DS])
    XC = at("lru_xc", w + 8928, [P, TW])
    A1 = at("lru_a1", w + 8928 + TA, [P, TW])
    A2 = at("lru_a2", w + 8928 + 2 * TA, [P, TW])
    A3 = at("lru_a3", w + 8928 + 3 * TA, [P, TW])
    A4 = at("lru_a4", w + 8928 + 4 * TA, [P, TW])
    w = O_WORK
    A5 = at("lru_a5", w, [P, TW])
    YL = at("lru_y", w + TA, [P, 2, TW])
    WR = at("lru_wr", w + 3 * TA, [P, 4, P])
    WI = at("lru_wi", w + 3 * TA + 2048, [P, 4, P])
    CR = at("lru_conv_rows", w + 3 * TA + 4096, [DB * 3, LW])
    HR = at("lru_h_rows", w + 3 * TA + 6144, [DB, LW])
    HT = at("lru_h0", w + 3 * TA + 8192, [P, 4, DB])
    CT = at("lru_conv0", w + 3 * TA + 8320, [P, 4, DB * 3])
    NO = 36
    GO = at("lru_out_cols", w + 3 * TA + 8704, [P, 4, NO])
    RO = at("lru_out_rows", w + 3 * TA + 9280, [NO, LW])
    SC = at("lru_sc", w + 3 * TA + 11328, [P, 8, 4])
    A6 = at("lru_a6", w + 3 * TA + 11456, [P, TW])
    A7 = at("lru_a7", w + 4 * TA + 11456, [P, TW])
    TMP = at("lru_tmp", w + 5 * TA + 11456, [P, DB])
    l_ld, l_st, l_ct, l_d, l_a, l_pe, l_out, l_rows, l_sp, l_z = (sem("lru_" + x) for x in (
        "consts_in", "start_turned", "start_out", "dve", "act", "pe", "rows_in", "stored", "softplus", "zero"))
    l_x = [sem(f"lru_tile_in{i}") for i in range(2)]
    GC = (2.0 / np.pi) ** 0.5

    def s5_pool(pool):
        pool.memset(XPP[:, :, 0:CONV - 1], 0.0).then_inc(l_z, 1)
        pool.memset(XC[:, SEQ:S0], 0.0).then_inc(l_z, 1)
        for t, n in ((WR, "w_rgate"), (WI, "w_igate")):
            pool.dma_start(t[:, :, :], a[n][0].rearrange("n i j -> i n j")).then_inc(l_ld, 16)
        pool.dma_start(CR[:, :], a["state_conv"][0].rearrange("b c w -> (b c) w")).then_inc(l_ld, 16)
        pool.dma_start(HR[:, :], a["state_lru"][0]).then_inc(l_ld, 16)

        def load(j):
            s = j % 2
            pool.dma_start(XPP[:, s, CONV - 1:], proj[8 + j, :, 0:SEQ]).then_inc(l_x[s], 16)
            pool.dma_start(XPS[:, s, :, CONV - 1:], proj[8 + j, :, S0:TW].rearrange("p (b s) -> p b s", b=DB)).then_inc(l_x[s], 16)
            pool.dma_start(YL[:, s, :], proj[12 + j]).then_inc(l_x[s], 16)

        load(0)
        load(1)
        for j in (2, 3):
            pool.wait_ge(l_d, ND * (j - 1))
            load(j)
        pool.wait_ge(l_out, 1)
        o = [("lru_prompt", 0, 1), ("lru_sample", 1, 9), ("conv_prompt", 9, 12), ("conv_sample", 12, 36)]
        for name, r0, r1 in o:
            dst = a[name][0] if name != "conv_sample" else a[name][0].rearrange("b c w -> (b c) w")
            if name == "conv_prompt":
                dst = dst[0]
            pool.dma_start(dst, RO[r0:r1, :]).then_inc(l_rows, 16)
        pool.wait_ge(l_rows, 64)

    def s5_pe(pe):
        pe.wait_ge(l_ld, 64)
        for j in range(4):
            pe.transpose(PS[:, 6, j * 24:(j + 1) * 24], CR[:, j * P:(j + 1) * P], ident[0:24, 0:24])
            mm = pe.transpose(PS[:, 6, 128 + j * DB:128 + (j + 1) * DB], HR[:, j * P:(j + 1) * P], ident[0:DB, 0:DB])
        mm.then_inc(l_st, 1)
        for j in range(4):
            pe.wait_ge(l_d, ND * j + 4)
            if j:
                pe.wait_ge(l_a, NA_ * (j - 1) + 4)
            for g, wt in enumerate((WR, WI)):
                for c in range(NCH):
                    mm = pe.matmul(PS[:, 3 * g + c, 0:CW], wt[:, j, :], XC[:, c * CW:(c + 1) * CW], start=True, stop=True)
                mm.then_inc(l_pe, 1)
        pe.wait_ge(l_d, ND * 4)
        for j in range(4):
            mm = pe.transpose(PS[0:NO, 7, j * P:(j + 1) * P], GO[:, j, :], ident[:, :])
        mm.then_inc(l_st, 1)

    ND, NA_ = 22, 8

    def s5_act(act):
        act.activation(SC[:, 0, :], vec[:, V_LAM:V_LAM + 4], ACT.Abs).then_inc(l_sp, 1)
        act.wait_ge(l_sp, 1)
        act.activation(SC[:, 1, :], SC[:, 0, :], ACT.Exp, scale=-1.0).then_inc(l_sp, 1)
        act.wait_ge(l_sp, 2)
        act.activation(SC[:, 2, :], SC[:, 1, :], ACT.Ln, bias=1.0).then_inc(l_sp, 1)
        act.wait_ge(l_sp, 6)
        v3 = lambda t: t.rearrange("p (c w) -> p c w", c=NCH)
        for j in range(4):
            s = j % 2
            n = NA_ * j
            act.wait_ge(l_x[s], 48 * (j // 2 + 1))
            act.wait_ge(l_z, 2)
            if j:
                act.wait_ge(l_d, ND * (j - 1) + 15)
            w3 = vec[:, V_CW + 12 + j:V_CW + 13 + j]
            cb = vec[:, V_CB + j:V_CB + j + 1]
            act.wait_ge(l_ct, 1)
            act.activation(XC[:, 0:SEQ], XPP[:, s, CONV - 1:], ACT.Identity, bias=cb, scale=w3).then_inc(l_a, 1)
            act.activation(XC[:, S0:TW].rearrange("p (b s) -> p b s", b=DB), XPS[:, s, :, CONV - 1:], ACT.Identity,
                           bias=cb, scale=w3).then_inc(l_a, 1)
            if j:
                act.wait_ge(l_d, ND * j)
            act.wait_ge(l_pe, 2 * j + 1)
            act.activation(v3(A1[:, :]), PS[:, 0:3, 0:CW], ACT.Tanh, bias=SC[:, 4, j:j + 1], scale=0.5).then_inc(l_a, 1)
            act.wait_ge(l_pe, 2 * j + 2)
            act.activation(v3(A2[:, :]), PS[:, 3:6, 0:CW], ACT.Tanh, bias=SC[:, 5, j:j + 1], scale=0.5).then_inc(l_a, 1)
            act.wait_ge(l_a, n + 3)
            act.activation(A1[:, :], A1[:, :], ACT.Tanh, bias=SC[:, 6, j:j + 1], scale=SC[:, 6, j:j + 1]).then_inc(l_a, 1)
            act.activation(A6[:, :], YL[:, s, :], ACT.Square).then_inc(l_a, 1)
            act.wait_ge(l_d, ND * j + 6)
            act.activation(A7[:, :], A7[:, :], ACT.Tanh, scale=GC).then_inc(l_a, 1)
            act.wait_ge(l_d, ND * j + 12)
            act.activation(A5[:, :], A5[:, :], ACT.Sqrt).then_inc(l_a, 1)
            act.wait_ge(l_d, ND * j + 21)
            act.activation(HHI[:, 4 + j, :], A7[:, :], ACT.Copy, scale=0.5).then_inc(l_sp, 1)

    def s5_dve(dve):
        dve.wait_ge(l_sp, 3)
        dve.tensor_scalar(SC[:, 3, :], vec[:, V_LAM:V_LAM + 4], -1.0, 0.0, ALU.mult, ALU.max).then_inc(l_sp, 1)
        dve.wait_ge(l_sp, 4)
        dve.tensor_tensor(SC[:, 7, :], SC[:, 3, :], SC[:, 2, :], ALU.add).then_inc(l_sp, 1)
        dve.tensor_scalar(SC[:, 4:6, :], vec[:, V_BR:V_BR + 8].rearrange("p (a b) -> p a b", a=2), 0.5, None, ALU.mult)
        dve.wait_ge(l_sp, 5)
        dve.tensor_scalar(SC[:, 6, :], SC[:, 7, :], LRU_C / 4, None, ALU.mult).then_inc(l_sp, 1)
        dve.wait_ge(l_st, 1)
        dve.tensor_copy(CT[:, :, :], PS[:, 6, 0:96].rearrange("p (j c) -> p j c", j=4)).then_inc(l_ct, 1)
        dve.tensor_copy(HT[:, :, :], PS[:, 6, 128:160].rearrange("p (j c) -> p j c", j=4)).then_inc(l_ct, 1)
        dve.wait_ge(l_ct, 2)
        for j in range(4):
            s = j % 2
            n = [ND * j]

            def step(x):
                x.then_inc(l_d, 1)
                n[0] += 1
                dve.wait_ge(l_d, n[0])

            xs = XC[:, S0:TW].rearrange("p (b s) -> p b s", b=DB)
            dve.wait_ge(l_x[s], 48 * (j // 2 + 1))
            step(dve.tensor_copy(XPS[:, s, :, 0:CONV - 1], CT[:, j, :].rearrange("p (b c) -> p b c", b=DB)))
            dve.wait_ge(l_a, NA_ * j + 2)
            for i in range(CONV - 1):
                wc = vec[:, V_CW + 4 * i + j:V_CW + 4 * i + j + 1]
                dve.scalar_tensor_tensor(XC[:, 0:SEQ], XPP[:, s, i:i + SEQ], wc, XC[:, 0:SEQ], ALU.mult, ALU.add)
                step(dve.scalar_tensor_tensor(xs, XPS[:, s, :, i:i + DS], wc, xs, ALU.mult, ALU.add))
            dve.wait_ge(l_a, NA_ * j + 6)
            y = YL[:, s, :]
            step(dve.scalar_tensor_tensor(A7[:, :], A6[:, :], 0.044715, y, ALU.mult, ALU.mult))
            step(dve.tensor_tensor(A7[:, :], A7[:, :], y, ALU.add))
            step(dve.tensor_scalar(A3[:, :], A1[:, :], 1.0, None, ALU.add))
            step(dve.reciprocal(A3[:, :], A3[:, :]))
            step(dve.tensor_scalar(A4[:, :], A1[:, :], -1.0, 1.0, ALU.mult, ALU.add))
            step(dve.tensor_tensor(A4[:, :], A4[:, :], A3[:, :], ALU.mult))
            step(dve.scalar_tensor_tensor(A5[:, :], A1[:, :], 2.0, A3[:, :], ALU.mult, ALU.mult))
            step(dve.scalar_tensor_tensor(A5[:, :], A4[:, :], 1.0, A5[:, :], ALU.add, ALU.mult))
            step(dve.scalar_tensor_tensor(A2[:, :], A2[:, :], 1.0, XC[:, :], ALU.add, ALU.mult))
            dve.wait_ge(l_a, NA_ * j + 8)
            step(dve.scalar_tensor_tensor(A2[:, :], A2[:, :], 0.5, A5[:, :], ALU.mult, ALU.mult))
            a0 = A4[:, S0:TW].rearrange("p (b s) -> p b s", b=DB)[:, :, 0]
            b0 = A2[:, S0:TW].rearrange("p (b s) -> p b s", b=DB)[:, :, 0]
            step(dve.tensor_tensor(TMP[:, :], a0, HT[:, j, :], ALU.mult))
            step(dve.tensor_tensor(b0, b0, TMP[:, :], ALU.add))
            step(dve.tensor_scalar(a0, a0, 0.0, None, ALU.mult))
            step(dve.tensor_tensor_scan(A3[:, :], A4[:, :], A2[:, :], 0.0, ALU.mult, ALU.add))
            dve.tensor_copy(GO[:, j, 0:1], A3[:, SEQ - 1:SEQ])
            dve.tensor_copy(GO[:, j, 1:1 + DB], A3[:, S0:TW].rearrange("p (b s) -> p b s", b=DB)[:, :, DS - 1])
            dve.tensor_copy(GO[:, j, 9:12], XPP[:, s, SEQ:SEQ + 3])
            step(dve.tensor_copy(GO[:, j, 12:NO].rearrange("p (b c) -> p b c", b=DB), XPS[:, s, :, DS:DS + 3]))
            step(dve.scalar_tensor_tensor(A7[:, :], A7[:, :], 1.0, y, ALU.add, ALU.mult))
            step(dve.tensor_tensor(A7[:, :], A7[:, :], A3[:, :], ALU.mult))
            dve.wait_ge(l_sp, 7 + j)
            step(dve.scalar_tensor_tensor(HLO[:, 4 + j, :], A7[:, :], 0.5, HHI[:, 4 + j, :].bitcast(F32),
                                          ALU.mult, ALU.subtract))
        dve.wait_ge(l_st, 2)
        dve.tensor_copy(RO[:, :], PS[0:NO, 7, :]).then_inc(l_out, 1)

    stage(s5_pe, s5_act, s5_dve, s5_pool)

    def out_projection(tag, n0, park):
        o_in, o_out, o_x = sem("tile_in_" + tag), sem("tile_out_" + tag), sem("x_back_" + tag)

        def pe_(pe):
            for j in range(N_OUT):
                pe.wait_ge(wl_done, n0 + j + 1)
                for m in range(2):
                    t = 2 * j + m
                    if t >= 2:
                        pe.wait_ge(o_out, t - 1)
                    fm_tile(pe, 3 * m, (n0 + j) % RING, col_tiles(m), None, HHI, HLO, o_in)
                pe.drain().then_inc(pe_done, 1)

        def act_(act):
            for j in range(N_OUT):
                split_hi(act, n0 + j + RING, (n0 + j) % RING)

        def dve_(dve):
            dve.wait_ge(o_x, 16)
            for j in range(N_OUT):
                for m in range(2):
                    t = 2 * j + m
                    dve.wait_ge(o_in, t + 1)
                    x = X[:, t, :].rearrange("p (c w) -> p c w", c=NCH)
                    dve.tensor_tensor(x, x, PS[:, 3 * m:3 * m + 3, 0:CW], ALU.add).then_inc(o_out, 1)
                split_lo(dve, n0 + j + RING, (n0 + j) % RING)

        def pool_(pool):
            pool.dma_start(X[:, :, :].rearrange("p k w -> p (k w)"), park).then_inc(o_x, 16)

        return pe_, act_, dve_, pool_

    stage(*out_projection("out0", B_OUT0, parkx))

    TG = at("ffn_t", O_WORK + TA, [P, TW])
    TT = at("ffn_t2", O_WORK + 2 * TA, [P, TW])
    GH = at("ffn_hi", O_WORK + 3 * TA, [P, 2, 2, TW], F32R)
    GL = at("ffn_lo", O_WORK + 3 * TA + 4 * TB, [P, 2, 2, TW], F32R)

    def ffn_load(sp, n0, layer):
        wg, wu, wd = a["w_ffn_gate"][layer], a["w_ffn_up"][layer], a["w_ffn_down"][layer]
        load_block(sp, n0, columns(wg, 0))
        load_block(sp, n0 + 1, columns(wu, 0))
        with sp.Fori(1, NG) as g:
            load_block(sp, n0 - 1 + 3 * g, columns(wg, g))
            load_block(sp, n0 + 3 * g, columns(wu, g))
            load_block(sp, n0 + 1 + 3 * g, rows(wd, g - 1))
        load_block(sp, n0 + 3 * NG - 1, rows(wd, NG - 1))

    def ffn(tag, n0, g_col, layer):
        q = 3 if layer else 1
        a_in, a_out, b_in, b_out, fch, fgh, gl_in = (sem(f"{x}_{tag}") for x in (
            "bank_a_in", "bank_a_out", "bank_b_in", "bank_b_out", "hidden_steps", "hidden_act", "hidden_lo"))
        sg, su, sd = ((n0 + i) % RING for i in (2, 0, 1))
        last = n0 + 3 * NG == NBLK
        v3 = lambda t: t.rearrange("p (c w) -> p c w", c=NCH)

        def pe_(pe):
            prep_pe(pe, q)

            def up(nb, slots, xa):
                hold(pe, wl_done, nb + 2, "pe")
                for f in range(2):
                    if not isinstance(xa, int) or xa + f > 0:
                        hold(pe, a_out, xa + f, "pe")
                    fm_tile(pe, 0, slots[0], col_tiles(f), None, HHI, HLO, a_in)
                    if f == 1:
                        pe.drain().then_inc(pe_done, 1)
                    if not isinstance(xa, int) or xa + f > 0:
                        hold(pe, b_out, xa + f, "pe")
                    else:
                        prep_wait(pe, q, "rchain", 1)
                    fm_tile(pe, 3, slots[1], col_tiles(f), None, HHI, HLO, b_in)
                pe.drain().then_inc(pe_done, 1)

            def down(g, nb, slot, par, xa):
                hold(pe, wl_done, nb + 1, "pe")
                hold(pe, gl_in, g * 2 + 2, "pe")
                for m in range(KT):
                    hold(pe, (a_out, b_out)[m % 2], xa + m // 2, "pe")
                    fm_tile(pe, 3 * (m % 2), slot, [f * D + m * P for f in range(2)], None, GH[:, par], GL[:, par],
                            (a_in, b_in)[m % 2])
                pe.drain().then_inc(pe_done, 1)

            def group(g, par):
                up(n0 - 1 + 3 * g, (sg, su), g * 6 - 4)
                down(g - 1, n0 + 1 + 3 * g, sd, 1 - par, g * 6 - 2)

            up(n0, (n0 % RING, (n0 + 1) % RING), 0)
            with pe.Fori(0, (NG - 3) // 2) as i:
                group(2 * i + 1, 1)
                group(2 * i + 2, 0)
            group(NG - 2, 1)
            group(NG - 1, 0)
            down(NG - 1, n0 + 3 * NG - 1, (n0 + 2) % RING, 0, 6 * NG - 4)

        def act_(act):
            prep_act(act, q, g_col)

            def hidden(x, par, f):
                hold(act, fch, x * 4 + 1, "act")
                act.activation(TT[:, :], TG[:, :], ACT.Tanh, scale=0.5).then_inc(fgh, 1)
                hold(act, fch, x * 4 + 4, "act")
                act.activation(GH[:, par, f, :], TG[:, :], ACT.Copy).then_inc(fgh, 1)

            def group(g, par, s):
                for f in range(2):
                    hidden(2 * g + f, par, f)
                for i, slot in enumerate((sg, su, sd)):
                    if i < s:
                        split_hi(act, n0 + 2 + 3 * g + i, slot)

            for f in range(2):
                hidden(f, 0, f)
            split_hi(act, n0 + 3, n0 % RING)
            split_hi(act, n0 + 4, (n0 + 1) % RING)
            with act.Fori(0, (NG - 3) // 2) as i:
                group(2 * i + 1, 1, 3)
                group(2 * i + 2, 0, 3)
            group(NG - 2, 1, 3)
            group(NG - 1, 0, 1 if last else 3)
            if not last:
                split_hi(act, n0 + 3 * NG + 2, (n0 + 2) % RING)

        def dve_(dve):
            prep_dve(dve, q, g_col)
            r3 = v3(R[:, :])

            def gate(x, xa):
                hold(dve, a_in, xa + 1, "dve")
                i = dve.tensor_tensor(v3(TG[:, :]), PS[:, 0:3, 0:CW], r3, ALU.mult)
                i.then_inc(fch, 1)
                hold(dve, fgh, x * 2 + 1, "dve")
                dve.sem_inc(a_out, 1)
                dve.scalar_tensor_tensor(TT[:, :], TT[:, :], 1.0, TG[:, :], ALU.add, ALU.mult).then_inc(fch, 1)

            def product(x, xa):
                hold(dve, b_in, xa + 1, "dve")
                hold(dve, fch, x * 4 + 2, "dve")
                dve.tensor_tensor(v3(TG[:, :]), PS[:, 3:6, 0:CW], r3, ALU.mult).then_inc(fch, 1)
                hold(dve, fch, x * 4 + 3, "dve")
                dve.scalar_tensor_tensor(TG[:, :], TT[:, :], 0.5, TG[:, :], ALU.mult, ALU.mult).then_inc(fch, 1)
                dve.sem_inc(b_out, 1)

            def low(x, par, f):
                hold(dve, fgh, x * 2 + 2, "dve")
                dve.tensor_tensor(GL[:, par, f, :], TG[:, :], GH[:, par, f, :].bitcast(F32), ALU.subtract).then_inc(gl_in, 1)
                hold(dve, gl_in, x + 1, "dve")

            def residual(m, xa):
                hold(dve, (a_in, b_in)[m % 2], xa + m // 2 + 1, "dve")
                x = v3(X[:, m, :])
                b0 = 3 * (m % 2)
                dve.tensor_tensor(x, x, PS[:, b0:b0 + 3, 0:CW], ALU.add).then_inc((a_out, b_out)[m % 2], 1)

            def group(g, par, s):
                x, xa = 2 * g, g * 6 - 4
                gate(x, xa)
                product(x, xa)
                low(x, par, 0)
                gate(x + 1, xa + 1)
                product(x + 1, xa + 1)
                residual(0, xa + 2)
                low(x + 1, par, 1)
                residual(1, xa + 2)
                residual(2, xa + 2)
                split_lo(dve, n0 + 2 + 3 * g, sg)
                residual(3, xa + 2)
                residual(4, xa + 2)
                if s > 1:
                    split_lo(dve, n0 + 3 + 3 * g, su)
                for m in (5, 6, 7):
                    residual(m, xa + 2)
                if s > 2:
                    split_lo(dve, n0 + 4 + 3 * g, sd)

            for f in range(2):
                gate(f, f)
                product(f, f)
                low(f, 0, f)
            split_lo(dve, n0 + 3, n0 % RING)
            split_lo(dve, n0 + 4, (n0 + 1) % RING)
            with dve.Fori(0, (NG - 3) // 2) as i:
                group(2 * i + 1, 1, 3)
                group(2 * i + 2, 0, 3)
            group(NG - 2, 1, 3)
            group(NG - 1, 0, 1 if last else 3)
            for m in range(KT):
                residual(m, 6 * NG - 4)
            if not last:
                split_lo(dve, n0 + 3 * NG + 2, (n0 + 2) % RING)

        def pool_(pool):
            pass

        return pe_, act_, dve_, pool_

    stage(*ffn("ffn0", B_FFN0, G_FFN[0], 0))

    q8 = 2
    (v_in, v_out, v_rt, v_ro, v_st, v_sq, v_nrm, v_park) = (sem("qkv_" + x) for x in (
        "unit_in", "unit_out", "rtok_in", "rtok_out", "steps", "root", "normed", "parked"))
    v_dma = [sem(f"qkv_stored{i}") for i in range(2)]
    AB = at("qkv_tok", O_WORK + TA, [P, 2, NT, BW])
    SB = at("qkv_sq", O_WORK + TA + 2 * NT * BW * 4, [P, NT, BW])
    NHB = BW // DH
    SSV = at("qkv_ss", O_WORK + TA + 3 * NT * BW * 4, [P, NT * NHB])
    SSR = at("qkv_rs", O_WORK + TA + 3 * NT * BW * 4 + 160, [P, NT * NHB])
    SSU = at("qkv_ru", O_WORK + TA + 3 * NT * BW * 4 + 320, [P, NT * NHB])
    BANKS = (6, 7, 0)

    def s8_pe(pe):
        prep_pe(pe, q8)
        rtok_pe(pe, q8, v_rt)
        pe.wait_ge(v_ro, 1)
        with pe.Fori(0, N_QKV // RING) as i:
            for jj in range(RING):
                hold(pe, wl_done, B_QKV + 1 + jj + i * RING, "pe")
                for t in range(NT):
                    hold(pe, v_out, i * (RING * NT) + (jj * NT + t + 1), "pe")
                    tm_unit(pe, BANKS[(jj * NT + t) % 3], (B_QKV + jj) % RING, t, v_in)
                pe.drain().then_inc(pe_done, 1)

    def s8_act(act):
        prep_act(act, q8, G_MIX[1])
        act.wait_ge(v_ro, 1)
        act.sem_inc(v_out, 3)

        def root(j):
            act.wait_ge(v_st, 9 * j + 4)
            act.activation(SSR[:, :], SSU[:, :], ACT.Sqrt).then_inc(v_sq, 1)

        for j in range(N_QKV):
            par = j % 2
            for t in range(NT):
                u = j * NT + t
                act.wait_ge(v_in, u + 1)
                if t == 0 and j >= 2:
                    act.wait_ge(v_dma[par], 32 * (j // 2))
                act.activation(AB[:, par, t, :], PS[:, BANKS[u % 3], 0:BW], ACT.Copy, scale=rtok[:, t, 0:1]).then_inc(v_out, 1)
                if t == 3 and 1 <= j <= 8:
                    root(j - 1)
            split_hi(act, B_QKV + j + RING, (B_QKV + j) % RING)

    def s8_dve(dve):
        prep_dve(dve, q8, G_MIX[1])
        dve.wait_ge(v_rt, 1)
        dve.tensor_copy(rtok[:, :, :], PS[:, 7, 0:2 * NT].rearrange("p (t e) -> p t e", e=2)).then_inc(v_ro, 1)
        for j in range(N_QKV):
            if j < 8:
                n = [9 * j]

                def step(x):
                    x.then_inc(v_st, 1)
                    n[0] += 1
                    dve.wait_ge(v_st, n[0])

                dve.wait_ge(v_out, 3 + NT * (j + 1))
                ab = AB[:, j % 2].rearrange("p t (h d) -> p (t h) d", h=NHB)
                step(dve.tensor_tensor(SB[:, :, :], AB[:, j % 2], AB[:, j % 2], ALU.mult))
                step(dve.tensor_reduce(SSV[:, :], SB[:, :, :].rearrange("p t (h d) -> p (t h) d", h=NHB), AX.X, ALU.add))
                step(dve.tensor_scalar(SSV[:, :], SSV[:, :], 1.0 / DH, EPS, ALU.mult, ALU.add))
                step(dve.reciprocal(SSU[:, :], SSV[:, :]))
                dve.wait_ge(v_sq, j + 1)
                step(dve.tensor_tensor(SSU[:, :], SSR[:, :], SSR[:, :], ALU.mult))
                step(dve.tensor_tensor(SSU[:, :], SSU[:, :], SSV[:, :], ALU.mult))
                step(dve.tensor_scalar(SSU[:, :], SSU[:, :], -0.5, 1.5, ALU.mult, ALU.add))
                step(dve.tensor_tensor(SSR[:, :], SSR[:, :], SSU[:, :], ALU.mult))
                step(dve.tensor_tensor(ab, ab, SSR[:, :].unsqueeze(2).to_broadcast([P, NT * NHB, DH]), ALU.mult))
                dve.tensor_tensor(ab, ab, gqk[:, j // 4, :].unsqueeze(1).to_broadcast([P, NT * NHB, DH]),
                                  ALU.mult).then_inc(v_nrm, 1)
            split_lo(dve, B_QKV + j + RING, (B_QKV + j) % RING)

    qp = qtok[0:SEQ, :].rearrange("(t p) c -> p t c", p=P)
    kp = a["k_prompt"][0, 0].rearrange("(t p) h d -> p t (h d)", p=P)
    vp = a["v_prompt"][0, 0].rearrange("(t p) h d -> p t (h d)", p=P)
    qs_, ks_, vs_ = (qtok[SEQ:SEQ + NS, :], a["k_sample"][0].rearrange("b s h d -> (b s) (h d)"),
                     a["v_sample"][0].rearrange("b s h d -> (b s) (h d)"))

    def s8_pool(pool):
        pool.dma_start(parkx, X[:, :, :].rearrange("p k w -> p (k w)")).then_inc(v_park, 16)
        for j in range(N_QKV):
            if j < 8:
                pool.wait_ge(v_nrm, j + 1)
            else:
                pool.wait_ge(v_out, 3 + NT * (j + 1))
            c = slice((j % 4) * BW, (j % 4 + 1) * BW)
            pool.dma_start((qp, kp, vp)[j // 4][:, :, c], AB[:, j % 2, 0:QT, :]).then_inc(v_dma[j % 2], 16)
            pool.dma_start((qs_, ks_, vs_)[j // 4][:, c], AB[P - NS:P, j % 2, QT, :]).then_inc(v_dma[j % 2], 16)
        for i in range(2):
            pool.wait_ge(v_dma[i], 32 * (N_QKV // 2))
        pool.wait_ge(v_park, 16)

    stage(s8_pe, s8_act, s8_dve, s8_pool)

    w = O_X
    QN = at("att_q", w, [P, QT, P])
    KN = at("att_k", w + 4096, [P, QT, P])
    VN = at("att_v", w + 8192, [P, 2, QT, P])
    SKQ = at("att_stack_q", w + 16384, [P, QT, P], F32R)
    SKH = at("att_stack_kh", w + 20480, [P, QT, P], F32R)
    SKL = at("att_stack_kl", w + 24576, [P, QT, P], F32R)
    w = O_WORK
    QS = at("att_qs", w, [P, SEQ], F32R)
    KHH = at("att_khh", w + 4096, [P, SEQ], F32R)
    KLL = at("att_kll", w + 8192, [P, SEQ], F32R)
    BI = at("att_bias", w + 12288, [P, 2, SEQ])
    SX = at("att_scores", w + 20480, [P, 2, SEQ])
    PT = at("att_pt", w + 28672, [P, 2, QT, P])
    OO = at("att_o", w + 36864, [P, QT, P])
    NBM = at("att_max", w + 40960, [P, 4])
    DEN = at("att_den", w + 40992, [P, 4])
    RDN = at("att_rden", w + 41024, [P, 4])
    (a_s, a_red, a_p, a_tp, a_tv, a_ta, a_oi, a_oo, a_sa, a_sv, a_qk, a_hh, a_rd, a_kh) = (sem("att_" + x) for x in (
        "scores_in", "scores_max", "probs", "turned", "taken_dve", "taken_act", "out_in", "out_done", "split_act",
        "split_dve", "qk_loaded", "out_hi", "rden", "kh"))
    a_vl = [sem(f"att_v_loaded{i}") for i in range(2)]
    a_bl = [sem(f"att_bias_loaded{i}") for i in range(2)]
    NST = 4 * QT

    units = []
    for n in range(NST + 2):
        if n < NST and n % QT == 0:
            units += [("stack", n // QT, arr, half, "a") for arr in range(3) for half in range(2)]
        if 1 <= n <= NST:
            qb = (n - 1) % QT
            units.append(("p", n - 1, 0, 0, "v"))
            if qb >= 4:
                units.append(("p", n - 1, 1, 0, "a"))
        if n >= 2 and (n - 2) % (2 * QT) == 2 * QT - 1:
            units += [("out", (n - 2) // (2 * QT), half, 0, "v") for half in range(2)]
    taken = {"v": 0, "a": 0}
    after = []
    for x in units:
        taken[x[4]] += 1
        after.append(taken[x[4]])
    NU, NV_, NA2 = len(units), taken["v"], taken["a"]

    def unit_at(key):
        return next(u for u, x in enumerate(units) if x[:len(key)] == key)

    def s9_pe(pe):
        pe.sem_inc(tick["pe"], 1)
        with pe.Fori(0, 4) as i:
            def turn(u, srcs):
                if u >= 2:
                    e = units[u - 2][4]
                    hold(pe, (a_tv if e == "v" else a_ta), i * (NV_ if e == "v" else NA2) + after[u - 2], "pe")
                for x, src in enumerate(srcs):
                    mm = pe.transpose(PS[:, 4 + u % 2, x * P:(x + 1) * P], src, ident[:, :])
                mm.then_inc(a_tp, 1)

            for n in range(NST + 2):
                if n < NST and n % QT == 0:
                    hh = n // QT
                    hold(pe, a_sa, i * 4 + hh + 1, "pe")
                    hold(pe, a_sv, i * 4 + hh + 1, "pe")
                    for arr, t in enumerate((SKQ, SKH, SKL)):
                        for half in range(2):
                            turn(unit_at(("stack", hh, arr, half)),
                                 [t[:, x, :].bitcast(F32) for x in range(4 * half, 4 * half + 4)])
                if n < NST:
                    hh, qb = divmod(n, QT)
                    if qb == 0:
                        hold(pe, a_ta, i * NA2 + after[unit_at(("stack", hh, 2, 1))], "pe")
                    if n >= 2:
                        hold(pe, a_red, i * NST + n - 1, "pe")
                    W = (qb + 1) * P
                    for ps_, t in enumerate((KHH, KLL)):
                        for c in range(0, W, 512):
                            mm = pe.matmul(PS[:, 2 * (n % 2) + c // 512, 0:min(512, W - c)], QS[:, qb * P:(qb + 1) * P],
                                           t[:, c:min(W, c + 512)], start=(ps_ == 0), stop=(ps_ == 1))
                    mm.then_inc(a_s, 1)
                if 1 <= n <= NST:
                    m = n - 1
                    hold(pe, a_p, i * NST + m + 1, "pe")
                    qb = m % QT
                    for g in range(1 + (qb >= 4)):
                        turn(unit_at(("p", m, g)), [SX[:, m % 2, x * P:(x + 1) * P]
                                                    for x in range(4 * g, min(qb + 1, 4 * g + 4))])
                if n >= 2:
                    m = n - 2
                    hh, qb = divmod(m, QT)
                    hold(pe, a_tv, i * NV_ + after[unit_at(("p", m, 0))], "pe")
                    if qb >= 4:
                        hold(pe, a_ta, i * NA2 + after[unit_at(("p", m, 1))], "pe")
                    if m >= 2:
                        hold(pe, a_oo, i * NST + m - 1, "pe")
                    if m % (2 * QT) == 0:
                        hold(pe, a_vl[hh // 2], i * 16 + 16, "pe")
                    for x in range(qb + 1):
                        mm = pe.matmul(PS[:, 6 + m % 2, 0:DH], PT[:, m % 2, x, :],
                                       VN[:, hh // 2, x, (hh % 2) * DH:(hh % 2 + 1) * DH], start=(x == 0), stop=(x == qb))
                    mm.then_inc(a_oi, 1)
                    if m % (2 * QT) == 2 * QT - 1:
                        hold(pe, a_oo, i * NST + m + 1, "pe")
                        for half in range(2):
                            turn(unit_at(("out", hh // 2, half)), [OO[:, x, :] for x in range(4 * half, 4 * half + 4)])
            hold(pe, a_tv, i * NV_ + NV_, "pe")
            hold(pe, a_ta, i * NA2 + NA2, "pe")

    def ps4(u, n=4):
        return PS[:, 4 + u % 2, 0:n * P]

    def s9_act(act):
        with act.Fori(0, 4) as i:
            def split(hh):
                hold(act, a_qk, i * 64 + 32 * (hh // 2 + 1), "act")
                if hh:
                    hold(act, a_tp, i * NU + unit_at(("stack", hh - 1, 2, 1)) + 1, "act")
                e = slice((hh % 2) * DH, (hh % 2 + 1) * DH)
                act.activation(SKQ[:, :, 0:DH], QN[:, :, e], ACT.Copy)
                for r in range(2):
                    x = act.activation(SKH[:, :, r * DH:(r + 1) * DH], KN[:, :, e], ACT.Copy)
                x.then_inc(a_sa, 1)

            split(0)
            for n in range(NST + 2):
                if n < NST and n % QT == 0:
                    hh = n // QT
                    if hh:
                        hold(act, a_s, i * NST + n, "act")
                    for arr, t in enumerate((QS, KHH, KLL)):
                        for half in range(2):
                            u = unit_at(("stack", hh, arr, half))
                            hold(act, a_tp, i * NU + u + 1, "act")
                            act.activation(t[:, half * 512:(half + 1) * 512], ps4(u), ACT.Copy).then_inc(a_ta, 1)
                if n < NST:
                    W = (n % QT + 1) * P
                    hold(act, a_red, i * NST + n + 1, "act")
                    act.activation(SX[:, n % 2, 0:W], SX[:, n % 2, 0:W], ACT.Exp, bias=NBM[:, n % 4:n % 4 + 1],
                                   scale=-1.0, accum_out=DEN[:, n % 4:n % 4 + 1]).then_inc(a_p, 1)
                if 1 <= n <= NST and (n - 1) % QT >= 4:
                    m = n - 1
                    qb = m % QT
                    u = unit_at(("p", m, 1))
                    hold(act, a_tp, i * NU + u + 1, "act")
                    hold(act, a_oi, i * NST + m - 1, "act")
                    act.activation(PT[:, m % 2, 4:qb + 1, :], ps4(u, qb - 3).rearrange("p (x w) -> p x w", w=P),
                                   ACT.Copy).then_inc(a_ta, 1)
                if n < NST and n % QT == 4 and n // QT < 3:
                    split(n // QT + 1)
                if n >= 2 and (n - 2) % (2 * QT) == 2 * QT - 1:
                    pp = (n - 2) // (2 * QT)
                    for half in range(2):
                        u = unit_at(("out", pp, half))
                        hold(act, a_tp, i * NU + u + 1, "act")
                        act.activation(HHI[:, bass.ds(i * 2 + pp, 1), half * 512:(half + 1) * 512].rearrange("p a w -> p (a w)"),
                                       ps4(u), ACT.Copy).then_inc(a_hh, 1)

    def s9_dve(dve):
        with dve.Fori(0, 4) as i:
            def split(hh):
                hold(dve, a_sa, i * 4 + hh + 1, "dve")
                e = slice((hh % 2) * DH, (hh % 2 + 1) * DH)
                dve.tensor_tensor(SKQ[:, :, DH:P], QN[:, :, e], SKQ[:, :, 0:DH].bitcast(F32), ALU.subtract)
                for r in range(2):
                    x = dve.tensor_tensor(SKL[:, :, r * DH:(r + 1) * DH], KN[:, :, e], SKH[:, :, 0:DH].bitcast(F32),
                                          ALU.subtract)
                x.then_inc(a_sv, 1)

            split(0)
            for n in range(NST + 2):
                if n < NST:
                    hh, qb = divmod(n, QT)
                    W = (qb + 1) * P
                    hold(dve, a_s, i * NST + n + 1, "dve")
                    if qb == 0:
                        hold(dve, a_bl[hh % 2], i * 32 + 16 * (hh // 2 + 1), "dve")
                    src = PS[:, 2 * (n % 2):2 * (n % 2) + 2, :].rearrange("p a w -> p (a w)")[:, 0:W]
                    dve.tensor_tensor_reduce(SX[:, n % 2, 0:W], src, BI[:, hh % 2, SEQ - W:SEQ], -(DH ** -0.5), 3.0e38,
                                             ALU.add, ALU.min, NBM[:, n % 4:n % 4 + 1]).then_inc(a_red, 1)
                if 1 <= n <= NST:
                    m = n - 1
                    k = min(m % QT + 1, 4)
                    u = unit_at(("p", m, 0))
                    hold(dve, a_tp, i * NU + u + 1, "dve")
                    if m >= 2:
                        hold(dve, a_oi, i * NST + m - 1, "dve")
                    dve.tensor_copy(PT[:, m % 2, 0:k, :], ps4(u, k).rearrange("p (x w) -> p x w", w=P)).then_inc(a_tv, 1)
                if n < NST and n % QT == 4 and n // QT < 3:
                    split(n // QT + 1)
                if n >= 2:
                    m = n - 2
                    hh, qb = divmod(m, QT)
                    hold(dve, a_p, i * NST + m + 1, "dve")
                    dve.reciprocal(RDN[:, m % 4:m % 4 + 1], DEN[:, m % 4:m % 4 + 1]).then_inc(a_rd, 1)
                    hold(dve, a_rd, i * NST + m + 1, "dve")
                    hold(dve, a_oi, i * NST + m + 1, "dve")
                    dve.tensor_scalar(OO[:, qb, (hh % 2) * DH:(hh % 2 + 1) * DH], PS[:, 6 + m % 2, 0:DH],
                                      RDN[:, m % 4:m % 4 + 1], None, ALU.mult).then_inc(a_oo, 1)
                    if m % (2 * QT) == 2 * QT - 1:
                        pp = hh // 2
                        for half in range(2):
                            hold(dve, a_hh, i * 4 + pp * 2 + half + 1, "dve")
                            u = unit_at(("out", pp, half))
                            o = (bass.ds(i * 2 + pp, 1), slice(half * 512, (half + 1) * 512))
                            dve.tensor_tensor(HLO[:, o[0], o[1]].rearrange("p a w -> p (a w)"), ps4(u),
                                              HHI[:, o[0], o[1]].rearrange("p a w -> p (a w)").bitcast(F32),
                                              ALU.subtract).then_inc(a_tv, 1)

    def s9_pool(pool):
        def pair(view, hp):
            return view[:, :, bass.ds(hp * P, P)]

        def load_qk(hp):
            pool.dma_start(QN[:, :, :], pair(qp, hp)).then_inc(a_qk, 16)
            pool.dma_start(KN[:, :, :], pair(kp, hp)).then_inc(a_qk, 16)

        def load_v(hp, slot):
            pool.dma_start(VN[:, slot, :, :], pair(vp, hp)).then_inc(a_vl[slot], 16)

        def load_b(h, slot):
            pool.dma_start(BI[:, slot, :], a["c_bp"][bass.ds(h, 1), :, :].rearrange("a p w -> p (a w)")).then_inc(a_bl[slot], 16)

        load_qk(0)
        load_b(0, 0)
        load_b(1, 1)
        load_v(0, 0)
        load_v(1, 1)

        def pairs(i, last):
            for hh in range(4):
                if hh == 1:
                    hold(pool, a_sv, i * 4 + 2, "pool")
                    load_qk(i * 2 + 1)
                if hh == 3 and not last:
                    hold(pool, a_sv, i * 4 + 4, "pool")
                    load_qk(i * 2 + 2)
                if hh < 2 or not last:
                    hold(pool, a_red, i * NST + (hh + 1) * QT, "pool")
                    load_b(i * 4 + hh + 2, hh % 2)
                if hh % 2 and not last:
                    hold(pool, a_oi, i * NST + (hh + 1) * QT, "pool")
                    load_v(i * 2 + 2 + hh // 2, hh // 2)

        with pool.Fori(0, 3) as i:
            pairs(i, False)
        pairs(3, True)

    stage(s9_pe, s9_act, s9_dve, s9_pool)

    NU10 = 5
    UROW = 2 * P
    NPOS = NU10 * UROW + DS
    NQ = 4 * DS
    NZ, NZA, NZD = 23, 12, 11
    NSC = NU10 + 1
    UNIT = [at(f"cache_unit{u}", O_X + u * 8192 if u < 4 else O_WORK, [P, 2, D]) for u in range(NU10)]
    OALL = at("smp_out", O_X + 4 * 8192, [P, DB * DH])
    w = O_WORK + 8192
    KTS = at("smp_kt", w, [P, 2, HP, UROW])
    QSN = at("smp_q_rows", w, [NS, D])
    KSN = at("smp_k_rows", w + 8192, [NS, D])
    ODUP = at("smp_out_twice", w, [P, DB, 2, DH])
    w += 16384
    SS = at("smp_scores", w, [P, NPOS])
    O4 = at("smp_out4", w, [P, 4, DH])
    w += (NPOS * 4 + 31) // 32 * 32
    PTS = at("smp_pt", w, [P, 2 * NU10 + 1, P])
    w += 11 * 512
    BSS = at("smp_bias", w, [P, NPOS])
    w += (NPOS * 4 + 31) // 32 * 32
    QB = at("smp_q_blocks", w, [P, HP, NQ])
    QTS = at("smp_qt", w + 1024, [P, HP, NS])
    VNB = at("smp_v_new", w + 3072, [DS, D])
    KNB = at("smp_k_new", w + 7168, [P, HP, DS])
    KTNF = at("smp_ktn", O_HH, [P, KT, TW])
    KTN = KTNF[:, :, S0:TW]
    w = O_X + 4 * 8192 + 2048
    NMN = at("smp_min", w, [P, 1])
    DNS = at("smp_den", w + 32, [P, 1])
    RDS = at("smp_rden", w + 64, [P, 1])
    (b_ld, b_qk, b_qt, b_qb, b_z, b_za, b_zd, b_sc, b_red, b_p, b_rd, b_ku, b_vu, b_pv, b_o4, b_oc, b_du, b_dt, b_hh, b_qc) = (
        sem("smp_" + x) for x in (
            "rows_in", "qk_turned", "qk_out", "q_blocks", "turned", "out_act", "out_dve", "scores", "reduced", "probs",
            "rden", "k_used", "v_used", "pv", "weighed", "summed", "twice", "out_turned", "hi", "q_copies"))
    b_unit = [sem(f"smp_unit_in{u}") for u in range(NU10)]
    b_vn = sem("smp_v_new_in")

    def cache_load(sp):
        sp.wait_ge(met, 4 * 9)
        sp.sem_inc(b_vu, NU10)
        with sp.Fori(0, DB) as b:
            for name, used in (("cache_k", b_vu), ("cache_v", b_ku)):
                src = a[name][0].rearrange("b (a r) h d -> a b r (h d)", r=16)
                for u in range(NU10):
                    hold(sp, used, b * NU10 + u + 1, "sp")
                    if u < 4:
                        sp.dma_start(UNIT[u][:, :, :], src[:, bass.ds(b, 1), 2 * u:2 * u + 2, :].rearrange(
                            "a b r c -> a (b r) c")).then_inc(b_unit[u], 16)
                    else:
                        for j in range(4):
                            sp.dma_start(UNIT[u][32 * j:32 * j + 32, :, :],
                                         src[P - 32:P, bass.ds(b, 1), 8 + 2 * j:10 + 2 * j, :].rearrange(
                                             "a b r c -> a (b r) c")).then_inc(b_unit[u], 16)
            sp.dma_start(VNB[:, :], a["v_sample"][0][bass.ds(b, 1)].rearrange("a s h d -> (a s) (h d)")).then_inc(b_vn, 16)

    def s10_pool(pool):
        pool.dma_start(QSN[:, :], qtok[SEQ:SEQ + NS, :]).then_inc(b_ld, 16)
        pool.dma_start(KSN[:, :], a["k_sample"][0].rearrange("b s h d -> (b s) (h d)")).then_inc(b_ld, 16)
        pool.dma_start(BSS[:, :], a["c_bs"]).then_inc(b_ld, 16)
        pool.memset(QB[:, :, :], 0.0).then_inc(b_qb, 1)
        pool.wait_ge(b_qb, 1)
        pool.wait_ge(b_qt, 2)
        pool.sem_inc(b_sc, 1)
        with pool.Fori(0, DB) as b:
            hold(pool, b_sc, b * NSC + 1, "pool")
            for hpar in range(2):
                for e in range(2):
                    c = (2 * hpar + e) * DS
                    r = slice(e * DH, (e + 1) * DH)
                    pool.tensor_copy(QB[r, :, :].rearrange("p (g t) c -> p g t c", t=2)[:, :, hpar, c:c + DS],
                                     QTS[r, :, bass.ds(b * DS, DS)].rearrange("p (g t) c -> p g t c", t=2)[
                                         :, :, hpar, :]).then_inc(b_qc, 1)
                    hold(pool, b_qc, b * 4 + 2 * hpar + e + 1, "pool")
            x = pool.tensor_copy(KNB[:, :, :], KTNF[:, :, bass.ds(b * DS + S0, DS)])
            x.then_inc(b_qb, 1)
        pool.wait_ge(b_ld, 48)

    def s10_pe(pe):
        pe.wait_ge(b_ld, 48)
        for i, t in enumerate((QSN, KSN)):
            for hp in range(HP):
                mm = pe.transpose(PS[:, 3 + i, hp * NS:(hp + 1) * NS], t[:, hp * P:(hp + 1) * P], ident[0:NS, 0:NS])
            mm.then_inc(b_qk, 1)
        pe.wait_ge(b_qt, 2)

        def scores(rhs, bank, c0, n):
            for i in range(2):
                for g in range(4):
                    mm = pe.matmul(PS[NQ * g:NQ * (g + 1), bank, c0:c0 + n], QB[:, 2 * g + i, :], rhs(2 * g + i),
                                   start=(i == 0), stop=(i == 1), tile_position=(0, NQ * g))
            mm.then_inc(b_sc, 1)

        with pe.Fori(0, DB) as b:
            def free(z):
                if z >= 4:
                    hold(pe, (b_za, b_zd)[z % 2], b * (NZA, NZD)[z % 2] + (z - 4) // 2 + 1, "pe")

            for u in range(NU10 + 1):
                if u < NU10:
                    n = 16 if u < 4 else 64
                    hold(pe, b_unit[u], b * 2 * n + n, "pe")
                    for c in range(4):
                        z = 4 * u + c
                        free(z)
                        for x in range(4):
                            hp, e = 2 * c + x // 2, x % 2
                            mm = pe.transpose(PS[:, 3 + z % 4, x * P:(x + 1) * P], UNIT[u][:, e, hp * P:(hp + 1) * P],
                                              ident[:, :])
                        mm.then_inc(b_z, 1)
                    hold(pe, b_z, b * NZ + 4 * u + 4, "pe")
                    pe.sem_inc(b_ku, 1)
                if u:
                    if u == 1:
                        hold(pe, b_qb, b + 2, "pe")
                    hold(pe, b_za, b * NZA + 2 * u, "pe")
                    hold(pe, b_zd, b * NZD + 2 * u, "pe")
                    v = u - 1
                    scores(lambda hp: KTS[:, v % 2, hp, :], v // 2, (v % 2) * UROW, UROW)
            scores(lambda hp: KNB[:, hp, :], 2, UROW, DS)
            hold(pe, b_p, b + 1, "pe")
            for z in (20, 21, 22):
                free(z)
                for x in range(4 if z < 22 else 2):
                    t = 4 * (z - 20) + x
                    mm = pe.transpose(PS[:, 3 + z % 4, x * P:(x + 1) * P], SS[:, t * P:(t + 1) * P], ident[:, :])
                if z == 22:
                    mm = pe.transpose(PS[0:DS, 3 + z % 4, 2 * P:3 * P], SS[:, 10 * P:NPOS], ident[:, :])
                mm.then_inc(b_z, 1)
            hold(pe, b_za, b * NZA + NZA, "pe")
            hold(pe, b_zd, b * NZD + NZD, "pe")
            hold(pe, b_vn, b * 16 + 16, "pe")
            for i, t in enumerate([10] + list(range(10))):
                r = DS if t == 10 else P
                if t < 10 and t % 2 == 0:
                    n = 16 if t < 8 else 64
                    hold(pe, b_unit[t // 2], b * 2 * n + 2 * n, "pe")
                for g in range(4):
                    rhs = VNB[:, 256 * g:256 * (g + 1)] if t == 10 else UNIT[t // 2][:, t % 2, 256 * g:256 * (g + 1)]
                    mm = pe.matmul(PS[NQ * g:NQ * (g + 1), 7, 0:256], PTS[0:r, t, NQ * g:NQ * (g + 1)], rhs,
                                   start=(i == 0), stop=(i == 10), tile_position=(0, NQ * g))
                if t < 10 and t % 2:
                    mm.then_inc(b_vu, 1)
            pe.drain().then_inc(b_pv, 1)
            hold(pe, b_o4, b + 1, "pe")
        pe.wait_ge(b_du, 2)
        for b in range(DB):
            mm = pe.transpose(PS[:, 3 + b // 4, (b % 4) * P:(b % 4 + 1) * P],
                              ODUP[:, b, :, :].rearrange("p a d -> p (a d)"), ident[:, :])
        mm.then_inc(b_dt, 1)

    def s10_out(z, eng, copy, done, b):
        hold(eng, b_z, b * NZ + z + 1, "act" if done is b_za else "dve")
        u = z // 4
        src = PS[:, 3 + z % 4, :]
        if z < 20:
            if u >= 2:
                hold(eng, b_sc, b * NSC + u, "act" if done is b_za else "dve")
            c = z % 4
            copy(KTS[:, u % 2, 2 * c:2 * c + 2, :].rearrange("p a w -> p (a w)"), src).then_inc(done, 1)
        elif z < 22:
            copy(PTS[:, 4 * (z - 20):4 * (z - 19), :].rearrange("p a w -> p (a w)"), src).then_inc(done, 1)
        else:
            copy(PTS[:, 8:10, :].rearrange("p a w -> p (a w)"), src[:, 0:2 * P])
            copy(PTS[0:DS, 10, :], src[0:DS, 2 * P:3 * P]).then_inc(done, 1)

    def s10_act(act):
        copy = lambda o, i: act.activation(o, i, ACT.Copy)
        act.wait_ge(b_qk, 1)
        copy(QTS[:, :, :].rearrange("p a w -> p (a w)"), PS[:, 3, :]).then_inc(b_qt, 1)
        with act.Fori(0, DB) as b:
            for z in range(0, 20, 2):
                s10_out(z, act, copy, b_za, b)
            hold(act, b_red, b + 1, "act")
            act.activation(SS[:, :], SS[:, :], ACT.Exp, bias=NMN[:, 0:1], scale=-1.0, accum_out=DNS[:, 0:1]).then_inc(b_p, 1)
            for z in (20, 22):
                s10_out(z, act, copy, b_za, b)
        act.wait_ge(b_oc, DB)
        o = OALL[:, :].rearrange("p (b d) -> p b d", b=DB)
        for e in range(2):
            copy(ODUP[:, :, e, :], o).then_inc(b_du, 1)
        act.wait_ge(b_dt, 1)
        for e in range(2):
            for b in range(0, DB, 4):
                copy(*smp_out(e, b, HHI)).then_inc(b_hh, 1)

    def smp_out(e, b, t):
        r = slice(e * DH, (e + 1) * DH)
        dst = t[r, :, S0 + b * DS:S0 + (b + 4) * DS].rearrange("p k (b q) -> p b k q", q=DS)
        src = PS[r, 3 + b // 4, :].rearrange("p (b k e q) -> p b k e q", b=4, e=2, q=DS)[:, :, :, e, :]
        return dst, src

    def s10_dve(dve):
        dve.wait_ge(b_qk, 2)
        dve.tensor_copy(KTN, PS[:, 4, :].rearrange("p (a w) -> p a w", w=NS)).then_inc(b_qt, 1)
        with dve.Fori(0, DB) as b:
            for z in range(1, 20, 2):
                s10_out(z, dve, dve.tensor_copy, b_zd, b)
            hold(dve, b_sc, b * NSC + NSC + 1, "dve")
            dve.tensor_tensor_reduce(SS[:, :], PS[:, 0:3, :].rearrange("p a w -> p (a w)")[:, 0:NPOS], BSS[:, :],
                                     -(DH ** -0.5), 3.0e38, ALU.add, ALU.min, NMN[:, 0:1]).then_inc(b_red, 1)
            s10_out(21, dve, dve.tensor_copy, b_zd, b)
            hold(dve, b_p, b + 1, "dve")
            dve.reciprocal(RDS[:, :], DNS[:, :]).then_inc(b_rd, 1)
            hold(dve, b_rd, b + 1, "dve")
            hold(dve, b_pv, b + 1, "dve")
            dve.scalar_tensor_tensor(O4[:, :, :], PS[:, 7, 0:256].rearrange("p (a d) -> p a d", a=4), RDS[:, 0:1],
                                     mask4[:, :].unsqueeze(2).to_broadcast([P, 4, DH]), ALU.mult, ALU.mult).then_inc(b_o4, 1)
            hold(dve, b_o4, b + 1, "dve")
            dve.tensor_reduce(OALL[:, bass.ds(b * DH, DH)], O4[:, :, :].rearrange("p a d -> p d a"), AX.X, ALU.add).then_inc(b_oc, 1)
        for i, (e, b) in enumerate(((0, 0), (0, 4), (1, 0), (1, 4))):
            dve.wait_ge(b_hh, i + 1)
            dst, src = smp_out(e, b, HLO)
            dve.tensor_tensor(dst, src, smp_out(e, b, HHI)[0].bitcast(F32), ALU.subtract)

    stage(s10_pe, s10_act, s10_dve, s10_pool)

    stage(*out_projection("out1", B_OUT1, parkx))
    stage(*ffn("ffn1", B_FFN1, G_FFN[1], 1))

    YT = at("y_tok", O_HH, [P, NT, D])
    y_in, y_a, y_v, y_st = sem("y_turned"), sem("y_out_act"), sem("y_out_dve"), sem("y_stored")

    def s13_pe(pe):
        for t in range(NT):
            if t >= 3:
                pe.wait_ge(y_a, t - 2)
                pe.wait_ge(y_v, t - 2)
            r = P if t < QT else NS
            c0 = t * P if t < QT else S0
            for k in range(KT):
                mm = pe.transpose(PS[0:r, 2 * (t % 3) + k // 4, (k % 4) * P:(k % 4 + 1) * P], X[:, k, c0:c0 + r], ident[:, :])
            mm.then_inc(y_in, 1)

    def y_half(t, half):
        r = P if t < QT else NS
        return YT[0:r, t, half * 512:(half + 1) * 512], PS[0:r, 2 * (t % 3) + half, :]

    def s13_act(act):
        for t in range(NT):
            act.wait_ge(y_in, t + 1)
            act.activation(*y_half(t, 0), ACT.Copy).then_inc(y_a, 1)

    def s13_dve(dve):
        for t in range(NT):
            dve.wait_ge(y_in, t + 1)
            dve.tensor_copy(*y_half(t, 1)).then_inc(y_v, 1)

    def s13_pool(pool):
        y = a["y_prompt"][0].rearrange("(t p) c -> p t c", p=P)
        for t in range(NT):
            pool.wait_ge(y_a, t + 1)
            pool.wait_ge(y_v, t + 1)
            if t < QT:
                pool.dma_start(y[:, t, :], YT[:, t, :]).then_inc(y_st, 16)
            else:
                pool.dma_start(a["y_sample"].rearrange("b s c -> (b s) c"), YT[0:NS, t, :]).then_inc(y_st, 16)
        pool.wait_ge(y_st, 16 * NT)

    stage(s13_pe, s13_act, s13_dve, s13_pool)
    def run(eng, name):
        for n in range(len(stages[name])):
            stages[name][n](eng)
            meet(eng, n + 1)

    with ctx:
        block = ctx.enter_context(nc.Block())

        @block.sync
        def _(sp):
            load_block(sp, 0, columns(a["w_in_rec"][0], 0), wait=False)
            with sp.Fori(1, N_IN0) as n:
                load_block(sp, n, columns(a["w_in_rec"][0], n))
            with sp.Fori(0, N_OUT) as j:
                load_block(sp, B_OUT0 + j, columns(a["w_out_rec"][0], j))
            ffn_load(sp, B_FFN0, 0)
            with sp.Fori(0, N_QKV) as j:
                load_block(sp, B_QKV + j, columns(a["w_in_att"][0], j))
            with sp.Fori(0, RING) as j:
                load_block(sp, B_OUT1 + j, columns(a["w_out_att"][0], j))
            cache_load(sp)
            load_block(sp, B_OUT1 + RING, columns(a["w_out_att"][0], RING))
            ffn_load(sp, B_FFN1, 1)

        @block.tensor
        def _(pe):
            run(pe, "pe")

        @block.scalar
        def _(act):
            run(act, "act")

        @block.vector
        def _(dve):
            run(dve, "dve")

        @block.gpsimd
        def _(pool):
            run(pool, "pool")


_OUTS = [((1, SEQ, D), "y_prompt"), ((DB, DS, D), "y_sample"), ((1, 1, RH, DK, DV), "ret_prompt"),
         ((1, 1, LW), "lru_prompt"), ((1, 1, CONV - 1, LW), "conv_prompt"), ((1, 1, SEQ, H, DH), "k_prompt"),
         ((1, 1, SEQ, H, DH), "v_prompt"), ((1, DB, RH, DK, DV), "ret_sample"), ((1, DB, LW), "lru_sample"),
         ((1, DB, CONV - 1, LW), "conv_sample"), ((1, DB, DS, H, DH), "k_sample"), ((1, DB, DS, H, DH), "v_sample")]
_INS = ["x_prompt", "x_sample", "state_ret", "state_lru", "state_conv", "cache_k", "cache_v", "norm_mix", "norm_ffn",
        "w_in_rec", "w_out_rec", "ret_norm_g", "conv_w", "conv_b", "w_rgate", "b_rgate", "w_igate", "b_igate",
        "lru_lambda", "w_in_att", "w_out_att", "q_norm_g", "k_norm_g", "w_ffn_gate", "w_ffn_up", "w_ffn_down"]


def kernel(**inputs):
    import concourse.bacc as bacc
    from concourse.bass_utils import run_bass_kernel_spmd

    nc = bacc.Bacc("TRN2", target_bir_lowering=False, num_devices=1)
    arrays, aps = {}, {}
    for name in _INS:
        arr = np.ascontiguousarray(inputs[name])
        arrays["in_" + name] = arr
        aps[name] = nc.dram_tensor("in_" + name, arr.shape, mybir.dt.from_np(arr.dtype), kind="ExternalInput").ap()
    for name, arr in constants().items():
        arrays["in_" + name] = arr
        aps[name] = nc.dram_tensor("in_" + name, arr.shape, F32, kind="ExternalInput").ap()
    for shape, name in _OUTS:
        aps[name] = nc.dram_tensor("out_" + name, shape, F32, kind="ExternalOutput").ap()
    build(nc, aps)
    r = run_bass_kernel_spmd(nc, [arrays], core_ids=[0])
    return tuple(r.results[0]["out_" + name] for _, name in _OUTS)
```

```python
from contextlib import ExitStack

import numpy as np

import concourse.bass as bass
from concourse import mybir

F32 = mybir.dt.float32
F32R = mybir.dt.float32r
ALU = mybir.AluOpType
ACT = mybir.ActivationFunctionType
AX = mybir.AxisListType

P = 128
D = 1024
KT = D // P
SEQ = 1024
QT = SEQ // P
DB, DS = 8, 8
NS = DB * DS
PAST = 2048
F = 2816
EPS = 1e-6
RH, DK, DV = 4, 64, 128
LW = 512
CONV = 4
LRU_C = 8.0
H, DH = 16, 64
HP = H // 2
CW = 364
NCH = 3
TW = CW * NCH
S0 = TW - NS
NT = QT + 1
BW = 256
BE = KT * BW
RING = 3
NG = F // BW
REC_IN = 2560
N_IN0, N_OUT, N_FFN, N_QKV = REC_IN // BW, D // BW, 3 * NG, 3 * D // BW
B_IN0 = 0
B_OUT0 = B_IN0 + N_IN0
B_FFN0 = B_OUT0 + N_OUT
B_QKV = B_FFN0 + N_FFN
B_OUT1 = B_QKV + N_QKV
B_FFN1 = B_OUT1 + N_OUT
NBLK = B_FFN1 + N_FFN
MASKED = -1.0e30
RS_CHUNK = 128


def win(t):
    return t * P if t < QT else TW - P


def constants():
    gamma = 1.0 - 2.0 ** (-5.0 - np.arange(RH))
    i = np.arange(P)
    c = {}
    c["c_ident"] = np.eye(P, dtype=np.float32)
    diff = i[None, :] - i[:, None]
    scale = DK ** -0.5
    dec = np.where(diff >= 0, gamma[:, None, None] ** np.maximum(diff, 0), 0.0) * scale
    c["c_dec"] = np.ascontiguousarray(dec.transpose(1, 0, 2)).astype(np.float32)
    j = np.arange(NS)
    sd = (j % DS)[None, :] - (j % DS)[:, None]
    same = (j // DS)[None, :] == (j // DS)[:, None]
    decs = np.where(same & (sd >= 0), gamma[:, None, None] ** np.maximum(sd, 0), 0.0) * scale
    c["c_decs"] = np.ascontiguousarray(decs.transpose(1, 0, 2)).astype(np.float32)
    qd = np.zeros((P, 2, P + NS))
    for h in range(RH):
        rows = slice(DK * (h % 2), DK * (h % 2) + DK)
        qd[rows, h // 2, :P] = gamma[h] ** (i + 1.0)
        qd[rows, h // 2, P:] = gamma[h] ** (j % DS + 1.0)
    c["c_qd"] = qd.astype(np.float32)
    kd = np.zeros((P, RH + RH * DB))
    for h in range(RH):
        kd[:, h] = gamma[h] ** (P - 1.0 - i) * scale
        for b in range(DB):
            r = slice(b * DS, b * DS + DS)
            kd[r, RH + h * DB + b] = gamma[h] ** (DS - 1.0 - np.arange(DS)) * scale
    c["c_kd"] = kd.astype(np.float32)
    slope = 2.0 ** (-8.0 * np.arange(1, H + 1) / H)

    def bias(delta, sl):
        n = ((delta >= 0) & (delta <= 128)).astype(np.float64)
        n += (delta >= 0) & (delta <= 512) & (delta % 4 == 0)
        n += (delta >= 0) & (delta <= 2048) & (delta % 16 == 0)
        return np.where(n > 0, (np.log(np.maximum(n, 1)) - sl * delta) * DH ** 0.5, MASKED)

    x = np.arange(SEQ)
    c["c_bp"] = bias((SEQ - P) + i[None, :, None] - x[None, None, :], slope[:, None, None]).astype(np.float32)
    pos = sample_positions()
    hq_s = np.tile(np.arange(DS), H)
    hq_h = np.repeat(np.arange(H), DS)
    c["c_bs"] = bias(PAST + hq_s[:, None] - pos[None, :], slope[hq_h][:, None]).astype(np.float32)
    m = np.zeros((P, 4))
    m[i, (i // DS) % 4] = 1.0
    c["c_mask"] = m.astype(np.float32)
    return c


def sample_positions():
    a = np.arange(P)
    pos = [16 * a + r for r in range(8)]
    p = np.arange(P)
    for e in range(2):
        pos.append(1536 + 16 * (p % 32) + 8 + 2 * (p // 32) + e)
    pos.append(PAST + np.arange(DS))
    return np.concatenate(pos)


CONSTS = {k: v.shape for k, v in constants().items()}


def build(nc, a):
    ctx = ExitStack()
    base = (nc.sbuf_base + 31) // 32 * 32
    base = max(base, 16512)

    def at(name, off, shape, dt=F32):
        return nc.alloc_sbuf_tensor_at(name, shape, dt, offset=base + off)

    def sem(name):
        return ctx.enter_context(nc.semaphore(name))

    TB = TW * 4
    TA = (TB + 31) // 32 * 32
    O_X, O_HH, O_HL = 0, KT * TB, 2 * KT * TB
    O_WH = 3 * KT * TB
    O_WL = O_WH + RING * BE * 4
    O_RAW = O_WL + RING * BE * 4
    O_C = O_RAW + BE * 4
    O_WORK = O_C + 2080
    X = at("x_res", O_X, [P, KT, TW])
    HHI = at("h_hi", O_HH, [P, KT, TW], F32R)
    HLO = at("h_lo", O_HL, [P, KT, TW], F32R)
    WHI = at("w_hi", O_WH, [P, RING, BE], F32R)
    WLO = at("w_lo", O_WL, [P, RING, BE], F32R)
    RAW = at("w_raw", O_RAW, [P, BE])
    ident = at("ident", O_C, [P, P])
    ones = at("ones", O_C + 512, [P, P])
    vecr = at("vec_rows", O_WORK, [P, P])
    NV = 68
    vec = at("vec_cols", O_C + 1056, [P, NV])
    rtok = at("rtok", O_C + 1344, [P, NT, 2])
    gqk = at("gqk", O_C + 1440, [P, 2, DH])
    mask4 = at("mask4", O_C + 2016, [P, 4])
    XN = at("x_natural", O_HH, [P, NT, D])
    G_MIX, G_FFN = (0, 8), (16, 24)
    V_CW, V_CB, V_BR, V_BI, V_LAM, V_RG = 32, 48, 52, 56, 60, 64

    PS = ctx.enter_context(nc.psum_tensor("psum", [P, 8, 512], F32))

    def dram(name, shape):
        return nc.dram_tensor(name, shape, F32, kind="Internal").ap()

    proj = dram("proj_t", [16, P, TW])
    vtok = dram("v_tok", [NT * P, LW])
    parkx = dram("park_x", [P, KT * TW])
    qtok = dram("q_tok", [NT * P, D])

    met = sem("stages_met")
    tick = {e: sem(f"tick_{e}") for e in ("pe", "act", "dve", "pool", "sp")}
    raw_in, wh_done, wl_done, pe_done = sem("raw_in"), sem("wh_done"), sem("wl_done"), sem("pe_done")

    def hold(eng, s, value, who):
        eng.wait_ge(s, value)
        if not isinstance(value, int):
            eng.sem_inc(tick[who], 1)

    def meet(eng, n):
        eng.drain().then_inc(met, 1)
        eng.wait_ge(met, 4 * n)

    def load_block(sp, n, src, wait=True):
        if wait:
            hold(sp, wl_done, n, "sp")
        sp.dma_start(RAW[:, :].rearrange("p (k c) -> p k c", k=src.shape[1]), src).then_inc(raw_in, 16)

    def columns(w, j):
        return w.rearrange("(k p) c -> p k c", p=P)[:, :, bass.ds(j * BW, BW)]

    def rows(w, g):
        return w[bass.ds(g * BW, BW), :].rearrange("(f p) c -> p f c", p=P)

    def split_hi(act, n, slot, first=False):
        if not first:
            hold(act, pe_done, n - RING + 1, "act")
        hold(act, raw_in, n * 16 + 16, "act")
        act.activation(WHI[:, slot, :], RAW[:, :], ACT.Copy).then_inc(wh_done, 1)

    def split_lo(dve, n, slot):
        hold(dve, wh_done, n + 1, "dve")
        dve.tensor_tensor(WLO[:, slot, :], RAW[:, :], WHI[:, slot, :].bitcast(F32),
                          ALU.subtract).then_inc(wl_done, 1)

    def fm_tile(pe, bank, slot, kcols, before, hi, lo, done):
        nk = len(kcols)
        i = 0
        for k, wc in enumerate(kcols):
            if before is not None:
                before(k)
            for st, mv in ((WHI, hi), (WHI, lo), (WLO, hi)):
                for c in range(NCH):
                    mm = pe.matmul(PS[:, bank + c, 0:CW], st[:, slot, wc:wc + P],
                                   mv[:, k, c * CW:(c + 1) * CW],
                                   start=(i < NCH), stop=(i >= 3 * NCH * nk - NCH))
                    i += 1
        mm.then_inc(done, 1)
        return mm

    def col_tiles(m):
        return [k * BW + m * P for k in range(KT)]

    ld, vt_done, xt_in, xt_v, xt_a, cst = (sem(x) for x in
                                           ("loaded", "vec_turned", "x_turned", "x_out_dve", "x_out_act", "consts"))

    def s1_pool(pool):
        r = 0
        for name, n in (("norm_mix", 16), ("norm_ffn", 16), ("conv_w", 16), ("conv_b", 4), ("b_rgate", 4),
                        ("b_igate", 4), ("lru_lambda", 4)):
            src = a[name]
            src = (src[0] if name == "conv_w" else src).rearrange("a (k p) -> (a k) p", p=P)
            pool.dma_start(vecr[r:r + n, :], src).then_inc(ld, 16)
            r += n
        pool.dma_start(vecr[r:r + RH, :], a["ret_norm_g"][0]).then_inc(ld, 16)
        for i, name in enumerate(("q_norm_g", "k_norm_g")):
            pool.dma_start(gqk[:, i, :], a[name].to_broadcast([P, DH])).then_inc(ld, 16)
        pool.dma_start(mask4[:, :], a["c_mask"]).then_inc(ld, 16)
        pool.memset(ones[:, :], 1.0).then_inc(cst, 1)
        pool.memset(X[:, :, SEQ:S0], 0.0).then_inc(cst, 1)

    N_LD = 11
    x_in = [sem(f"x_in{i}") for i in range(5)]

    def s1_pe(pe):
        for t in range(NT):
            pe.wait_ge(x_in[t // 2], 16 if t >= 2 else 32)
            if t >= 3:
                pe.wait_ge((xt_v, xt_a)[(t - 3) % 2], (t - 3) // 2 + 1)
            r0 = 0 if t < QT else P - NS
            for k in range(KT):
                mm = pe.transpose(PS[:, 2 * (t % 3) + k // 4, (k % 4) * P:(k % 4) * P + P - r0],
                                  XN[r0:P, t, k * P:(k + 1) * P], ident[r0:P, r0:P])
            mm.then_inc(xt_in, 1)
        pe.wait_ge(ld, 16 * N_LD)
        pe.transpose(PS[:, 7, 0:NV], vecr[0:NV, :], ident[0:NV, 0:NV]).then_inc(vt_done, 1)

    def x_tile(t):
        r0 = 0 if t < QT else P - NS
        c0 = t * P if t < QT else S0
        src = PS[:, 2 * (t % 3):2 * (t % 3) + 2, :].rearrange("p a (k c) -> p (a k) c", c=P)
        return X[:, :, c0:c0 + P - r0], src[:, :, 0:P - r0]

    def s1_act(act):
        act.dma_start(ident[:, :], a["c_ident"]).then_inc(x_in[0], 16)
        x = a["x_prompt"][0].rearrange("(t p) c -> p t c", p=P)
        for t in range(0, QT, 2):
            act.dma_start(XN[:, t:t + 2, :], x[:, t:t + 2, :]).then_inc(x_in[t // 2], 16)
        act.dma_start(XN[P - NS:P, QT, :], a["x_sample"].rearrange("b s c -> (b s) c")).then_inc(x_in[QT // 2], 16)
        for t in range(1, NT, 2):
            act.wait_ge(xt_in, t + 1)
            o, i = x_tile(t)
            act.activation(o, i, ACT.Copy).then_inc(xt_a, 1)
        split_hi(act, 0, 0, first=True)

    def s1_dve(dve):
        for t in range(0, NT, 2):
            dve.wait_ge(xt_in, t + 1)
            o, i = x_tile(t)
            dve.tensor_copy(o, i).then_inc(xt_v, 1)
        dve.wait_ge(vt_done, 1)
        dve.tensor_copy(vec[:, :], PS[:, 7, 0:NV])
        split_lo(dve, 0, 0)

    R = at("rstd", O_WORK, [P, TW])
    RM, RU, RN = (at("rms_" + x, O_WORK + TA + 96 * n, [P, NT, 2]) for n, x in enumerate(("mean", "inverse", "newton")))
    DIA = at("rms_diag", O_WORK + 2 * TA, [P, NT, P])
    NSQ = 7
    SQ = [at(f"prep_sq{n}", O_WORK + (4 + n) * TA, [P, TW]) for n in range(NSQ)]

    PREP = {"sq_in": KT, "sq_sum": KT - 1, "sums": 1, "hh_in": KT, "hl_in": KT, "rchain": 6, "rroot": 1,
            "diag": 1, "spread": 3, "spread_out": 3}
    prep_sem = {k: sem(k) for k in PREP}
    SPREAD = ((6, 0, 4), (7, 4, 4), (6, 8, 1))

    def prep_wait(eng, use, k, value):
        if k in ("diag", "spread", "spread_out"):
            use -= use > 2
        eng.wait_ge(prep_sem[k], use * PREP[k] + value)

    def prep_act(act, q, g, fm=True):
        for k in range(KT):
            act.activation(HHI[:, k, :], X[:, k, :], ACT.Copy, scale=vec[:, g + k:g + k + 1]).then_inc(prep_sem["hh_in"], 1)
        for k in range(KT):
            if k == NSQ:
                prep_wait(act, q, "sq_sum", 1)
            act.activation(SQ[k if k < NSQ else 1][:, :], X[:, k, :], ACT.Square).then_inc(prep_sem["sq_in"], 1)
        prep_wait(act, q, "rchain", 2)
        act.activation(rtok[:, :, :], RU[:, :, :], ACT.Sqrt).then_inc(prep_sem["rroot"], 1)
        if fm:
            for i, (bank, t, n) in enumerate(SPREAD):
                prep_wait(act, q, "spread", i + 1)
                w = min(n * P, TW - t * P)
                act.activation(R[:, t * P:t * P + w], PS[:, bank, 0:w], ACT.Copy).then_inc(prep_sem["spread_out"], 1)

    def prep_dve(dve, q, g, fm=True):
        for k in range(KT):
            prep_wait(dve, q, "hh_in", k + 1)
            dve.scalar_tensor_tensor(HLO[:, k, :], X[:, k, :], vec[:, g + k:g + k + 1],
                                     HHI[:, k, :].bitcast(F32), ALU.mult, ALU.subtract).then_inc(prep_sem["hl_in"], 1)
        for k in range(1, KT):
            prep_wait(dve, q, "sq_in", k + 1)
            if k > 1:
                prep_wait(dve, q, "sq_sum", k - 1)
            dve.tensor_tensor(SQ[0][:, :], SQ[0][:, :], SQ[k if k < NSQ else 1][:, :], ALU.add).then_inc(prep_sem["sq_sum"], 1)
        c = prep_sem["rchain"]
        prep_wait(dve, q, "sums", 1)
        dve.tensor_scalar(RM[:, :, :], PS[:, 7, 0:2 * NT].rearrange("p (t e) -> p t e", e=2), 1.0 / D, EPS,
                          ALU.mult, ALU.add).then_inc(c, 1)
        prep_wait(dve, q, "rchain", 1)
        dve.reciprocal(RU[:, :, :], RM[:, :, :]).then_inc(c, 1)
        prep_wait(dve, q, "rroot", 1)
        dve.tensor_tensor(RN[:, :, :], rtok[:, :, :], rtok[:, :, :], ALU.mult).then_inc(c, 1)
        prep_wait(dve, q, "rchain", 3)
        dve.tensor_tensor(RN[:, :, :], RN[:, :, :], RM[:, :, :], ALU.mult).then_inc(c, 1)
        prep_wait(dve, q, "rchain", 4)
        dve.tensor_scalar(RN[:, :, :], RN[:, :, :], -0.5, 1.5, ALU.mult, ALU.add).then_inc(c, 1)
        prep_wait(dve, q, "rchain", 5)
        dve.tensor_tensor(rtok[:, :, :], rtok[:, :, :], RN[:, :, :], ALU.mult).then_inc(c, 1)
        prep_wait(dve, q, "rchain", 6)
        if fm:
            dve.tensor_tensor(DIA[:, :, :], ident[:, :].unsqueeze(1).to_broadcast([P, NT, P]),
                              rtok[:, :, 0:1].to_broadcast([P, NT, P]), ALU.mult).then_inc(prep_sem["diag"], 1)
            prep_wait(dve, q, "spread_out", 3)

    def prep_sums(pe, q):
        prep_wait(pe, q, "sq_sum", KT - 1)
        for t in range(NT):
            mm = pe.matmul(PS[:, 7, 2 * t:2 * t + 2], SQ[0][:, win(t):win(t) + P], ones[:, 0:2],
                           start=True, stop=True)
        mm.then_inc(prep_sem["sums"], 1)

    def prep_spread(pe, q, parts):
        prep_wait(pe, q, "diag", 1)
        for bank, t0, m in parts:
            if t0 == KT:
                prep_wait(pe, q, "spread_out", 1)
            for t in range(t0, t0 + m):
                r0 = t * P - win(t)
                mm = pe.matmul(PS[:, bank, (t - t0) * P:(t - t0 + 1) * P - r0], ones[:, :], DIA[:, t, r0:P],
                               start=True, stop=True)
            mm.then_inc(prep_sem["spread"], 1)

    def prep_tile(pe, q, n):
        def first(k):
            prep_wait(pe, q, "hl_in", k + 1)

        def second(k):
            if k == 4:
                prep_sums(pe, q)
            if k == KT - 1:
                prep_spread(pe, q, SPREAD[:2])

        return (first, second)[n]

    q2 = 0
    fm_in, fm_out, tm_in, tm_out = (sem(x + "_in0") for x in
                                                   ("fm_in", "fm_out", "tm_in", "tm_out"))
    stg_out = [sem(f"stg_out{i}_in0") for i in range(2)]
    vst_out = [sem(f"vst_out{i}_in0") for i in range(2)]
    xpark = sem("x_parked_0")
    STG = at("in0_stage", O_WORK + 6 * TA, [P, 2, TW])
    VST = at("in0_vstage", O_WORK + 8 * TA, [P, 2, BW])

    def tm_unit(pe, bank, slot, t, done):
        w = win(t)
        i = 0
        for k in range(KT):
            for st, mv in ((HHI, WHI), (HHI, WLO), (HLO, WHI)):
                mm = pe.matmul(PS[:, bank, 0:BW], st[:, k, w:w + P], mv[:, slot, k * BW:(k + 1) * BW],
                               start=(i == 0), stop=(i == 3 * KT - 1))
                i += 1
        mm.then_inc(done, 1)
        return mm

    def s2_pe(pe):
        def block(idx, n, slot, first):
            hold(pe, wl_done, n + 1, "pe")
            for m in range(2):
                if not first:
                    hold(pe, fm_out, idx + m - 1, "pe")
                mm = fm_tile(pe, 3 * m, slot, col_tiles(m), prep_tile(pe, q2, m) if first else None, HHI, HLO, fm_in)
                if first and m:
                    prep_spread(pe, q2, SPREAD[2:])
            return mm

        def finished(pe):
            pe.drain().then_inc(pe_done, 1)

        block(0, 0, 0, True); finished(pe)
        block(2, 1, 1, False); finished(pe)
        prep_wait(pe, q2, "spread_out", 3)
        u = 0
        for j in (2, 3):
            pe.wait_ge(wl_done, j + 1)
            for t in range(NT):
                if u >= 2:
                    pe.wait_ge(tm_out, u - 1)
                tm_unit(pe, 6 + u % 2, j % RING, t, tm_in)
                u += 1
            finished(pe)
        with pe.Fori(0, 2) as i:
            for jj in range(3):
                block(4 + i * 6 + 2 * jj, 4 + i * 3 + jj, (4 + jj) % RING, False)
                finished(pe)

    def s2_act(act):
        prep_act(act, q2, G_MIX[0])
        split_hi(act, 1, 1, first=True)
        split_hi(act, 2, 2, first=True)
        split_hi(act, 3, 0)
        split_hi(act, 4, 1)
        u = 0
        for j in (2, 3):
            for t in range(NT):
                act.wait_ge(tm_in, u + 1)
                if u == 0:
                    prep_wait(act, q2, "rchain", 6)
                if u >= 2:
                    act.wait_ge(vst_out[u % 2], 16 * (u // 2))
                act.activation(VST[:, u % 2, :], PS[:, 6 + u % 2, 0:BW], ACT.Copy,
                               scale=rtok[:, t, 0:1]).then_inc(tm_out, 1)
                u += 1
            split_hi(act, j + 3, (j + 3) % RING)
        with act.Fori(0, 2) as i:
            for jj in range(3):
                split_hi(act, 7 + i * 3 + jj, (7 + jj) % RING)

    def s2_dve(dve):
        prep_dve(dve, q2, G_MIX[0])
        split_lo(dve, 1, 1)

        def evac(use, half, free):
            hold(dve, fm_in, use * 2 + half + 1, "dve")
            if free:
                hold(dve, stg_out[half], use * 16, "dve")
            dve.tensor_tensor(STG[:, half, :].rearrange("p (c w) -> p c w", c=NCH), PS[:, 3 * half:3 * half + 3, 0:CW],
                              R[:, :].rearrange("p (c w) -> p c w", c=NCH), ALU.mult).then_inc(fm_out, 1)

        evac(0, 0, False)
        evac(0, 1, False)
        split_lo(dve, 2, 2)
        split_lo(dve, 3, 0)
        evac(1, 0, True)
        evac(1, 1, True)
        for n in (4, 5, 6):
            split_lo(dve, n, n % RING)
        with dve.Fori(0, 2) as i:
            for jj in range(3):
                for m in range(2):
                    evac(2 + i * 3 + jj, m, True)
                split_lo(dve, 7 + i * 3 + jj, (7 + jj) % RING)

    def s2_pool(pool):
        pool.dma_start(parkx, X[:, :, :].rearrange("p k w -> p (k w)")).then_inc(xpark, 16)

        def out(idx, half):
            hold(pool, fm_out, idx + 1, "pool")
            pool.dma_start(proj[bass.ds(idx, 1), :, :].rearrange("a p w -> p (a w)"), STG[:, half, :]).then_inc(stg_out[half], 16)

        for i in range(4):
            out(i, i % 2)
        u = 0
        for j in (2, 3):
            for t in range(NT):
                pool.wait_ge(tm_out, u + 1)
                pool.dma_start(vtok[t * P:(t + 1) * P, (j - 2) * BW:(j - 1) * BW], VST[:, u % 2, :]).then_inc(vst_out[u % 2], 16)
                u += 1
        prep_wait(pool, q2, "spread_out", 3)
        s3_tables(pool)
        with pool.Fori(0, 6) as i:
            for half in range(2):
                out(4 + i * 2 + half, half)
        for half in range(2):
            pool.wait_ge(stg_out[half], 16 * 8)
            pool.wait_ge(vst_out[half], 16 * NT)
        pool.wait_ge(xpark, 16)

    stages = {e: [] for e in ("pe", "act", "dve", "pool")}

    def stage(pe, act, dve, pool):
        for e, f in zip(("pe", "act", "dve", "pool"), (pe, act, dve, pool)):
            stages[e].append(f)

    stage(s1_pe, s1_act, s1_dve, s1_pool)
    stage(s2_pe, s2_act, s2_dve, s2_pool)

    gam = [1.0 - 2.0 ** (-5.0 - h) for h in range(RH)]
    OTP = at("ret_o", O_X + 4 * TB, [P, RH, TW])
    VS = at("ret_vs", O_X, [P, RH * DV])
    KM = at("ret_km", O_X + 2048, [NS, DB, RH, DK])
    ATTS = at("ret_atts", O_X + 10240, [P, 2, 2, NS])
    KTS = at("ret_kts", O_X + 11264, [NS, RH, DK])
    QKS = at("ret_qks", O_X + 12288, [P, 2, 2, NS])
    QDS = at("ret_qds", O_X + 13312, [P, 2, NS])
    w = O_WORK
    S0S = at("ret_s0", w, [P, DB, 2, DV])
    DEC = at("ret_dec", w + 8192, [P, RH, P])
    DECS = at("ret_decs", w + 10240, [NS, RH, NS])
    QD = at("ret_qd", w + 11264, [P, 2, P + NS])
    KD = at("ret_kd", w + 12800, [P, RH + RH * DB])
    ST = at("ret_state", w + 12960, [P, 2, DV])
    QC = at("ret_q", w + 13984, [P, 2, 2, P])
    KC = at("ret_k", w + 16032, [P, 2, 2, P])
    VC = at("ret_v", w + 18080, [P, 2, RH * DV])
    ATT = at("ret_att", w + 22176, [P, 2, 2, P])
    KTOK = at("ret_ktok", w + 24224, [P, RH, DK])
    QDT = at("ret_qdt", w + 25248, [P, 2, P])
    NCHK = SEQ // P
    (r_cst, r_tab, r_kt, r_att, r_o, r_s, r_ktok, r_attr, r_qd, r_str, r_oo, r_so, r_sld, r_sstep) = (
        sem("ret_" + x) for x in ("cst", "tables", "kt_in", "att_in", "o_in", "s_in", "ktok_rdy", "att_rdy", "qd_rdy",
                                  "state_rdy", "o_out", "stored", "sample_in", "sample_steps"))
    r_ss = sem("ret_sample_stored")
    c_gt = sem("gate_in")
    r_ld = [sem(f"ret_chunk_in{i}") for i in range(2)]
    projc = proj.rearrange("m p w -> p m w")

    def par(h):
        return slice(DK * (h % 2), DK * (h % 2) + DK)

    def s3_tables(pool):
        for t, c in ((DEC, "c_dec"), (DECS, "c_decs"), (QD, "c_qd")):
            pool.dma_start(t[:, :, :], a[c]).then_inc(r_tab, 16)
        pool.dma_start(KD[:, :], a["c_kd"]).then_inc(r_tab, 16)

    def s3_pool(pool):
        pool.memset(OTP[:, :, SEQ:S0], 0.0).then_inc(r_cst, 1)
        pool.memset(ST[:, :, :], 0.0).then_inc(r_cst, 1)
        pool.memset(VS[:, :], 0.0).then_inc(r_cst, 1)
        pool.memset(ATTS[:, :, :, :], 0.0).then_inc(r_cst, 1)

        def load(c, slot):
            pool.dma_start(QC[:, slot, :, :], projc[:, 0:2, bass.ds(c * P, P)]).then_inc(r_ld[slot], 16)
            pool.dma_start(KC[:, slot, :, :], projc[:, 2:4, bass.ds(c * P, P)]).then_inc(r_ld[slot], 16)
            pool.dma_start(VC[:, slot, :], vtok[bass.ds(c * P, P), :]).then_inc(r_ld[slot], 16)

        for slot in range(2):
            load(slot, slot)
        pool.dma_start(T2[:, :, :], proj[4:8].rearrange("m p w -> p m w")).then_inc(c_gt, 16)
        with pool.Fori(0, NCHK // 2 - 1) as i:
            for slot in range(2):
                hold(pool, r_s, 2 * i + slot + 1, "pool")
                load(2 * i + 2 + slot, slot)
        pool.wait_ge(r_cst, 3)
        pool.dma_start(VS[0:NS, :], vtok[(NT - 1) * P + P - NS:NT * P, :]).then_inc(r_sld, 16)
        for i in range(2):
            pool.dma_start(QKS[:, i, :, :], projc[:, 2 * i:2 * i + 2, S0:TW]).then_inc(r_sld, 16)
        s0 = a["state_ret"][0].rearrange("b (g e) k v -> g e k b v", e=2)
        for g in range(2):
            for e in range(2):
                pool.dma_start(S0S[e * DK:(e + 1) * DK, :, g, :], s0[g, e]).then_inc(r_sld, 16)
        pool.wait_ge(r_str, NCHK + 1)
        sp = a["ret_prompt"][0, 0].rearrange("(g e) k v -> e k g v", e=2)
        for e in range(2):
            pool.dma_start(sp[e], ST[e * DK:(e + 1) * DK, :, :]).then_inc(r_so, 16)

    def s3_pe(pe):
        pe.wait_ge(r_cst, 4)
        pe.wait_ge(r_tab, 64)

        def chunk(i, s):
            c = 2 * i + s
            hold(pe, r_ld[s], i * 48 + 48, "pe")
            hold(pe, r_ktok, c + 1, "pe")
            for g in range(2):
                mm = pe.transpose(PS[:, 0, g * P:(g + 1) * P], KC[:, s, g, :], ident[:, :])
            mm.then_inc(r_kt, 1)
            hold(pe, r_attr, c + 1, "pe")
            for h in range(RH):
                mm = pe.matmul(PS[:, 1 + h % 2, (h // 2) * P:(h // 2 + 1) * P], KC[par(h), s, h // 2, :],
                               QC[par(h), s, h // 2, :], start=True, stop=True)
                if h >= 2:
                    mm.then_inc(r_att, 1)
            hold(pe, r_attr, c + 2, "pe")
            hold(pe, r_qd, c + 1, "pe")
            hold(pe, r_str, c + 1, "pe")
            hold(pe, r_oo, c + 1, "pe")
            for h in range(RH):
                o = PS[:, 3 + h % 2, (h // 2) * P:(h // 2 + 1) * P]
                pe.matmul(o, VC[:, s, h * DV:(h + 1) * DV], ATT[:, h % 2, h // 2, :], start=True, stop=False)
                mm = pe.matmul(o, ST[par(h), h // 2, :], QDT[par(h), h // 2, :], start=False, stop=True)
                if h >= 2:
                    mm.then_inc(r_o, 1)
            hold(pe, r_ktok, c + 2, "pe")
            for h in range(RH):
                mm = pe.matmul(PS[par(h), 5, (h // 2) * DV:(h // 2 + 1) * DV], KTOK[:, h, :],
                               VC[:, s, h * DV:(h + 1) * DV], start=True, stop=True)
            mm.then_inc(r_s, 1)

        with pe.Fori(0, NCHK // 2) as i:
            for s in range(2):
                chunk(i, s)
        pe.wait_ge(r_sld, 16 * 7)
        pe.wait_ge(r_ktok, NCHK + 1)
        for g in range(2):
            mm = pe.transpose(PS[0:NS, 0, g * P:(g + 1) * P], QKS[:, 1, g, :], ident[:, :])
        mm.then_inc(r_sstep, 1)
        for h in range(RH):
            mm = pe.matmul(PS[0:NS, 1 + h % 2, (h // 2) * NS:(h // 2 + 1) * NS], QKS[par(h), 1, h // 2, :],
                           QKS[par(h), 0, h // 2, :], start=True, stop=True)
            if h >= 2:
                mm.then_inc(r_sstep, 1)
        pe.wait_ge(r_sstep, 6)
        pe.wait_ge(r_oo, NCHK + 1)
        for h in range(RH):
            c0 = (h // 2) * NS
            pe.matmul(PS[:, 3 + h % 2, c0:c0 + NS], VS[:, h * DV:(h + 1) * DV], ATTS[:, h % 2, h // 2, :],
                      start=True, stop=False, skip_group_check=True)
            for b in range(DB):
                mm = pe.matmul(PS[:, 3 + h % 2, c0 + b * DS:c0 + (b + 1) * DS], S0S[par(h), b, h // 2, :],
                               QDS[par(h), h // 2, b * DS:(b + 1) * DS], start=False, stop=(b == DB - 1),
                               skip_group_check=True)
            if h >= 2:
                mm.then_inc(r_o, 1)
        pe.wait_ge(r_sstep, 7)
        for b in range(DB):
            for h in range(RH):
                c0 = ((b % 2) * 2 + h // 2) * DV
                mm = pe.matmul(PS[par(h), (0, 1, 2, 5)[b // 2], c0:c0 + DV], KM[:, b, h, :],
                               VS[0:NS, h * DV:(h + 1) * DV], start=True, stop=True)
        mm.then_inc(r_sstep, 1)

    def s3_act(act):
        act.sem_inc(r_ktok, 1)
        act.sem_inc(r_oo, 1)
        act.wait_ge(r_tab, 64)
        act.wait_ge(r_cst, 1)

        def chunk(c):
            hold(act, r_kt, c + 1, "act")
            for h in range(RH):
                i = act.activation(KTOK[:, h, :], PS[:, 0, h * DK:(h + 1) * DK], ACT.Copy, scale=KD[:, h:h + 1])
            i.then_inc(r_ktok, 1)
            hold(act, r_o, 2 * c + 2, "act")
            for e in range(2):
                out = OTP[:, :, bass.ds(c * P, P)].rearrange("p (g e) w -> p e g w", e=2)[:, e]
                i = act.activation(out, PS[:, 3 + e, 0:2 * P].rearrange("p (g w) -> p g w", g=2), ACT.Copy)
            i.then_inc(r_oo, 1)

        with act.Fori(0, NCHK) as c:
            chunk(c)
        act.wait_ge(r_o, 2 * NCHK + 2)
        for e in range(2):
            out = OTP[:, :, S0:TW].rearrange("p (g e) w -> p e g w", e=2)[:, e]
            act.activation(out, PS[:, 3 + e, 0:2 * NS].rearrange("p (g w) -> p g w", g=2), ACT.Copy)
        so = a["ret_sample"][0].rearrange("b (g e) k v -> g e k b v", e=2)
        act.wait_ge(r_sstep, 10)
        for g in range(2):
            for e in range(2):
                act.dma_start(so[g, e], S0S[e * DK:(e + 1) * DK, :, g, :]).then_inc(r_ss, 16)

    def s3_dve(dve):
        dve.wait_ge(r_cst, 2)
        dve.sem_inc(r_attr, 1)
        dve.sem_inc(r_str, 1)
        dve.wait_ge(r_tab, 64)
        dec = DEC[:, :, :].rearrange("p (g e) w -> p e g w", e=2)
        with dve.Fori(0, NCHK // 2) as i:
            for s in range(2):
                c = 2 * i + s
                hold(dve, r_att, 2 * c + 2, "dve")
                for e in range(2):
                    x = dve.tensor_tensor(ATT[:, e, :, :], PS[:, 1 + e, 0:2 * P].rearrange("p (g w) -> p g w", g=2),
                                          dec[:, e], ALU.mult)
                x.then_inc(r_attr, 1)
                dve.tensor_tensor(QDT[:, :, :], QC[:, s, :, :], QD[:, :, 0:P], ALU.mult).then_inc(r_qd, 1)
                hold(dve, r_s, c + 1, "dve")
                hold(dve, r_str, c + 1, "dve")
                for h in range(RH):
                    x = dve.scalar_tensor_tensor(ST[par(h), h // 2, :], ST[par(h), h // 2, :], gam[h] ** RS_CHUNK,
                                                 PS[par(h), 5, (h // 2) * DV:(h // 2 + 1) * DV], ALU.mult, ALU.add)
                x.then_inc(r_str, 1)
        dve.wait_ge(r_cst, 4)
        dve.wait_ge(r_sstep, 3)
        dve.tensor_tensor(QDS[:, :, :], QKS[:, 0, :, :], QD[:, :, P:P + NS], ALU.mult).then_inc(r_sstep, 1)
        decs = DECS[:, :, :].rearrange("p (g e) w -> p e g w", e=2)
        for e in range(2):
            dve.tensor_tensor(ATTS[0:NS, e, :, :], PS[0:NS, 1 + e, 0:2 * NS].rearrange("p (g w) -> p g w", g=2),
                              decs[:, e], ALU.mult).then_inc(r_sstep, 1)
        kdm = KD[0:NS, RH:RH + RH * DB].rearrange("p (h b) -> p b h", b=DB)
        for b in range(DB):
            x = dve.tensor_tensor(KM[:, b, :, :], PS[0:NS, 0, 0:RH * DK].rearrange("p (h k) -> p h k", h=RH),
                                  kdm[:, b, :].unsqueeze(2).to_broadcast([NS, RH, DK]), ALU.mult)
        x.then_inc(r_sstep, 1)
        dve.wait_ge(r_sstep, 8)
        for h in range(RH):
            for q, bank in enumerate((0, 1, 2, 5)):
                st = S0S[par(h), 2 * q:2 * q + 2, h // 2, :]
                src = PS[par(h), bank, :].rearrange("p (b g v) -> p b g v", b=2, g=2)[:, :, h // 2, :]
                x = dve.scalar_tensor_tensor(st, st, gam[h] ** DS, src, ALU.mult, ALU.add)
            if h >= 2:
                x.then_inc(r_sstep, 1)

    stage(s3_pe, s3_act, s3_dve, s3_pool)

    T1 = at("cmb_squares", O_HH + 4 * TB, [P, RH, TW])
    T2 = at("cmb_gate", O_HL + 4 * TB, [P, RH, TW])
    T3 = at("cmb_tanh", O_HH, [P, RH, TW])
    w = O_WORK + 4 * TB
    DG = at("cmb_diag", w, [P, 2, NT, P])
    CM, CU, CR_, CN = (at("cmb_" + x, w + 2 * NT * 512 + n * 160, [P, RH * NT]) for n, x in enumerate(
        ("mean", "inv", "rstd", "newton")))
    c_sq, c_ps, c_ch, c_rt, c_th, c_hh, c_dg, c_bc, c_si, c_mx, c_ot = (sem("cmb_" + x) for x in (
        "squares", "sums", "chain", "root", "tanh", "hi", "diag", "spread", "silu", "scaled", "mixed"))

    def s4_pool(pool):
        for t, n in ((WR, "w_rgate"), (WI, "w_igate")):
            pool.dma_start(t[:, :, :], a[n][0].rearrange("n i j -> i n j")).then_inc(l_ld, 16)
        pool.dma_start(CR[:, :], a["state_conv"][0].rearrange("b c w -> (b c) w")).then_inc(l_ld, 16)
        pool.dma_start(HR[:, :], a["state_lru"][0]).then_inc(l_ld, 16)
        pool.wait_ge(c_gt, 16)
        pool.wait_ge(r_so, 32)
        pool.wait_ge(r_ss, 64)

    def s4_act(act):
        for h in range(RH):
            act.activation(T1[:, h, :], OTP[:, h, :], ACT.Square).then_inc(c_sq, 1)
        for h in range(RH):
            if h == 0:
                act.wait_ge(c_gt, 16)
            act.activation(T3[:, h, :], T2[:, h, :], ACT.Tanh, scale=0.5).then_inc(c_th, 1)
        act.wait_ge(c_ch, 2)
        act.activation(CR_[:, :], CU[:, :], ACT.Sqrt).then_inc(c_rt, 1)
        for h in range(RH):
            act.wait_ge(c_ot, h + 1)
            act.activation(HHI[:, h, :], OTP[:, h, :], ACT.Copy, scale=0.5).then_inc(c_hh, 1)

    def s4_pe(pe):
        for h in range(RH):
            pe.wait_ge(c_sq, h + 1)
            for t in range(NT):
                c0 = (h * NT + t) * 2
                mm = pe.matmul(PS[:, 6, c0:c0 + 2], T1[:, h, win(t):win(t) + P], ones[:, 0:2], start=True, stop=True)
        mm.then_inc(c_ps, 1)
        for h in range(RH):
            pe.wait_ge(c_dg, h + 1)
            if h >= 2:
                pe.wait_ge(c_mx, h - 1)
            for t in range(NT):
                c0 = t * P
                r0 = 0 if t < QT else TW - SEQ - P
                mm = pe.matmul(PS[:, 3 * (h % 2) + c0 // 512, c0 % 512:c0 % 512 + P + min(r0, 0)], ones[:, :],
                               DG[:, h % 2, t, -min(r0, 0):P], start=True, stop=True)
            mm.then_inc(c_bc, 1)

    def s4_dve(dve):
        for h in range(RH):
            dve.wait_ge(c_th, h + 1)
            dve.scalar_tensor_tensor(T2[:, h, :], T3[:, h, :], 1.0, T2[:, h, :], ALU.add, ALU.mult).then_inc(c_si, 1)
            if h == 0:
                dve.wait_ge(c_ps, 1)
                dve.tensor_scalar(CM[:, :], PS[:, 6, 0:2 * RH * NT].rearrange("p (t e) -> p t e", e=2)[:, :, 0], 1.0 / DV,
                                  EPS, ALU.mult, ALU.add).then_inc(c_ch, 1)
                dve.wait_ge(c_ch, 1)
                dve.reciprocal(CU[:, :], CM[:, :]).then_inc(c_ch, 1)
        dve.wait_ge(c_rt, 1)
        dve.tensor_tensor(CN[:, :], CR_[:, :], CR_[:, :], ALU.mult).then_inc(c_ch, 1)
        dve.wait_ge(c_ch, 3)
        dve.tensor_tensor(CN[:, :], CN[:, :], CM[:, :], ALU.mult).then_inc(c_ch, 1)
        dve.wait_ge(c_ch, 4)
        dve.tensor_scalar(CN[:, :], CN[:, :], -0.5, 1.5, ALU.mult, ALU.add).then_inc(c_ch, 1)
        dve.wait_ge(c_ch, 5)
        dve.tensor_tensor(CR_[:, :], CR_[:, :], CN[:, :], ALU.mult).then_inc(c_ch, 1)
        dve.wait_ge(c_ch, 6)
        dve.wait_ge(c_si, RH)

        def diag(h):
            if h >= 2:
                dve.wait_ge(c_bc, h - 1)
            dve.tensor_tensor(DG[:, h % 2, :, :], ident[:, :].unsqueeze(1).to_broadcast([P, NT, P]),
                              CR_[:, h * NT:(h + 1) * NT].unsqueeze(2).to_broadcast([P, NT, P]), ALU.mult).then_inc(c_dg, 1)

        diag(0)
        diag(1)
        for h in range(RH):
            dve.wait_ge(c_bc, h + 1)
            r = PS[:, 3 * (h % 2):3 * (h % 2) + 3, :].rearrange("p a w -> p (a w)")[:, 0:TW]
            dve.scalar_tensor_tensor(OTP[:, h, :], OTP[:, h, :], vec[:, V_RG + h:V_RG + h + 1], r,
                                     ALU.mult, ALU.mult).then_inc(c_mx, 1)
            if h + 2 < RH:
                diag(h + 2)
            dve.wait_ge(c_mx, h + 1)
            dve.tensor_tensor(OTP[:, h, :], OTP[:, h, :], T2[:, h, :], ALU.mult).then_inc(c_ot, 1)
            if h:
                low(dve, h - 1)
        low(dve, RH - 1)

    def low(dve, h):
        dve.wait_ge(c_hh, h + 1)
        dve.scalar_tensor_tensor(HLO[:, h, :], OTP[:, h, :], 0.5, HHI[:, h, :].bitcast(F32), ALU.mult, ALU.subtract)

    stage(s4_pe, s4_act, s4_dve, s4_pool)

    w = O_X
    XPP = at("lru_x", w, [P, 2, CONV - 1 + SEQ])
    XPS = at("lru_xs", w + 8224, [P, 2, DB, CONV - 1 + DS])
    bufs = [w + 8928 + n * TA for n in range(5)] + [O_WORK + n * TA for n in range(3)]
    w = O_WORK + 3 * TA
    YL = at("lru_y", w, [P, 2, TW])
    w += 2 * TA
    bufs += [w + n * TA for n in range(3)]
    w += 3 * TA
    XC, GR, GI, AA, GE = ([at(f"lru_{x}{i}", bufs[2 * n + i], [P, TW]) for i in range(2)]
                          for n, x in enumerate(("xc", "r", "i", "a", "gelu")))
    SA = at("lru_1_aa", bufs[10], [P, TW])
    WR = at("lru_wr", w, [P, 4, P])
    WI = at("lru_wi", w + 2048, [P, 4, P])
    CR = at("lru_conv_rows", w + 4096, [DB * 3, LW])
    HR = at("lru_h_rows", w + 6144, [DB, LW])
    HT = at("lru_h0", w + 8192, [P, 4, DB])
    CT = at("lru_conv0", w + 8320, [P, 4, DB * 3])
    NO = 36
    GO = at("lru_out_cols", w + 8704, [P, 4, NO])
    RO = at("lru_out_rows", w + 4096, [NO, LW])
    SC = at("lru_sc", w + 9280, [P, 8, 4])
    TMP = at("lru_tmp", w + 9408, [P, DB])
    l_ld, l_st, l_ct, l_d, l_a, l_pe, l_out, l_rows, l_sp, l_z = (sem("lru_" + x) for x in (
        "consts_in", "start_turned", "start_out", "dve", "act", "pe", "rows_in", "stored", "softplus", "zero"))
    l_x = [sem(f"lru_x_in{i}") for i in range(2)]
    l_y = [sem(f"lru_y_in{i}") for i in range(2)]
    GC = (2.0 / np.pi) ** 0.5

    def s5_pool(pool):
        def load_x(j):
            s = j % 2
            pool.dma_start(XPP[:, s, CONV - 1:], proj[8 + j, :, 0:SEQ]).then_inc(l_x[s], 16)
            pool.dma_start(XPS[:, s, :, CONV - 1:], proj[8 + j, :, S0:TW].rearrange("p (b s) -> p b s", b=DB)).then_inc(l_x[s], 16)

        def load_y(j):
            pool.dma_start(YL[:, j % 2, :], proj[12 + j]).then_inc(l_y[j % 2], 16)

        load_x(0)
        pool.memset(XPP[:, :, 0:CONV - 1], 0.0).then_inc(l_z, 1)
        for t in XC:
            pool.memset(t[:, SEQ:S0], 0.0).then_inc(l_z, 1)
        load_y(0)
        load_x(1)
        load_y(1)
        for j in (2, 3):
            pool.wait_ge(l_d, dn["gx", j - 2])
            pool.wait_ge(l_a, an["x", j - 2])
            load_x(j)
            pool.wait_ge(l_d, dn["g", j - 2])
            load_y(j)
        pool.wait_ge(l_out, 1)
        o = [("lru_prompt", 0, 1), ("lru_sample", 1, 9), ("conv_prompt", 9, 12), ("conv_sample", 12, 36)]
        for name, r0, r1 in o:
            dst = a[name][0] if name != "conv_sample" else a[name][0].rearrange("b c w -> (b c) w")
            if name == "conv_prompt":
                dst = dst[0]
            pool.dma_start(dst, RO[r0:r1, :]).then_inc(l_rows, 16)

    d_order = [(x, 0) for x in ("xs", "c0", "c1", "c2", "gx", "gi")]
    a_order = [(x, 0) for x in ("x", "q", "gt", "r", "i", "e", "t")]
    for j in range(4):
        nxt = j + 1 if j < 3 else None
        for x, y in (("u", j), ("xs", nxt), ("c0", nxt), ("c1", nxt), ("c2", nxt), ("gx", nxt), ("s", j),
                     ("g", j), ("i", j), ("gi", nxt), ("b", j), ("b0", j), ("b1", j), ("b2", j), ("h", j), ("go", j),
                     ("m", j), ("lo", j)):
            if y is not None:
                d_order.append((x, y))
        for x, y in (("x", nxt), ("a", j), ("q", nxt), ("sq", j), ("gt", nxt), ("r", nxt), ("i", nxt), ("e", nxt),
                     ("t", nxt), ("hh", j)):
            if y is not None:
                a_order.append((x, y))
    dn = {x: n + 1 for n, x in enumerate(d_order)}
    an = {x: n + 1 for n, x in enumerate(a_order)}

    def s5_pe(pe):
        pe.wait_ge(l_ld, 64)
        for j in range(4):
            pe.transpose(PS[:, 6, j * 24:(j + 1) * 24], CR[:, j * P:(j + 1) * P], ident[0:24, 0:24])
            mm = pe.transpose(PS[:, 6, 128 + j * DB:128 + (j + 1) * DB], HR[:, j * P:(j + 1) * P], ident[0:DB, 0:DB])
        mm.then_inc(l_st, 1)
        for j in range(4):
            pe.wait_ge(l_d, dn["c2", j])
            if j:
                pe.wait_ge(l_a, an["i", j - 1])
            for g, wt in enumerate((WR, WI)):
                for c in range(NCH):
                    mm = pe.matmul(PS[:, 3 * g + c, 0:CW], wt[:, j, :], XC[j % 2][:, c * CW:(c + 1) * CW],
                                   start=True, stop=True)
                mm.then_inc(l_pe, 1)
        pe.wait_ge(l_d, dn["lo", 3])
        for j in range(4):
            mm = pe.transpose(PS[0:NO, 7, j * P:(j + 1) * P], GO[:, j, :], ident[:, :])
        mm.then_inc(l_st, 1)

    def s5_act(act):
        act.activation(SC[:, 0, :], vec[:, V_LAM:V_LAM + 4], ACT.Abs).then_inc(l_sp, 1)
        act.wait_ge(l_sp, 1)
        act.activation(SC[:, 1, :], SC[:, 0, :], ACT.Exp, scale=-1.0).then_inc(l_sp, 1)
        act.wait_ge(l_sp, 2)
        act.activation(SC[:, 2, :], SC[:, 1, :], ACT.Ln, bias=1.0).then_inc(l_sp, 1)
        act.wait_ge(l_z, 3)
        act.wait_ge(l_ct, 1)
        v3 = lambda t: t.rearrange("p (c w) -> p c w", c=NCH)
        for x, j in a_order:
            s = j % 2
            if x == "x":
                act.wait_ge(l_x[s], 32 * (j // 2 + 1))
                if j >= 2:
                    act.wait_ge(l_d, dn["i", j - 2])
                w3 = vec[:, V_CW + 12 + j:V_CW + 13 + j]
                cb = vec[:, V_CB + j:V_CB + j + 1]
                act.activation(XC[s][:, 0:SEQ], XPP[:, s, CONV - 1:], ACT.Identity, bias=cb, scale=w3)
                op = act.activation(XC[s][:, S0:TW].rearrange("p (b s) -> p b s", b=DB), XPS[:, s, :, CONV - 1:],
                                    ACT.Identity, bias=cb, scale=w3)
            elif x == "q":
                if j >= 2:
                    act.wait_ge(l_d, dn["lo", j - 2])
                act.wait_ge(l_y[s], 16 * (j // 2 + 1))
                op = act.activation(GE[s][:, :], YL[:, s, :], ACT.Square, scale=0.044715 ** 0.5)
            elif x == "gt":
                act.wait_ge(l_d, dn["gi", j])
                op = act.activation(GE[s][:, :], GE[s][:, :], ACT.Tanh, scale=GC)
            elif x == "r":
                act.wait_ge(l_sp, 6)
                act.wait_ge(l_pe, 2 * j + 1)
                op = act.activation(v3(GR[s][:, :]), PS[:, 0:3, 0:CW], ACT.Tanh, bias=SC[:, 4, j:j + 1], scale=0.5)
            elif x == "i":
                act.wait_ge(l_pe, 2 * j + 2)
                op = act.activation(v3(GI[s][:, :]), PS[:, 3:6, 0:CW], ACT.Tanh, bias=SC[:, 5, j:j + 1], scale=0.5)
            elif x == "e":
                act.wait_ge(l_a, an["r", j])
                op = act.activation(AA[s][:, :], GR[s][:, :], ACT.Exp, bias=SC[:, 1, j:j + 1], scale=SC[:, 1, j:j + 1])
            elif x == "t":
                act.wait_ge(l_a, an["e", j])
                op = act.activation(GR[s][:, :], GR[s][:, :], ACT.Tanh, bias=SC[:, 6, j:j + 1], scale=SC[:, 6, j:j + 1])
            elif x == "a":
                act.wait_ge(l_d, dn["u", j])
                op = act.activation(AA[s][:, :], GR[s][:, :], ACT.Identity, bias=1.0, scale=-1.0)
            elif x == "sq":
                act.wait_ge(l_d, dn["s", j])
                op = act.activation(SA[:, :], SA[:, :], ACT.Sqrt)
            else:
                act.wait_ge(l_d, dn["m", j])
                op = act.activation(HHI[:, 4 + j, :], GE[s][:, :], ACT.Copy, scale=0.5)
            op.then_inc(l_a, 1)

    def s5_dve(dve):
        dve.wait_ge(l_sp, 3)
        dve.tensor_scalar(SC[:, 3, :], vec[:, V_LAM:V_LAM + 4], -1.0, 0.0, ALU.mult, ALU.max).then_inc(l_sp, 1)
        dve.wait_ge(l_sp, 4)
        dve.tensor_tensor(SC[:, 7, :], SC[:, 3, :], SC[:, 2, :], ALU.add).then_inc(l_sp, 1)
        dve.tensor_scalar(SC[:, 4:6, :], vec[:, V_BR:V_BR + 8].rearrange("p (a b) -> p a b", a=2), 0.5, None, ALU.mult)
        dve.wait_ge(l_sp, 5)
        dve.tensor_scalar(SC[:, 1, :], SC[:, 7, :], -LRU_C / 2, None, ALU.mult)
        dve.tensor_scalar(SC[:, 6, :], SC[:, 7, :], LRU_C / 4, None, ALU.mult).then_inc(l_sp, 1)
        dve.wait_ge(l_st, 1)
        dve.tensor_copy(CT[:, :, :], PS[:, 6, 0:96].rearrange("p (j c) -> p j c", j=4)).then_inc(l_ct, 1)
        dve.tensor_copy(HT[:, :, :], PS[:, 6, 128:160].rearrange("p (j c) -> p j c", j=4)).then_inc(l_ct, 1)
        dve.wait_ge(l_ct, 2)
        for n, (x, j) in enumerate(d_order):
            s = j % 2
            rows = lambda t: t[:, S0:TW].rearrange("p (b s) -> p b s", b=DB)
            y, xc, r, gi, aa, ge = YL[:, s, :], XC[s], GR[s], GI[s], AA[s], GE[s]
            a0, b0 = rows(aa)[:, :, 0], rows(gi)[:, :, 0]
            if x == "xs":
                dve.wait_ge(l_x[s], 32 * (j // 2 + 1))
                op = dve.tensor_copy(XPS[:, s, :, 0:CONV - 1], CT[:, j, :].rearrange("p (b c) -> p b c", b=DB))
            elif x in ("c0", "c1", "c2"):
                i = int(x[1])
                if i == 0:
                    dve.wait_ge(l_a, an["x", j])
                wc = vec[:, V_CW + 4 * i + j:V_CW + 4 * i + j + 1]
                dve.scalar_tensor_tensor(xc[:, 0:SEQ], XPP[:, s, i:i + SEQ], wc, xc[:, 0:SEQ], ALU.mult, ALU.add)
                op = dve.scalar_tensor_tensor(rows(xc), XPS[:, s, :, i:i + DS], wc, rows(xc), ALU.mult, ALU.add)
            elif x == "gi":
                dve.wait_ge(l_y[s], 16 * (j // 2 + 1))
                dve.wait_ge(l_a, an["q", j])
                op = dve.scalar_tensor_tensor(ge[:, :], ge[:, :], 1.0, y, ALU.add, ALU.mult)
            elif x == "u":
                dve.wait_ge(l_a, an["t", j])
                op = dve.scalar_tensor_tensor(r[:, :], aa[:, :], 1.0, r[:, :], ALU.add, ALU.mult)
            elif x == "s":
                dve.wait_ge(l_a, an["a", j])
                op = dve.scalar_tensor_tensor(SA[:, :], aa[:, :], 1.0, r[:, :], ALU.add, ALU.mult)
            elif x == "i":
                op = dve.scalar_tensor_tensor(gi[:, :], gi[:, :], 1.0, xc[:, :], ALU.add, ALU.mult)
            elif x == "b":
                dve.wait_ge(l_a, an["sq", j])
                op = dve.scalar_tensor_tensor(gi[:, :], gi[:, :], 0.5, SA[:, :], ALU.mult, ALU.mult)
            elif x == "b0":
                op = dve.tensor_tensor(TMP[:, :], a0, HT[:, j, :], ALU.mult)
            elif x == "b1":
                op = dve.tensor_tensor(b0, b0, TMP[:, :], ALU.add)
            elif x == "b2":
                op = dve.tensor_scalar(a0, a0, 0.0, None, ALU.mult)
            elif x == "h":
                op = dve.tensor_tensor_scan(r[:, :], aa[:, :], gi[:, :], 0.0, ALU.mult, ALU.add)
            elif x == "go":
                dve.tensor_copy(GO[:, j, 0:1], r[:, SEQ - 1:SEQ])
                op = dve.tensor_copy(GO[:, j, 1:1 + DB], rows(r)[:, :, DS - 1])
            elif x == "gx":
                dve.tensor_copy(GO[:, j, 9:12], XPP[:, s, SEQ:SEQ + 3])
                op = dve.tensor_copy(GO[:, j, 12:NO].rearrange("p (b c) -> p b c", b=DB), XPS[:, s, :, DS:DS + 3])
            elif x == "g":
                dve.wait_ge(l_a, an["gt", j])
                op = dve.scalar_tensor_tensor(ge[:, :], ge[:, :], 1.0, y, ALU.add, ALU.mult)
            elif x == "m":
                op = dve.tensor_tensor(ge[:, :], ge[:, :], r[:, :], ALU.mult)
            else:
                dve.wait_ge(l_a, an["hh", j])
                op = dve.scalar_tensor_tensor(HLO[:, 4 + j, :], ge[:, :], 0.5, HHI[:, 4 + j, :].bitcast(F32),
                                              ALU.mult, ALU.subtract)
            op.then_inc(l_d, 1)
            dve.wait_ge(l_d, n + 1)
        dve.wait_ge(l_st, 2)
        dve.tensor_copy(RO[:, :], PS[0:NO, 7, :]).then_inc(l_out, 1)

    stage(s5_pe, s5_act, s5_dve, s5_pool)

    o_in, o_out, o_x = sem("out_tile_in"), sem("out_tile_done"), sem("x_back")

    def out_projection(layer, n0, park):
        d0 = layer * KT

        def pe_(pe):
            for j in range(N_OUT):
                pe.wait_ge(wl_done, n0 + j + 1)
                for m in range(2):
                    t = 2 * j + m
                    if t >= 2:
                        pe.wait_ge(o_out, d0 + t - 1)
                    fm_tile(pe, 3 * m, (n0 + j) % RING, col_tiles(m), None, HHI, HLO, o_in)
                pe.drain().then_inc(pe_done, 1)

        def act_(act):
            for j in range(N_OUT):
                split_hi(act, n0 + j + RING, (n0 + j) % RING)

        def dve_(dve):
            dve.wait_ge(o_x, 16 * (layer + 1))
            for j in range(N_OUT):
                for m in range(2):
                    t = 2 * j + m
                    dve.wait_ge(o_in, d0 + t + 1)
                    x = X[:, t, :].rearrange("p (c w) -> p c w", c=NCH)
                    dve.tensor_tensor(x, x, PS[:, 3 * m:3 * m + 3, 0:CW], ALU.add).then_inc(o_out, 1)
                split_lo(dve, n0 + j + RING, (n0 + j) % RING)

        def pool_(pool):
            pool.dma_start(X[:, :, :].rearrange("p k w -> p (k w)"), park).then_inc(o_x, 16)
            if layer == 0:
                pool.wait_ge(l_rows, 64)

        return pe_, act_, dve_, pool_

    stage(*out_projection(0, B_OUT0, parkx))

    TG = at("ffn_t", O_WORK + TA, [P, TW])
    TT = at("ffn_t2", O_WORK + 2 * TA, [P, TW])
    GH = at("ffn_hi", O_WORK + 3 * TA, [P, 2, 2, TW], F32R)
    GL = at("ffn_lo", O_WORK + 3 * TA + 4 * TB, [P, 2, 2, TW], F32R)

    def ffn_load(sp, n0, layer):
        wg, wu, wd = a["w_ffn_gate"][layer], a["w_ffn_up"][layer], a["w_ffn_down"][layer]
        load_block(sp, n0, columns(wg, 0))
        load_block(sp, n0 + 1, columns(wu, 0))
        with sp.Fori(1, NG) as g:
            load_block(sp, n0 - 1 + 3 * g, columns(wg, g))
            load_block(sp, n0 + 3 * g, columns(wu, g))
            load_block(sp, n0 + 1 + 3 * g, rows(wd, g - 1))
        load_block(sp, n0 + 3 * NG - 1, rows(wd, NG - 1))

    def ffn(tag, n0, g_col, layer):
        q = 3 if layer else 1
        a_in, a_out, b_in, b_out, fch, fgh, gl_in = (sem(f"{x}_{tag}") for x in (
            "bank_a_in", "bank_a_out", "bank_b_in", "bank_b_out", "hidden_steps", "hidden_act", "hidden_lo"))
        sg, su, sd = ((n0 + i) % RING for i in (2, 0, 1))
        last = n0 + 3 * NG == NBLK
        v3 = lambda t: t.rearrange("p (c w) -> p c w", c=NCH)

        def pe_(pe):
            def up(nb, slots, xa, first=False):
                hold(pe, wl_done, nb + 2, "pe")
                for f in range(2):
                    if not isinstance(xa, int) or xa + f > 0:
                        hold(pe, a_out, xa + f, "pe")
                    hook = [prep_tile(pe, q, n) if first and f == 0 else None for n in range(2)]
                    fm_tile(pe, 0, slots[0], col_tiles(f), hook[0], HHI, HLO, a_in)
                    if f == 1:
                        pe.drain().then_inc(pe_done, 1)
                    if not isinstance(xa, int) or xa + f > 0:
                        hold(pe, b_out, xa + f, "pe")
                    fm_tile(pe, 3, slots[1], col_tiles(f), hook[1], HHI, HLO, b_in)
                    if first and f == 0:
                        prep_spread(pe, q, SPREAD[2:])
                pe.drain().then_inc(pe_done, 1)

            def down(g, nb, slot, par, xa):
                hold(pe, wl_done, nb + 1, "pe")
                hold(pe, gl_in, g * 2 + 2, "pe")
                for m in range(KT):
                    hold(pe, (a_out, b_out)[m % 2], xa + m // 2, "pe")
                    fm_tile(pe, 3 * (m % 2), slot, [f * D + m * P for f in range(2)], None, GH[:, par], GL[:, par],
                            (a_in, b_in)[m % 2])
                pe.drain().then_inc(pe_done, 1)

            def group(g, par):
                up(n0 - 1 + 3 * g, (sg, su), g * 6 - 4)
                down(g - 1, n0 + 1 + 3 * g, sd, 1 - par, g * 6 - 2)

            up(n0, (n0 % RING, (n0 + 1) % RING), 0, first=True)
            with pe.Fori(0, (NG - 3) // 2) as i:
                group(2 * i + 1, 1)
                group(2 * i + 2, 0)
            group(NG - 2, 1)
            group(NG - 1, 0)
            down(NG - 1, n0 + 3 * NG - 1, (n0 + 2) % RING, 0, 6 * NG - 4)

        def act_(act):
            prep_act(act, q, g_col)

            def hidden(x, par, f):
                hold(act, fch, x * 4 + 1, "act")
                act.activation(TT[:, :], TG[:, :], ACT.Tanh, scale=0.5).then_inc(fgh, 1)
                hold(act, fch, x * 4 + 4, "act")
                act.activation(GH[:, par, f, :], TG[:, :], ACT.Copy).then_inc(fgh, 1)

            def group(g, par, s):
                hidden(2 * g, par, 0)
                split_hi(act, n0 + 2 + 3 * g, sg)
                hidden(2 * g + 1, par, 1)
                for i, slot in ((1, su), (2, sd)):
                    if i < s:
                        split_hi(act, n0 + 2 + 3 * g + i, slot)

            hidden(0, 0, 0)
            split_hi(act, n0 + 3, n0 % RING)
            hidden(1, 0, 1)
            split_hi(act, n0 + 4, (n0 + 1) % RING)
            with act.Fori(0, (NG - 3) // 2) as i:
                group(2 * i + 1, 1, 3)
                group(2 * i + 2, 0, 3)
            group(NG - 2, 1, 3)
            group(NG - 1, 0, 1 if last else 3)
            if not last:
                split_hi(act, n0 + 3 * NG + 2, (n0 + 2) % RING)

        def dve_(dve):
            prep_dve(dve, q, g_col)
            r3 = v3(R[:, :])

            def gate(x, xa):
                hold(dve, a_in, xa + 1, "dve")
                i = dve.tensor_tensor(v3(TG[:, :]), PS[:, 0:3, 0:CW], r3, ALU.mult)
                i.then_inc(fch, 1)
                hold(dve, fgh, x * 2 + 1, "dve")
                dve.sem_inc(a_out, 1)
                dve.scalar_tensor_tensor(TT[:, :], TT[:, :], 1.0, TG[:, :], ALU.add, ALU.mult).then_inc(fch, 1)

            def product(x, xa):
                hold(dve, b_in, xa + 1, "dve")
                hold(dve, fch, x * 4 + 2, "dve")
                dve.tensor_tensor(v3(TG[:, :]), PS[:, 3:6, 0:CW], r3, ALU.mult).then_inc(fch, 1)
                hold(dve, fch, x * 4 + 3, "dve")
                dve.scalar_tensor_tensor(TG[:, :], TT[:, :], 0.5, TG[:, :], ALU.mult, ALU.mult).then_inc(fch, 1)
                dve.sem_inc(b_out, 1)

            def low(x, par, f):
                hold(dve, fgh, x * 2 + 2, "dve")
                dve.tensor_tensor(GL[:, par, f, :], TG[:, :], GH[:, par, f, :].bitcast(F32), ALU.subtract).then_inc(gl_in, 1)
                hold(dve, gl_in, x + 1, "dve")

            def residual(m, xa):
                hold(dve, (a_in, b_in)[m % 2], xa + m // 2 + 1, "dve")
                x = v3(X[:, m, :])
                b0 = 3 * (m % 2)
                dve.tensor_tensor(x, x, PS[:, b0:b0 + 3, 0:CW], ALU.add).then_inc((a_out, b_out)[m % 2], 1)

            def group(g, par, s):
                x, xa = 2 * g, g * 6 - 4
                gate(x, xa)
                product(x, xa)
                low(x, par, 0)
                gate(x + 1, xa + 1)
                split_lo(dve, n0 + 2 + 3 * g, sg)
                product(x + 1, xa + 1)
                residual(0, xa + 2)
                low(x + 1, par, 1)
                residual(1, xa + 2)
                residual(2, xa + 2)
                residual(3, xa + 2)
                if s > 1:
                    split_lo(dve, n0 + 3 + 3 * g, su)
                for m in (4, 5, 6, 7):
                    residual(m, xa + 2)
                if s > 2:
                    split_lo(dve, n0 + 4 + 3 * g, sd)

            gate(0, 0)
            product(0, 0)
            low(0, 0, 0)
            gate(1, 1)
            split_lo(dve, n0 + 3, n0 % RING)
            product(1, 1)
            low(1, 0, 1)
            split_lo(dve, n0 + 4, (n0 + 1) % RING)
            with dve.Fori(0, (NG - 3) // 2) as i:
                group(2 * i + 1, 1, 3)
                group(2 * i + 2, 0, 3)
            group(NG - 2, 1, 3)
            group(NG - 1, 0, 1 if last else 3)
            for m in range(KT):
                residual(m, 6 * NG - 4)
            if not last:
                split_lo(dve, n0 + 3 * NG + 2, (n0 + 2) % RING)

        def pool_(pool):
            pass

        return pe_, act_, dve_, pool_

    stage(*ffn("ffn0", B_FFN0, G_FFN[0], 0))

    q8 = 2
    (v_in, v_out, v_st, v_sq, v_nrm, v_park) = (sem("qkv_" + x) for x in (
        "unit_in", "unit_out", "steps", "root", "normed", "parked"))
    v_dma = [sem(f"qkv_stored{i}") for i in range(2)]
    AB = at("qkv_tok", O_WORK + TA, [P, 2, NT, BW])
    SB = at("qkv_sq", O_WORK + TA + 2 * NT * BW * 4, [P, NT, BW])
    NHB = BW // DH
    SSV = at("qkv_ss", O_WORK + TA + 3 * NT * BW * 4, [P, NT * NHB])
    SSR = at("qkv_rs", O_WORK + TA + 3 * NT * BW * 4 + 160, [P, NT * NHB])
    SSU = at("qkv_ru", O_WORK + TA + 3 * NT * BW * 4 + 320, [P, NT * NHB])
    BANKS = (6, 0, 1)

    def s8_pe(pe):
        prep_sums(pe, q8)
        prep_wait(pe, q8, "hl_in", KT)
        with pe.Fori(0, N_QKV // RING) as i:
            for jj in range(RING):
                hold(pe, wl_done, B_QKV + 1 + jj + i * RING, "pe")
                for t in range(NT):
                    hold(pe, v_out, i * (RING * NT) + (jj * NT + t + 1), "pe")
                    tm_unit(pe, BANKS[(jj * NT + t) % 3], (B_QKV + jj) % RING, t, v_in)
                pe.drain().then_inc(pe_done, 1)

    def s8_act(act):
        act.sem_inc(v_out, 3)
        prep_act(act, q8, G_MIX[1], fm=False)
        prep_wait(act, q8, "rchain", 6)

        def root(j):
            act.wait_ge(v_st, 9 * j + 4)
            act.activation(SSR[:, :], SSU[:, :], ACT.Sqrt).then_inc(v_sq, 1)

        for j in range(N_QKV):
            par = j % 2
            for t in range(NT):
                u = j * NT + t
                act.wait_ge(v_in, u + 1)
                if t == 0 and j >= 2:
                    act.wait_ge(v_dma[par], 32 * (j // 2))
                act.activation(AB[:, par, t, :], PS[:, BANKS[u % 3], 0:BW], ACT.Copy, scale=rtok[:, t, 0:1]).then_inc(v_out, 1)
                if t == 3 and 1 <= j <= 8:
                    root(j - 1)
            split_hi(act, B_QKV + j + RING, (B_QKV + j) % RING)

    def s8_dve(dve):
        prep_dve(dve, q8, G_MIX[1], fm=False)
        for j in range(N_QKV):
            if j < 8:
                n = [9 * j]

                def step(x):
                    x.then_inc(v_st, 1)
                    n[0] += 1
                    dve.wait_ge(v_st, n[0])

                dve.wait_ge(v_out, 3 + NT * (j + 1))
                ab = AB[:, j % 2].rearrange("p t (h d) -> p (t h) d", h=NHB)
                step(dve.tensor_tensor(SB[:, :, :], AB[:, j % 2], AB[:, j % 2], ALU.mult))
                step(dve.tensor_reduce(SSV[:, :], SB[:, :, :].rearrange("p t (h d) -> p (t h) d", h=NHB), AX.X, ALU.add))
                step(dve.tensor_scalar(SSV[:, :], SSV[:, :], 1.0 / DH, EPS, ALU.mult, ALU.add))
                step(dve.reciprocal(SSU[:, :], SSV[:, :]))
                dve.wait_ge(v_sq, j + 1)
                step(dve.tensor_tensor(SSU[:, :], SSR[:, :], SSR[:, :], ALU.mult))
                step(dve.tensor_tensor(SSU[:, :], SSU[:, :], SSV[:, :], ALU.mult))
                step(dve.tensor_scalar(SSU[:, :], SSU[:, :], -0.5, 1.5, ALU.mult, ALU.add))
                step(dve.tensor_tensor(SSR[:, :], SSR[:, :], SSU[:, :], ALU.mult))
                step(dve.tensor_tensor(ab, ab, SSR[:, :].unsqueeze(2).to_broadcast([P, NT * NHB, DH]), ALU.mult))
                dve.tensor_tensor(ab, ab, gqk[:, j // 4, :].unsqueeze(1).to_broadcast([P, NT * NHB, DH]),
                                  ALU.mult).then_inc(v_nrm, 1)
            split_lo(dve, B_QKV + j + RING, (B_QKV + j) % RING)

    qp = qtok[0:SEQ, :].rearrange("(t p) c -> p t c", p=P)
    kp = a["k_prompt"][0, 0].rearrange("(t p) h d -> p t (h d)", p=P)
    vp = a["v_prompt"][0, 0].rearrange("(t p) h d -> p t (h d)", p=P)
    qs_, ks_, vs_ = (qtok[SEQ:SEQ + NS, :], a["k_sample"][0].rearrange("b s h d -> (b s) (h d)"),
                     a["v_sample"][0].rearrange("b s h d -> (b s) (h d)"))

    def s8_pool(pool):
        pool.dma_start(parkx, X[:, :, :].rearrange("p k w -> p (k w)")).then_inc(v_park, 16)
        for j in range(N_QKV):
            if j < 8:
                pool.wait_ge(v_nrm, j + 1)
            else:
                pool.wait_ge(v_out, 3 + NT * (j + 1))
            c = slice((j % 4) * BW, (j % 4 + 1) * BW)
            pool.dma_start((qp, kp, vp)[j // 4][:, :, c], AB[:, j % 2, 0:QT, :]).then_inc(v_dma[j % 2], 16)
            pool.dma_start((qs_, ks_, vs_)[j // 4][:, c], AB[P - NS:P, j % 2, QT, :]).then_inc(v_dma[j % 2], 16)
        for i in range(2):
            pool.wait_ge(v_dma[i], 32 * (N_QKV // 2))
        pool.wait_ge(v_park, 16)

    stage(s8_pe, s8_act, s8_dve, s8_pool)

    w = O_X
    QN = at("att_q", w, [P, QT, P])
    KN = at("att_k", w + 4096, [P, QT, P])
    VN = at("att_v", w + 8192, [P, 2, QT, P])
    SKQ = at("att_stack_q", w + 16384, [P, QT, P], F32R)
    SKH = at("att_stack_kh", w + 20480, [P, QT, P], F32R)
    SKL = at("att_stack_kl", w + 24576, [P, QT, P], F32R)
    w = O_WORK
    QS = [at("att_qs0", w, [P, SEQ], F32R), at("att_qs1", O_X + 28672, [P, SEQ], F32R)]
    KHH = [at("att_khh0", w + 4096, [P, SEQ], F32R), at("att_khh1", O_RAW, [P, SEQ], F32R)]
    KLL = [at("att_kll0", w + 8192, [P, SEQ], F32R), at("att_kll1", O_RAW + 4096, [P, SEQ], F32R)]
    BI = at("att_bias", w + 12288, [P, 2, SEQ])
    SX = at("att_scores", w + 20480, [P, 2, SEQ])
    PT = at("att_pt", w + 28672, [P, 2, QT, P])
    OO = at("att_o", w + 36864, [P, QT, P])
    NBM = at("att_max", w + 40960, [P, 4])
    DEN = at("att_den", w + 40992, [P, 4])
    RDN = at("att_rden", w + 41024, [P, 4])
    (a_s, a_red, a_p, a_tp, a_tv, a_ta, a_oi, a_oo, a_sp, a_sv, a_qk, a_hh, a_rd) = (sem("att_" + x) for x in (
        "scores_in", "scores_max", "probs", "turned", "taken_dve", "taken_act", "out_in", "out_done", "split_steps",
        "split", "qk_loaded", "out_hi", "rden"))
    a_vl = [sem(f"att_v_loaded{i}") for i in range(2)]
    a_bl = [sem(f"att_bias_loaded{i}") for i in range(2)]
    NST = 4 * QT

    STACKS = 6

    def turns(last):
        units = []
        for n in range(NST + 2):
            if n < NST and n % QT >= 5 and not (last and n // QT == 3):
                units += [("stack", n // QT + 1, n % QT - 5, half, "a") for half in range(2)]
            if 1 <= n <= NST:
                qb = (n - 1) % QT
                units.append(("p", n - 1, 0, 0, "v"))
                if qb >= 4:
                    units.append(("p", n - 1, 1, 0, "a"))
            if n >= 2 and (n - 2) % (2 * QT) == 2 * QT - 1:
                units += [("out", (n - 2) // (2 * QT), half, 0, "v") for half in range(2)]
        taken = {"v": 0, "a": 0}
        after = []
        for x in units:
            taken[x[4]] += 1
            after.append(taken[x[4]])
        return units, after

    bodies = turns(False), turns(True)
    NU = len(bodies[0][0])
    NV_, NA2 = (sum(x[4] == e for x in bodies[0][0]) for e in "va")
    assert NU % 2 == 0

    def body_at(last):
        units, after = bodies[last]
        return units, after, lambda key: next(u for u, x in enumerate(units) if x[:len(key)] == key)

    def four_heads(eng, body):
        with eng.Fori(0, 3) as i:
            body(i, False)
        body(3, True)

    def s9_pe(pe):
        for u in range(STACKS):
            t = (SKQ, SKH, SKL)[u // 2]
            if u == 0:
                pe.wait_ge(a_sv, 1)
            if u >= 2:
                pe.wait_ge(a_ta, u - 1)
            for x in range(4):
                mm = pe.transpose(PS[:, 4 + u % 2, x * P:(x + 1) * P], t[:, 4 * (u % 2) + x, :].bitcast(F32), ident[:, :])
            mm.then_inc(a_tp, 1)
        pe.wait_ge(a_ta, STACKS)

        def body(i, last):
            units, after, unit_at = body_at(last)

            def turn(u, srcs):
                if u >= 2:
                    if units[u - 2][4] == "v":
                        hold(pe, a_tv, i * NV_ + after[u - 2], "pe")
                    else:
                        hold(pe, a_ta, i * NA2 + STACKS + after[u - 2], "pe")
                for x, src in enumerate(srcs):
                    mm = pe.transpose(PS[:, 4 + u % 2, x * P:(x + 1) * P], src, ident[:, :])
                mm.then_inc(a_tp, 1)

            for n in range(NST + 2):
                if n < NST:
                    hh, qb = divmod(n, QT)
                    if qb == 0 and hh:
                        hold(pe, a_ta, i * NA2 + STACKS + after[unit_at(("stack", hh, 2, 1))], "pe")
                    if n >= 2:
                        hold(pe, a_red, i * NST + n - 1, "pe")
                    W = (qb + 1) * P
                    for ps_, t in enumerate((KHH[hh % 2], KLL[hh % 2])):
                        for c in range(0, W, 512):
                            mm = pe.matmul(PS[:, 2 * (n % 2) + c // 512, 0:min(512, W - c)],
                                           QS[hh % 2][:, qb * P:(qb + 1) * P],
                                           t[:, c:min(W, c + 512)], start=(ps_ == 0), stop=(ps_ == 1))
                    mm.then_inc(a_s, 1)
                    if qb >= 5 and not (last and hh == 3):
                        if qb == 5:
                            hold(pe, a_sv, i * 4 + hh + 2, "pe")
                        t = (SKQ, SKH, SKL)[qb - 5]
                        for half in range(2):
                            turn(unit_at(("stack", hh + 1, qb - 5, half)),
                                 [t[:, x, :].bitcast(F32) for x in range(4 * half, 4 * half + 4)])
                if 1 <= n <= NST:
                    m = n - 1
                    hold(pe, a_p, i * NST + m + 1, "pe")
                    qb = m % QT
                    for g in range(1 + (qb >= 4)):
                        turn(unit_at(("p", m, g)), [SX[:, m % 2, x * P:(x + 1) * P]
                                                    for x in range(4 * g, min(qb + 1, 4 * g + 4))])
                if n >= 2:
                    m = n - 2
                    hh, qb = divmod(m, QT)
                    hold(pe, a_tv, i * NV_ + after[unit_at(("p", m, 0))], "pe")
                    if qb >= 4:
                        hold(pe, a_ta, i * NA2 + STACKS + after[unit_at(("p", m, 1))], "pe")
                    if m >= 2:
                        hold(pe, a_oo, i * NST + m - 1, "pe")
                    if m % (2 * QT) == 0:
                        hold(pe, a_vl[hh // 2], i * 16 + 16, "pe")
                    for x in range(qb + 1):
                        mm = pe.matmul(PS[:, 6 + m % 2, 0:DH], PT[:, m % 2, x, :],
                                       VN[:, hh // 2, x, (hh % 2) * DH:(hh % 2 + 1) * DH], start=(x == 0), stop=(x == qb))
                    mm.then_inc(a_oi, 1)
                    if m % (2 * QT) == 2 * QT - 1:
                        hold(pe, a_oo, i * NST + m + 1, "pe")
                        for half in range(2):
                            turn(unit_at(("out", hh // 2, half)), [OO[:, x, :] for x in range(4 * half, 4 * half + 4)])
            hold(pe, a_tv, i * NV_ + NV_, "pe")
            if not last:
                hold(pe, a_ta, i * NA2 + STACKS + NA2, "pe")

        four_heads(pe, body)

    def ps4(u, n=4):
        return PS[:, 4 + u % 2, 0:n * P]

    def s9_act(act):
        act.wait_ge(a_qk, 32)
        act.activation(SKQ[:, :, 0:DH], QN[:, :, 0:DH], ACT.Copy).then_inc(a_sp, 1)
        act.activation(SKH[:, :, :].rearrange("p t (r d) -> p t r d", r=2),
                       KN[:, :, 0:DH].unsqueeze(2).to_broadcast([P, QT, 2, DH]), ACT.Copy).then_inc(a_sp, 1)
        for u in range(STACKS):
            act.wait_ge(a_tp, u + 1)
            act.activation((QS, KHH, KLL)[u // 2][0][:, (u % 2) * 512:(u % 2 + 1) * 512], ps4(u), ACT.Copy).then_inc(a_ta, 1)

        def body(i, last):
            units, after, unit_at = body_at(last)

            def turned(u):
                hold(act, a_tp, i * NU + STACKS + u + 1, "act")

            for n in range(NST + 2):
                if n < NST:
                    hh, qb = divmod(n, QT)
                    if qb >= 5 and not (last and hh == 3):
                        for half in range(2):
                            u = unit_at(("stack", hh + 1, qb - 5, half))
                            turned(u)
                            t = (QS, KHH, KLL)[qb - 5][(hh + 1) % 2]
                            act.activation(t[:, half * 512:(half + 1) * 512], ps4(u), ACT.Copy).then_inc(a_ta, 1)
                    W = (qb + 1) * P
                    hold(act, a_red, i * NST + n + 1, "act")
                    act.activation(SX[:, n % 2, 0:W], SX[:, n % 2, 0:W], ACT.Exp, bias=NBM[:, n % 4:n % 4 + 1],
                                   scale=-1.0, accum_out=DEN[:, n % 4:n % 4 + 1]).then_inc(a_p, 1)
                if 1 <= n <= NST and (n - 1) % QT >= 4:
                    m = n - 1
                    qb = m % QT
                    u = unit_at(("p", m, 1))
                    turned(u)
                    hold(act, a_oi, i * NST + m - 1, "act")
                    act.activation(PT[:, m % 2, 4:qb + 1, :], ps4(u, qb - 3).rearrange("p (x w) -> p x w", w=P),
                                   ACT.Copy).then_inc(a_ta, 1)
                if n >= 2 and (n - 2) % (2 * QT) == 2 * QT - 1:
                    pp = (n - 2) // (2 * QT)
                    for half in range(2):
                        u = unit_at(("out", pp, half))
                        turned(u)
                        act.activation(HHI[:, bass.ds(i * 2 + pp, 1), half * 512:(half + 1) * 512].rearrange("p a w -> p (a w)"),
                                       ps4(u), ACT.Copy).then_inc(a_hh, 1)

        four_heads(act, body)

    def s9_dve(dve):
        dve.wait_ge(a_sp, 1)
        dve.tensor_tensor(SKQ[:, :, DH:P], QN[:, :, 0:DH], SKQ[:, :, 0:DH].bitcast(F32), ALU.subtract).then_inc(a_sp, 1)
        dve.wait_ge(a_sp, 3)
        dve.tensor_tensor(SKL[:, :, :].rearrange("p t (r d) -> p t r d", r=2),
                          KN[:, :, 0:DH].unsqueeze(2).to_broadcast([P, QT, 2, DH]),
                          SKH[:, :, :].rearrange("p t (r d) -> p t r d", r=2).bitcast(F32), ALU.subtract).then_inc(a_sp, 1)
        dve.wait_ge(a_sp, 4)
        dve.sem_inc(a_sv, 1)
        def body(i, last):
            units, after, unit_at = body_at(last)
            for n in range(NST + 2):
                if n >= 2:
                    m = n - 2
                    hold(dve, a_p, i * NST + m + 1, "dve")
                    dve.reciprocal(RDN[:, m % 4:m % 4 + 1], DEN[:, m % 4:m % 4 + 1]).then_inc(a_rd, 1)
                if n < NST:
                    hh, qb = divmod(n, QT)
                    W = (qb + 1) * P
                    hold(dve, a_s, i * NST + n + 1, "dve")
                    if qb == 0:
                        hold(dve, a_bl[hh % 2], i * 32 + 16 * (hh // 2 + 1), "dve")
                    src = PS[:, 2 * (n % 2):2 * (n % 2) + 2, :].rearrange("p a w -> p (a w)")[:, 0:W]
                    dve.tensor_tensor_reduce(SX[:, n % 2, 0:W], src, BI[:, hh % 2, SEQ - W:SEQ], -(DH ** -0.5), 3.0e38,
                                             ALU.add, ALU.min, NBM[:, n % 4:n % 4 + 1]).then_inc(a_red, 1)
                if 1 <= n <= NST:
                    m = n - 1
                    k = min(m % QT + 1, 4)
                    u = unit_at(("p", m, 0))
                    hold(dve, a_tp, i * NU + STACKS + u + 1, "dve")
                    if m >= 2:
                        hold(dve, a_oi, i * NST + m - 1, "dve")
                    dve.tensor_copy(PT[:, m % 2, 0:k, :], ps4(u, k).rearrange("p (x w) -> p x w", w=P)).then_inc(a_tv, 1)
                if n >= 2:
                    m = n - 2
                    hh, qb = divmod(m, QT)
                    hold(dve, a_rd, i * NST + m + 1, "dve")
                    hold(dve, a_oi, i * NST + m + 1, "dve")
                    dve.tensor_scalar(OO[:, qb, (hh % 2) * DH:(hh % 2 + 1) * DH], PS[:, 6 + m % 2, 0:DH],
                                      RDN[:, m % 4:m % 4 + 1], None, ALU.mult).then_inc(a_oo, 1)
                    if m % (2 * QT) == 2 * QT - 1:
                        pp = hh // 2
                        for half in range(2):
                            hold(dve, a_hh, i * 4 + pp * 2 + half + 1, "dve")
                            u = unit_at(("out", pp, half))
                            o = (bass.ds(i * 2 + pp, 1), slice(half * 512, (half + 1) * 512))
                            dve.tensor_tensor(HLO[:, o[0], o[1]].rearrange("p a w -> p (a w)"), ps4(u),
                                              HHI[:, o[0], o[1]].rearrange("p a w -> p (a w)").bitcast(F32),
                                              ALU.subtract).then_inc(a_tv, 1)

        four_heads(dve, body)

    def s9_pool(pool):
        def pair(view, hp):
            return view[:, :, bass.ds(hp * P, P)]

        def load_qk(hp):
            pool.dma_start(QN[:, :, :], pair(qp, hp)).then_inc(a_qk, 16)
            pool.dma_start(KN[:, :, :], pair(kp, hp)).then_inc(a_qk, 16)

        def load_v(hp, slot):
            pool.dma_start(VN[:, slot, :, :], pair(vp, hp)).then_inc(a_vl[slot], 16)

        def load_b(h, slot):
            pool.dma_start(BI[:, slot, :], a["c_bp"][bass.ds(h, 1), :, :].rearrange("a p w -> p (a w)")).then_inc(a_bl[slot], 16)

        def split(i, hh):
            hold(pool, a_qk, i * 64 + 32 * (hh // 2 + 1), "pool")
            e = slice((hh % 2) * DH, (hh % 2 + 1) * DH)
            k2 = KN[:, :, e].unsqueeze(2).to_broadcast([P, QT, 2, DH])
            v2 = lambda t: t[:, :, :].rearrange("p t (r d) -> p t r d", r=2)
            c = (i * 4 + hh) * 4
            pool.tensor_copy(SKQ[:, :, 0:DH], QN[:, :, e]).then_inc(a_sp, 1)
            hold(pool, a_sp, c + 1, "pool")
            pool.tensor_copy(v2(SKH), k2).then_inc(a_sp, 1)
            hold(pool, a_sp, c + 2, "pool")
            pool.tensor_tensor(SKQ[:, :, DH:P], QN[:, :, e], SKQ[:, :, 0:DH].bitcast(F32), ALU.subtract).then_inc(a_sp, 1)
            hold(pool, a_sp, c + 3, "pool")
            pool.tensor_tensor(v2(SKL), k2, v2(SKH).bitcast(F32), ALU.subtract).then_inc(a_sp, 1)
            hold(pool, a_sp, c + 4, "pool")
            pool.sem_inc(a_sv, 1)

        load_qk(0)
        load_b(0, 0)
        load_b(1, 1)
        load_v(0, 0)
        load_v(1, 1)

        def body(i, last):
            for hh in range(4):
                if not (last and hh == 3):
                    if hh:
                        hold(pool, a_tp, i * NU + STACKS + body_at(last)[2](("stack", hh, 2, 1)) + 1, "pool")
                    else:
                        hold(pool, a_tp, i * NU + STACKS, "pool")
                    split(i, hh + 1)
                    if hh == 0:
                        load_qk(i * 2 + 1)
                    if hh == 2 and not last:
                        load_qk(i * 2 + 2)
                if hh < 2 or not last:
                    hold(pool, a_red, i * NST + (hh + 1) * QT, "pool")
                    load_b(i * 4 + hh + 2, hh % 2)
                if hh % 2 and not last:
                    hold(pool, a_oi, i * NST + (hh + 1) * QT, "pool")
                    load_v(i * 2 + 2 + hh // 2, hh // 2)

        four_heads(pool, body)

    stage(s9_pe, s9_act, s9_dve, s9_pool)

    NU10 = 5
    UROW = 2 * P
    NPOS = NU10 * UROW + DS
    NQ = 4 * DS
    NZ, NZA, NZD = 23, 12, 11
    NSC = NU10 + 1
    UNIT = [at(f"cache_unit{u}", O_X + u * 8192 if u < 4 else O_WORK, [P, 2, D]) for u in range(NU10)]
    OALL = at("smp_out", O_X + 4 * 8192, [P, DB * DH])
    w = O_WORK + 8192
    KTS = at("smp_kt", w, [P, 2, HP, UROW])
    QSN = at("smp_q_rows", w, [NS, D])
    KSN = at("smp_k_rows", w + 8192, [NS, D])
    ODUP = at("smp_out_twice", w, [P, DB, 2, DH])
    w += 16384
    SS = at("smp_scores", w, [P, NPOS])
    O4 = at("smp_out4", w, [P, 4, DH])
    w += (NPOS * 4 + 31) // 32 * 32
    PTS = at("smp_pt", w, [P, 2 * NU10 + 1, P])
    w += 11 * 512
    BSS = at("smp_bias", w, [P, NPOS])
    w += (NPOS * 4 + 31) // 32 * 32
    QB = at("smp_q_blocks", w, [P, HP, NQ])
    QTS = at("smp_qt", w + 1024, [P, HP, NS])
    VNB = at("smp_v_new", w + 3072, [DS, D])
    KNB = at("smp_k_new", w + 7168, [P, HP, DS])
    KTNF = at("smp_ktn", O_HH, [P, KT, TW])
    KTN = KTNF[:, :, S0:TW]
    w = O_X + 4 * 8192 + 2048
    NMN = at("smp_min", w, [P, 1])
    DNS = at("smp_den", w + 32, [P, 1])
    RDS = at("smp_rden", w + 64, [P, 1])
    (b_ld, b_qk, b_qt, b_qb, b_z, b_za, b_zd, b_sc, b_red, b_p, b_rd, b_bs, b_vu, b_pv, b_o4, b_oc, b_du, b_dt, b_hh, b_qc) = (
        sem("smp_" + x) for x in (
            "rows_in", "qk_turned", "qk_out", "q_blocks", "turned", "out_act", "out_dve", "scores", "reduced", "probs",
            "rden", "bias_in", "v_used", "pv", "weighed", "summed", "twice", "out_turned", "hi", "q_copies"))
    b_unit = [sem(f"smp_unit_in{u}") for u in range(NU10)]
    b_vn = sem("smp_v_new_in")

    def cache_load(sp):
        sp.wait_ge(met, 4 * 9)
        sp.sem_inc(b_vu, NU10)
        with sp.Fori(0, DB) as b:
            for name in ("cache_k", "cache_v"):
                src = a[name][0].rearrange("b (a r) h d -> a b r (h d)", r=16)
                for u in range(NU10):
                    if name == "cache_k":
                        hold(sp, b_vu, b * NU10 + u + 1, "sp")
                    else:
                        hold(sp, b_z, b * NZ + 4 * u + 4, "sp")
                    if u < 4:
                        sp.dma_start(UNIT[u][:, :, :], src[:, bass.ds(b, 1), 2 * u:2 * u + 2, :].rearrange(
                            "a b r c -> a (b r) c")).then_inc(b_unit[u], 16)
                    else:
                        for j in range(4):
                            sp.dma_start(UNIT[u][32 * j:32 * j + 32, :, :],
                                         src[P - 32:P, bass.ds(b, 1), 8 + 2 * j:10 + 2 * j, :].rearrange(
                                             "a b r c -> a (b r) c")).then_inc(b_unit[u], 16)
            sp.dma_start(VNB[:, :], a["v_sample"][0][bass.ds(b, 1)].rearrange("a s h d -> (a s) (h d)")).then_inc(b_vn, 16)

    def s10_pool(pool):
        pool.dma_start(QSN[:, :], qtok[SEQ:SEQ + NS, :]).then_inc(b_ld, 16)
        pool.dma_start(KSN[:, :], a["k_sample"][0].rearrange("b s h d -> (b s) (h d)")).then_inc(b_ld, 16)
        pool.dma_start(BSS[:, :], a["c_bs"]).then_inc(b_bs, 16)
        pool.memset(QB[:, :, :], 0.0).then_inc(b_qb, 1)
        pool.wait_ge(b_qb, 1)
        pool.wait_ge(b_qt, 2)
        pool.sem_inc(b_sc, 1)
        with pool.Fori(0, DB) as b:
            hold(pool, b_sc, b * NSC + 1, "pool")
            for hpar in range(2):
                for e in range(2):
                    c = (2 * hpar + e) * DS
                    r = slice(e * DH, (e + 1) * DH)
                    pool.tensor_copy(QB[r, :, :].rearrange("p (g t) c -> p g t c", t=2)[:, :, hpar, c:c + DS],
                                     QTS[r, :, bass.ds(b * DS, DS)].rearrange("p (g t) c -> p g t c", t=2)[
                                         :, :, hpar, :]).then_inc(b_qc, 1)
                    hold(pool, b_qc, b * 4 + 2 * hpar + e + 1, "pool")
            x = pool.tensor_copy(KNB[:, :, :], KTNF[:, :, bass.ds(b * DS + S0, DS)])
            x.then_inc(b_qb, 1)

    def s10_pe(pe):
        pe.wait_ge(b_ld, 32)
        for i, t in enumerate((QSN, KSN)):
            for hp in range(HP):
                mm = pe.transpose(PS[:, 3 + i, hp * NS:(hp + 1) * NS], t[:, hp * P:(hp + 1) * P], ident[0:NS, 0:NS])
            mm.then_inc(b_qk, 1)
        pe.wait_ge(b_qt, 2)

        def scores(rhs, bank, c0, n):
            for i in range(2):
                for g in range(4):
                    mm = pe.matmul(PS[NQ * g:NQ * (g + 1), bank, c0:c0 + n], QB[:, 2 * g + i, :], rhs(2 * g + i),
                                   start=(i == 0), stop=(i == 1), tile_position=(0, NQ * g))
            mm.then_inc(b_sc, 1)

        with pe.Fori(0, DB) as b:
            def free(z):
                if z >= 4:
                    hold(pe, (b_za, b_zd)[z % 2], b * (NZA, NZD)[z % 2] + (z - 4) // 2 + 1, "pe")

            for u in range(NU10 + 1):
                if u < NU10:
                    n = 16 if u < 4 else 64
                    hold(pe, b_unit[u], b * 2 * n + n, "pe")
                    for c in range(4):
                        z = 4 * u + c
                        free(z)
                        for x in range(4):
                            hp, e = 2 * c + x // 2, x % 2
                            mm = pe.transpose(PS[:, 3 + z % 4, x * P:(x + 1) * P], UNIT[u][:, e, hp * P:(hp + 1) * P],
                                              ident[:, :])
                        mm.then_inc(b_z, 1)
                if u:
                    if u == 1:
                        hold(pe, b_qb, b + 2, "pe")
                    hold(pe, b_za, b * NZA + 2 * u, "pe")
                    hold(pe, b_zd, b * NZD + 2 * u, "pe")
                    v = u - 1
                    scores(lambda hp: KTS[:, v % 2, hp, :], v // 2, (v % 2) * UROW, UROW)
            scores(lambda hp: KNB[:, hp, :], 2, UROW, DS)
            hold(pe, b_p, b + 1, "pe")
            for z in (20, 21, 22):
                free(z)
                for x in range(4 if z < 22 else 2):
                    t = 4 * (z - 20) + x
                    mm = pe.transpose(PS[:, 3 + z % 4, x * P:(x + 1) * P], SS[:, t * P:(t + 1) * P], ident[:, :])
                if z == 22:
                    mm = pe.transpose(PS[0:DS, 3 + z % 4, 2 * P:3 * P], SS[:, 10 * P:NPOS], ident[:, :])
                mm.then_inc(b_z, 1)
            hold(pe, b_za, b * NZA + NZA, "pe")
            hold(pe, b_zd, b * NZD + NZD, "pe")
            hold(pe, b_vn, b * 16 + 16, "pe")
            for i, t in enumerate([10] + list(range(10))):
                r = DS if t == 10 else P
                if t < 10 and t % 2 == 0:
                    n = 16 if t < 8 else 64
                    hold(pe, b_unit[t // 2], b * 2 * n + 2 * n, "pe")
                for g in range(4):
                    rhs = VNB[:, 256 * g:256 * (g + 1)] if t == 10 else UNIT[t // 2][:, t % 2, 256 * g:256 * (g + 1)]
                    mm = pe.matmul(PS[NQ * g:NQ * (g + 1), 7, 0:256], PTS[0:r, t, NQ * g:NQ * (g + 1)], rhs,
                                   start=(i == 0), stop=(i == 10), tile_position=(0, NQ * g))
                if t < 10 and t % 2:
                    mm.then_inc(b_vu, 1)
            pe.drain().then_inc(b_pv, 1)
            hold(pe, b_o4, b + 1, "pe")
        pe.wait_ge(b_du, 2)
        for b in range(DB):
            mm = pe.transpose(PS[:, 3 + b // 4, (b % 4) * P:(b % 4 + 1) * P],
                              ODUP[:, b, :, :].rearrange("p a d -> p (a d)"), ident[:, :])
        mm.then_inc(b_dt, 1)

    def s10_out(z, eng, copy, done, b):
        hold(eng, b_z, b * NZ + z + 1, "act" if done is b_za else "dve")
        u = z // 4
        src = PS[:, 3 + z % 4, :]
        if z < 20:
            if u >= 2:
                hold(eng, b_sc, b * NSC + u, "act" if done is b_za else "dve")
            c = z % 4
            copy(KTS[:, u % 2, 2 * c:2 * c + 2, :].rearrange("p a w -> p (a w)"), src).then_inc(done, 1)
        elif z < 22:
            copy(PTS[:, 4 * (z - 20):4 * (z - 19), :].rearrange("p a w -> p (a w)"), src).then_inc(done, 1)
        else:
            copy(PTS[:, 8:10, :].rearrange("p a w -> p (a w)"), src[:, 0:2 * P])
            copy(PTS[0:DS, 10, :], src[0:DS, 2 * P:3 * P]).then_inc(done, 1)

    def s10_act(act):
        copy = lambda o, i: act.activation(o, i, ACT.Copy)
        act.wait_ge(b_qk, 1)
        copy(QTS[:, :, :].rearrange("p a w -> p (a w)"), PS[:, 3, :]).then_inc(b_qt, 1)
        with act.Fori(0, DB) as b:
            for z in range(0, 20, 2):
                s10_out(z, act, copy, b_za, b)
            hold(act, b_red, b + 1, "act")
            act.activation(SS[:, :], SS[:, :], ACT.Exp, bias=NMN[:, 0:1], scale=-1.0, accum_out=DNS[:, 0:1]).then_inc(b_p, 1)
            for z in (20, 22):
                s10_out(z, act, copy, b_za, b)
        act.wait_ge(b_oc, DB)
        o = OALL[:, :].rearrange("p (b d) -> p b d", b=DB)
        for e in range(2):
            copy(ODUP[:, :, e, :], o).then_inc(b_du, 1)
        act.wait_ge(b_dt, 1)
        for e in range(2):
            for b in range(0, DB, 4):
                copy(*smp_out(e, b, HHI)).then_inc(b_hh, 1)

    def smp_out(e, b, t):
        r = slice(e * DH, (e + 1) * DH)
        dst = t[r, :, S0 + b * DS:S0 + (b + 4) * DS].rearrange("p k (b q) -> p b k q", q=DS)
        src = PS[r, 3 + b // 4, :].rearrange("p (b k e q) -> p b k e q", b=4, e=2, q=DS)[:, :, :, e, :]
        return dst, src

    def s10_dve(dve):
        dve.wait_ge(b_qk, 2)
        dve.tensor_copy(KTN, PS[:, 4, :].rearrange("p (a w) -> p a w", w=NS)).then_inc(b_qt, 1)
        dve.wait_ge(b_bs, 16)
        with dve.Fori(0, DB) as b:
            for z in range(1, 20, 2):
                s10_out(z, dve, dve.tensor_copy, b_zd, b)
            hold(dve, b_sc, b * NSC + NSC + 1, "dve")
            dve.tensor_tensor_reduce(SS[:, :], PS[:, 0:3, :].rearrange("p a w -> p (a w)")[:, 0:NPOS], BSS[:, :],
                                     -(DH ** -0.5), 3.0e38, ALU.add, ALU.min, NMN[:, 0:1]).then_inc(b_red, 1)
            s10_out(21, dve, dve.tensor_copy, b_zd, b)
            hold(dve, b_p, b + 1, "dve")
            dve.reciprocal(RDS[:, :], DNS[:, :]).then_inc(b_rd, 1)
            hold(dve, b_rd, b + 1, "dve")
            hold(dve, b_pv, b + 1, "dve")
            dve.scalar_tensor_tensor(O4[:, :, :], PS[:, 7, 0:256].rearrange("p (a d) -> p a d", a=4), RDS[:, 0:1],
                                     mask4[:, :].unsqueeze(2).to_broadcast([P, 4, DH]), ALU.mult, ALU.mult).then_inc(b_o4, 1)
            hold(dve, b_o4, b + 1, "dve")
            dve.tensor_reduce(OALL[:, bass.ds(b * DH, DH)], O4[:, :, :].rearrange("p a d -> p d a"), AX.X, ALU.add).then_inc(b_oc, 1)
        for i, (e, b) in enumerate(((0, 0), (0, 4), (1, 0), (1, 4))):
            dve.wait_ge(b_hh, i + 1)
            dst, src = smp_out(e, b, HLO)
            dve.tensor_tensor(dst, src, smp_out(e, b, HHI)[0].bitcast(F32), ALU.subtract)

    stage(s10_pe, s10_act, s10_dve, s10_pool)

    stage(*out_projection(1, B_OUT1, parkx))
    stage(*ffn("ffn1", B_FFN1, G_FFN[1], 1))

    YT = at("y_tok", O_HH, [P, NT, D])
    y_in, y_a, y_v, y_st = sem("y_turned"), sem("y_out_act"), sem("y_out_dve"), sem("y_stored")

    def s13_pe(pe):
        for t in range(NT):
            if t >= 3:
                pe.wait_ge(y_a, t - 2)
                pe.wait_ge(y_v, t - 2)
            r = P if t < QT else NS
            c0 = t * P if t < QT else S0
            for k in range(KT):
                mm = pe.transpose(PS[0:r, 2 * (t % 3) + k // 4, (k % 4) * P:(k % 4 + 1) * P], X[:, k, c0:c0 + r], ident[:, :])
            mm.then_inc(y_in, 1)

    def y_half(t, half):
        r = P if t < QT else NS
        return YT[0:r, t, half * 512:(half + 1) * 512], PS[0:r, 2 * (t % 3) + half, :]

    def s13_act(act):
        for t in range(NT):
            act.wait_ge(y_in, t + 1)
            act.activation(*y_half(t, 0), ACT.Copy).then_inc(y_a, 1)

    def s13_dve(dve):
        for t in range(NT):
            dve.wait_ge(y_in, t + 1)
            dve.tensor_copy(*y_half(t, 1)).then_inc(y_v, 1)

    def s13_pool(pool):
        y = a["y_prompt"][0].rearrange("(t p) c -> p t c", p=P)
        for t in range(NT):
            pool.wait_ge(y_a, t + 1)
            pool.wait_ge(y_v, t + 1)
            if t < QT:
                pool.dma_start(y[:, t, :], YT[:, t, :]).then_inc(y_st, 16)
            else:
                pool.dma_start(a["y_sample"].rearrange("b s c -> (b s) c"), YT[0:NS, t, :]).then_inc(y_st, 16)
        pool.wait_ge(y_st, 16 * NT)

    stage(s13_pe, s13_act, s13_dve, s13_pool)

    def run(eng, name):
        for n in range(len(stages[name])):
            stages[name][n](eng)
            meet(eng, n + 1)

    with ctx:
        block = ctx.enter_context(nc.Block())

        @block.sync
        def _(sp):
            load_block(sp, 0, columns(a["w_in_rec"][0], 0), wait=False)
            with sp.Fori(1, N_IN0) as n:
                load_block(sp, n, columns(a["w_in_rec"][0], n))
            with sp.Fori(0, N_OUT) as j:
                load_block(sp, B_OUT0 + j, columns(a["w_out_rec"][0], j))
            ffn_load(sp, B_FFN0, 0)
            with sp.Fori(0, N_QKV) as j:
                load_block(sp, B_QKV + j, columns(a["w_in_att"][0], j))
            with sp.Fori(0, RING) as j:
                load_block(sp, B_OUT1 + j, columns(a["w_out_att"][0], j))
            cache_load(sp)
            load_block(sp, B_OUT1 + RING, columns(a["w_out_att"][0], RING))
            ffn_load(sp, B_FFN1, 1)

        @block.tensor
        def _(pe):
            run(pe, "pe")

        @block.scalar
        def _(act):
            run(act, "act")

        @block.vector
        def _(dve):
            run(dve, "dve")

        @block.gpsimd
        def _(pool):
            run(pool, "pool")


_OUTS = [((1, SEQ, D), "y_prompt"), ((DB, DS, D), "y_sample"), ((1, 1, RH, DK, DV), "ret_prompt"),
         ((1, 1, LW), "lru_prompt"), ((1, 1, CONV - 1, LW), "conv_prompt"), ((1, 1, SEQ, H, DH), "k_prompt"),
         ((1, 1, SEQ, H, DH), "v_prompt"), ((1, DB, RH, DK, DV), "ret_sample"), ((1, DB, LW), "lru_sample"),
         ((1, DB, CONV - 1, LW), "conv_sample"), ((1, DB, DS, H, DH), "k_sample"), ((1, DB, DS, H, DH), "v_sample")]
_INS = ["x_prompt", "x_sample", "state_ret", "state_lru", "state_conv", "cache_k", "cache_v", "norm_mix", "norm_ffn",
        "w_in_rec", "w_out_rec", "ret_norm_g", "conv_w", "conv_b", "w_rgate", "b_rgate", "w_igate", "b_igate",
        "lru_lambda", "w_in_att", "w_out_att", "q_norm_g", "k_norm_g", "w_ffn_gate", "w_ffn_up", "w_ffn_down"]


def kernel(**inputs):
    import concourse.bacc as bacc
    from concourse.bass_utils import run_bass_kernel_spmd

    nc = bacc.Bacc("TRN2", target_bir_lowering=False, num_devices=1)
    arrays, aps = {}, {}
    for name in _INS:
        arr = np.ascontiguousarray(inputs[name])
        arrays["in_" + name] = arr
        aps[name] = nc.dram_tensor("in_" + name, arr.shape, mybir.dt.from_np(arr.dtype), kind="ExternalInput").ap()
    for name, arr in constants().items():
        arrays["in_" + name] = arr
        aps[name] = nc.dram_tensor("in_" + name, arr.shape, F32, kind="ExternalInput").ap()
    for shape, name in _OUTS:
        aps[name] = nc.dram_tensor("out_" + name, shape, F32, kind="ExternalOutput").ap()
    build(nc, aps)
    r = run_bass_kernel_spmd(nc, [arrays], core_ids=[0])
    return tuple(r.results[0]["out_" + name] for _, name in _OUTS)
```
